# Optimizing a Trainium2 kernel written in Bass

```python
import math, functools
import jax, jax.numpy as jnp
from jax import lax
import numpy as np

D_MODEL = 1024
BATCH = 1
SEQ = 1024
DEPTH = 2
DEC_BATCH = 8
DEC_SEQ = 4
PAST_LEN = 8192
PAGE_SIZE = 128

A_HEADS = 8
A_HEAD_DIM = 64
IDX_HEADS = 8
IDX_DIM = 64
TOPK_MAX = 256
IDX_Q_BLOCK = 64
ROPE_THETA = 10000.0
B_HEADS = 4
B_KEY_DIM = 128
B_VAL_DIM = 128
GLR_CHUNK = 16
POOL_WINDOWS = (2, 4, 8, 16)
POOL_GROUP = D_MODEL // len(POOL_WINDOWS)
POOL_BUF = max(POOL_WINDOWS) - 1
D_FF = -(-8 * D_MODEL // (3 * 256)) * 256
PLE_DIM = 256
RMS_EPS = 1e-6
N_AB_LAYERS = (DEPTH + 1) // 2
N_C_LAYERS = DEPTH // 2
A_Q = A_HEADS * A_HEAD_DIM
IDX_Q = IDX_HEADS * IDX_DIM
B_K = B_HEADS * B_KEY_DIM
B_V = B_HEADS * B_VAL_DIM
IN_SIZES = (A_Q, A_Q, A_Q, IDX_Q, IDX_DIM, IDX_HEADS, B_K, B_K, B_V, B_V)
IN_COLS = sum(IN_SIZES)
IN_OFFSETS = tuple(sum(IN_SIZES[:n]) for n in range(1, len(IN_SIZES)))
MIX_WIDTH = A_Q + B_V

kernel_name = 'hybrid_dsa_hgrn2_pool_decode_step'

def rmsnorm(x, w):
    xf = x.astype(jnp.float32)
    y = xf * lax.rsqrt(jnp.mean(xf * xf, axis=-1, keepdims=True) + RMS_EPS)
    return (y * w.astype(jnp.float32)).astype(x.dtype)

def rope(x, pos):
    half = x.shape[-1] // 2
    inv = ROPE_THETA ** (-jnp.arange(half, dtype=jnp.float32) / half)
    ang = pos.astype(jnp.float32)[:, None] * inv[None, :]
    ang = ang.reshape(ang.shape[:1] + (1,) * (x.ndim - 3) + ang.shape[1:])
    c, s = jnp.cos(ang), jnp.sin(ang)
    xf = x.astype(jnp.float32)
    x1, x2 = xf[..., :half], xf[..., half:]
    return jnp.concatenate([x1 * c - x2 * s, x2 * c + x1 * s], axis=-1).astype(x.dtype)

def index_scores(qi, wi, ki):
    s = jnp.einsum('bthd,bsd->bths', qi.astype(jnp.float32), ki.astype(jnp.float32)) * (IDX_DIM ** -0.5)
    return jnp.einsum('bths,bth->bts', jax.nn.relu(s), wi.astype(jnp.float32) * (IDX_HEADS ** -0.5))

def sparse_attend(q, k_sel, v_sel, valid):
    lg = jnp.einsum('bthd,btkhd->bthk', q.astype(jnp.float32), k_sel.astype(jnp.float32)) * (A_HEAD_DIM ** -0.5)
    lg = jnp.where(valid[:, :, None, :], lg, -jnp.inf)
    p = jax.nn.softmax(lg, axis=-1)
    return jnp.einsum('bthk,btkhd->bthd', p, v_sel.astype(jnp.float32)).astype(q.dtype)

def dsa_prompt(q, k, v, qi, ki, wi):
    B, S = q.shape[:2]
    kk = min(TOPK_MAX, S // 4)
    qb = min(IDX_Q_BLOCK, S)
    nb = S // qb
    key_pos = jnp.arange(S)
    bidx = jnp.arange(B)[:, None, None]

    def blocks(a):
        return a.reshape((B, nb, qb) + a.shape[2:]).swapaxes(0, 1)

    def one_block(args):
        q_b, qi_b, wi_b, start = args
        qpos = start + jnp.arange(qb)
        sc = index_scores(qi_b, wi_b, ki)
        sc = jnp.where(key_pos[None, None, :] <= qpos[None, :, None], sc, -jnp.inf)
        _, idx = lax.top_k(sc, kk)
        valid = idx <= qpos[None, :, None]
        return sparse_attend(q_b, k[bidx, idx], v[bidx, idx], valid)

    out = lax.map(one_block, (blocks(q), blocks(qi), blocks(wi), jnp.arange(nb) * qb))
    return out.swapaxes(0, 1).reshape(B, S, A_HEADS, A_HEAD_DIM)

def dsa_sample(q, k, v, qi, ki, wi, *, layer, cache_k, cache_v, cache_kidx, page_table):
    Bd, T = q.shape[:2]
    past = page_table.shape[1] * PAGE_SIZE
    L = past + T
    kk = min(TOPK_MAX, L // 4)
    past_ki = cache_kidx[layer, page_table].reshape(Bd, past, IDX_DIM)
    all_ki = jnp.concatenate([past_ki, ki.astype(past_ki.dtype)], axis=1)
    qpos = past + jnp.arange(T)
    sc = index_scores(qi, wi, all_ki)
    sc = jnp.where(jnp.arange(L)[None, None, :] <= qpos[None, :, None], sc, -jnp.inf)
    _, idx = lax.top_k(sc, kk)
    valid = idx <= qpos[None, :, None]
    is_new = (idx >= past)[..., None, None]
    bidx = jnp.arange(Bd)[:, None, None]
    pidx = jnp.minimum(idx, past - 1)
    phys = page_table[bidx, pidx // PAGE_SIZE]
    off = pidx % PAGE_SIZE
    nidx = jnp.clip(idx - past, 0, T - 1)
    k_sel = jnp.where(is_new, k[bidx, nidx], cache_k[layer, phys, off].astype(k.dtype))
    v_sel = jnp.where(is_new, v[bidx, nidx], cache_v[layer, phys, off].astype(v.dtype))
    return sparse_attend(q, k_sel, v_sel, valid)

def glr_scan(q, k, v, log_f, s0):
    B, T, H, DK = q.shape
    C = math.gcd(T, GLR_CHUNK)
    n = T // C

    def chunks(a):
        return a.astype(jnp.float32).reshape((B, n, C) + a.shape[2:]).swapaxes(0, 1)

    causal = jnp.tril(jnp.ones((C, C), bool))[None, :, :, None, None]

    def step(S, inp):
        qc, kc, vc, lfc = inp
        b = jnp.cumsum(lfc, axis=1)
        decay = jnp.exp(jnp.where(causal, b[:, :, None] - b[:, None, :], -jnp.inf))
        att = jnp.einsum('bthd,bshd,btshd->bhts', qc, kc, decay)
        o = jnp.einsum('bhts,bshv->bthv', att, vc) + jnp.einsum('bthd,bhdv->bthv', qc * jnp.exp(b), S)
        b_last = b[:, -1]
        S = jnp.exp(b_last)[..., None] * S + jnp.einsum('bshd,bshv->bhdv', kc * jnp.exp(b_last[:, None] - b), vc)
        return S, o

    S, o = lax.scan(step, s0.astype(jnp.float32), (chunks(q), chunks(k), chunks(v), chunks(log_f)))
    return o.swapaxes(0, 1).reshape(B, T, H, v.shape[-1]), S

def glr_mix(bq, bf, bi, bg, lb, norm_w, s0):
    B, T, _ = bq.shape
    kshape = (B, T, B_HEADS, B_KEY_DIM)
    vshape = (B, T, B_HEADS, B_VAL_DIM)
    bf32 = bf.astype(jnp.float32)
    lb = lb.astype(jnp.float32)
    f = lb + (1.0 - lb) * jax.nn.sigmoid(bf32)
    k = (1.0 - lb) * jax.nn.sigmoid(-bf32)
    q = jax.nn.silu(bq)
    o, s = glr_scan(q.reshape(kshape), k.reshape(kshape), bi.reshape(vshape), jnp.log(f).reshape(kshape), s0)
    o = rmsnorm(o, norm_w) * jax.nn.silu(bg.astype(jnp.float32).reshape(vshape))
    return o.reshape(B, T, B_V).astype(bq.dtype), s.astype(s0.dtype)

def ab_mixer(h, pos, w_in, w_out, lb, glr_norm_w, s0, attend):
    B, T, _ = h.shape
    aq, ak, av, iq, ik, iw, bq, bf, bi, bg = jnp.split(h @ w_in, list(IN_OFFSETS), axis=-1)
    q = rope(aq.reshape(B, T, A_HEADS, A_HEAD_DIM), pos)
    k = rope(ak.reshape(B, T, A_HEADS, A_HEAD_DIM), pos)
    v = av.reshape(B, T, A_HEADS, A_HEAD_DIM)
    qi = rope(iq.reshape(B, T, IDX_HEADS, IDX_DIM), pos)
    ki = rope(ik, pos)
    att = attend(q, k, v, qi, ki, iw).reshape(B, T, A_Q)
    glr, s_new = glr_mix(bq, bf, bi, bg, lb, glr_norm_w, s0)
    y = jnp.concatenate([att, glr.astype(att.dtype)], axis=-1) @ w_out
    return y, k, v, ki, s_new

def pool_mix(h, prev, w_pool, scale):
    B, T, D = h.shape
    P = prev.shape[1]
    ext = jnp.concatenate([prev.astype(h.dtype), h], axis=1)
    cs = jnp.concatenate([jnp.zeros((B, 1, D), jnp.float32), jnp.cumsum(ext.astype(jnp.float32), axis=1)], axis=1)
    win = jnp.repeat(jnp.array(POOL_WINDOWS, jnp.int32), POOL_GROUP)
    end = P + 1 + jnp.arange(T)
    lo = jnp.maximum(end[:, None] - win[None, :], 0)
    cnt = jnp.minimum(end[:, None], win[None, :]).astype(jnp.float32)
    lo_sum = jnp.take_along_axis(cs, jnp.broadcast_to(lo[None], (B, T, D)), axis=1)
    mean = (cs[:, P + 1:] - lo_sum) / cnt
    z = (mean - h.astype(jnp.float32)).reshape(B, T, len(POOL_WINDOWS), POOL_GROUP)
    y = jnp.einsum('btgc,gcd->btgd', z, w_pool.astype(jnp.float32)).reshape(B, T, D) * scale.astype(jnp.float32)
    return y.astype(h.dtype), ext[:, -POOL_BUF:]

def swiglu(h, w_up, w_down):
    gate, up = jnp.split(h @ w_up, 2, axis=-1)
    return (jax.nn.silu(gate) * up) @ w_down

def trunk(x, p, pos, attends, glr_s0, pool_prev, W):
    new_k, new_v, new_ki, new_s, new_buf = [], [], [], [], []
    lb_all = jnp.cumsum(jax.nn.softmax(W['lb_logits'].astype(jnp.float32), axis=0), axis=0)
    for i in range(DEPTH):
        j = i // 2
        h = rmsnorm(x, W['mix_norm'][i])
        if i % 2 == 0:
            y, k, v, ki, s = ab_mixer(h, pos, W['w_in'][j], W['w_out'][j], lb_all[j], W['glr_norm'][j], glr_s0[j], attends[j])
            new_k.append(k)
            new_v.append(v)
            new_ki.append(ki)
            new_s.append(s)
        else:
            y, buf = pool_mix(h, pool_prev[j], W['pool_w'][j], W['pool_scale'][j])
            new_buf.append(buf)
        x = x + y
        x = x + swiglu(rmsnorm(x, W['ffn_norm'][i]), W['w_up'][i], W['w_down'][i])
        gate = jax.nn.sigmoid(rmsnorm(x, W['ple_norm'][i]) @ W['w_ple_gate'][i])
        x = x + (p[i] @ W['w_ple'][i]) * gate
    return (rmsnorm(x, W['final_norm']), jnp.stack(new_k), jnp.stack(new_v), jnp.stack(new_ki),
            jnp.stack(new_s), jnp.stack(new_buf))

def setup_inputs(seed: int = 0) -> dict:
    key = jax.random.key(seed)
    ks = jax.random.split(key, 32)
    f32 = jnp.float32
    n_pages = PAST_LEN // PAGE_SIZE
    n_used = DEC_BATCH * n_pages
    n_pool = n_used + n_used // 4

    def nrm(k, shape, s=1.0):
        return jax.random.normal(k, shape, f32) * s

    def gain(k, shape):
        return 1.0 + 0.02 * jax.random.normal(k, shape, f32)

    page_table = jax.random.permutation(ks[7], n_pool)[:n_used].reshape(DEC_BATCH, n_pages).astype(jnp.int32)
    return {
        'x_prompt': nrm(ks[0], (BATCH, SEQ, D_MODEL)),
        'x_sample': nrm(ks[1], (DEC_BATCH, DEC_SEQ, D_MODEL)),
        'cache_k': nrm(ks[2], (N_AB_LAYERS, n_pool, PAGE_SIZE, A_HEADS, A_HEAD_DIM)),
        'cache_v': nrm(ks[3], (N_AB_LAYERS, n_pool, PAGE_SIZE, A_HEADS, A_HEAD_DIM)),
        'cache_kidx': nrm(ks[4], (N_AB_LAYERS, n_pool, PAGE_SIZE, IDX_DIM)),
        'state_glr': nrm(ks[5], (N_AB_LAYERS, DEC_BATCH, B_HEADS, B_KEY_DIM, B_VAL_DIM), 0.5),
        'state_pool': nrm(ks[6], (N_C_LAYERS, DEC_BATCH, POOL_BUF, D_MODEL)),
        'page_table': page_table,
        'p_prompt': nrm(ks[8], (DEPTH, BATCH, SEQ, PLE_DIM)),
        'p_sample': nrm(ks[9], (DEPTH, DEC_BATCH, DEC_SEQ, PLE_DIM)),
        'mix_norm': gain(ks[10], (DEPTH, D_MODEL)),
        'w_in': nrm(ks[11], (N_AB_LAYERS, D_MODEL, IN_COLS), D_MODEL ** -0.5),
        'w_out': nrm(ks[12], (N_AB_LAYERS, MIX_WIDTH, D_MODEL), MIX_WIDTH ** -0.5),
        'lb_logits': nrm(ks[13], (N_AB_LAYERS + 1, B_K), 0.5),
        'glr_norm': gain(ks[14], (N_AB_LAYERS, B_VAL_DIM)),
        'pool_w': nrm(ks[15], (N_C_LAYERS, len(POOL_WINDOWS), POOL_GROUP, POOL_GROUP), POOL_GROUP ** -0.5),
        'pool_scale': gain(ks[16], (N_C_LAYERS, D_MODEL)),
        'ffn_norm': gain(ks[17], (DEPTH, D_MODEL)),
        'w_up': nrm(ks[18], (DEPTH, D_MODEL, 2 * D_FF), D_MODEL ** -0.5),
        'w_down': nrm(ks[19], (DEPTH, D_FF, D_MODEL), D_FF ** -0.5),
        'ple_norm': gain(ks[20], (DEPTH, D_MODEL)),
        'w_ple_gate': nrm(ks[21], (DEPTH, D_MODEL, D_MODEL), D_MODEL ** -0.5),
        'w_ple': nrm(ks[22], (DEPTH, PLE_DIM, D_MODEL), PLE_DIM ** -0.5),
        'final_norm': gain(ks[23], (D_MODEL,)),
    }

def reference(x_prompt, x_sample, cache_k, cache_v, cache_kidx, state_glr, state_pool, page_table,
              p_prompt, p_sample, mix_norm, w_in, w_out, lb_logits, glr_norm, pool_w, pool_scale,
              ffn_norm, w_up, w_down, ple_norm, w_ple_gate, w_ple, final_norm):
    W = dict(mix_norm=mix_norm, w_in=w_in, w_out=w_out, lb_logits=lb_logits, glr_norm=glr_norm,
             pool_w=pool_w, pool_scale=pool_scale, ffn_norm=ffn_norm, w_up=w_up, w_down=w_down,
             ple_norm=ple_norm, w_ple_gate=w_ple_gate, w_ple=w_ple, final_norm=final_norm)
    Bp, Sp = x_prompt.shape[:2]
    pos_p = jnp.arange(Sp, dtype=jnp.int32)
    glr0_p = [jnp.zeros((Bp, B_HEADS, B_KEY_DIM, B_VAL_DIM), state_glr.dtype) for _ in range(N_AB_LAYERS)]
    pool0_p = [jnp.zeros((Bp, 0, D_MODEL), x_prompt.dtype) for _ in range(N_C_LAYERS)]
    yp, kp, vp, kip, gp, pp = trunk(x_prompt, p_prompt, pos_p, [dsa_prompt] * N_AB_LAYERS, glr0_p, pool0_p, W)
    past = page_table.shape[1] * PAGE_SIZE
    pos_s = past + jnp.arange(x_sample.shape[1], dtype=jnp.int32)
    attends_s = [functools.partial(dsa_sample, layer=j, cache_k=cache_k, cache_v=cache_v,
                                   cache_kidx=cache_kidx, page_table=page_table) for j in range(N_AB_LAYERS)]
    glr0_s = [state_glr[j] for j in range(N_AB_LAYERS)]
    pool0_s = [state_pool[j] for j in range(N_C_LAYERS)]
    ys, ks_, vs_, kis, gs, ps = trunk(x_sample, p_sample, pos_s, attends_s, glr0_s, pool0_s, W)
    return (yp, ys, kp, vp, kip, gp, pp, ks_, vs_, kis, gs, ps)


_drawn_inputs = setup_inputs


def setup_inputs(seed=0):
    import zlib

    import numpy as np

    out = dict(_drawn_inputs(seed))
    spreads = {}
    factors = {'glr_norm': 6.988,
     'pool_scale': 5.174,
     'ffn_norm': 3.472,
     'ple_norm': 8.0,
     'final_norm': 2.896}
    for name, (base, spread) in spreads.items():
        noise = np.random.default_rng([zlib.crc32(name.encode()), seed]).standard_normal(out[name].shape)
        drawn = base * np.exp(spread * noise) if base else spread * noise
        out[name] = __import__('jax').numpy.asarray(drawn.astype(out[name].dtype))
    for name, factor in factors.items():
        out[name] = (out[name] * factor).astype(out[name].dtype)
    return out
```

```python
from contextlib import ExitStack
import math

import numpy as np

import concourse.bass as bass
from concourse import mybir

F32, I32, U32 = mybir.dt.float32, mybir.dt.int32, mybir.dt.uint32
ALU, ACT, AX = mybir.AluOpType, mybir.ActivationFunctionType, mybir.AxisListType

P = 128
D = 1024
SEQ = 1024
BD, TD = 8, 4
NS = BD * TD
R = SEQ + NS
PAGE, NPAGES = 128, 64
PAST = PAGE * NPAGES
H, DH = 8, 64
TOPK = 256
BH, BK = 4, 128
FF = 2816
PLE = 256
POOL_BUF = 15
WINDOWS = (2, 4, 8, 16)
EPS = 1e-6

KD = D // P
KF = FF // P
NT = SEQ // P
G, GC = 3, R // 3
COL = dict(aq=0, ak=512, av=1024, iq=1536, ik=2048, bq=2120, bf=2632, bi=3144, bg=3656)
IK_COLS = DH + H
QUARTER = PAST // 4
ROUNDS = TOPK // 8
MASKED = -1e30
UNSEEN = -3.0e38
TAKEN = -3.39e38
LEVELS = int(math.log2(P))


def rows_of(r):
    return P if r < NT else NS


def constants():
    half = DH // 2
    inv = (10000.0 ** (-np.arange(half) / half)).astype(np.float32)
    pos = np.concatenate([np.arange(SEQ), np.tile(PAST + np.arange(TD), BD)]).astype(np.float32)
    ang = pos[:, None] * inv[None, :]
    c, s = np.cos(ang), np.sin(ang)
    rope = np.stack([np.concatenate([c, c], 1), np.concatenate([-s, s], 1)], 1).astype(np.float32)
    a, b = np.arange(P)[:, None], np.arange(P)[None, :]
    level = [((a // (2 * w)) == (b // (2 * w))) & (a % (2 * w) < w) & (b % (2 * w) >= w)
             for w in (1 << n for n in range(LEVELS))] + [a == b]
    t = np.arange(R)
    reset = np.where(t < SEQ, t % P != 0, (t - SEQ) % TD != 0)
    q, n = np.arange(NS)[:, None], np.arange(NS)[None, :]
    same = q // TD == n // TD
    w = np.array(WINDOWS)[:, None]
    return dict(
        c_ident=np.eye(P, dtype=np.float32),
        c_rope=rope,
        c_level=np.stack(level, 1).astype(np.int32),
        c_causal=np.where(b <= a, 0.0, MASKED).astype(np.float32),
        c_reset=reset[None].astype(np.float32),
        c_batchcol=(n[0][None, :] // TD == np.arange(BD)[:, None]).reshape(1, BD * NS).astype(np.float32),
        c_batchrow=(np.arange(NS)[:, None] // TD == np.arange(BD)[None, :]).astype(np.float32),
        c_fold=(a % NS == n).astype(np.float32),
        c_newbias=np.where(same & (n % TD <= q % TD), 0.0, UNSEEN).astype(np.float32),
        c_same=same.astype(np.float32),
        c_iota=np.arange(TOPK)[None].astype(np.float32),
        c_part=np.concatenate([a % 8, (a // NS) * QUARTER], 1).astype(np.float32),
        c_invcnt=(1.0 / np.minimum(np.arange(16)[None] + 1, w)).reshape(1, -1).astype(np.float32),
    )


class Program:

    def __init__(self, nc, io, scratch):
        self.nc, self.io, self.scratch = nc, io, scratch
        self.keep = ExitStack()
        self.used = {}
        self.in_use = []

    def numbered(self, name):
        self.used[name] = self.used.get(name, 0) + 1
        return name if self.used[name] == 1 else f"{name}_{self.used[name]}"

    def sb(self, ctx, name, shape, dt=F32):
        return ctx.enter_context(self.nc.sbuf_tensor(self.numbered(name), shape, dt))

    def sems(self, ctx, *names):
        sems = [self.nc.alloc_semaphore(self.numbered("s_" + n)) for n in names]
        self.in_use += sems
        ctx.callback(self.clear_sems)
        return sems

    def sem_ring(self, ctx, name, n):
        return self.sems(ctx, *(f"{name}{i}" for i in range(n)))

    def clear_sems(self):
        if self.in_use:
            self.nc.clear_and_free_semaphores(self.in_use)
            self.in_use = []
            self.nc.all_engine_barrier()


def bank_cols(ps, b, n=G):
    return ps[:, b:b + n, 0:GC]


def grouped(ap):
    return ap.rearrange("p (g n) -> p g n", g=G)



def load_constants(k):
    nc, io = k.nc, k.io
    keep = k.keep
    k.ps = keep.enter_context(nc.psum_tensor("ps", [P, 8, 512], F32))
    k.xT = k.sb(keep, "xT", [P, KD, R])
    k.ident = k.sb(keep, "ident", [P, P])
    k.ones = k.sb(keep, "ones", [P, P])
    k.eps = k.sb(keep, "eps", [P, 1])
    k.vec = k.sb(keep, "vec", [P, 9 * KD])
    with ExitStack() as ctx:
        rows = k.sb(ctx, "vec_rows", [9 * KD, P])
        landed, made, turned = k.sems(ctx, "landed", "made", "turned")
        block = ctx.enter_context(nc.Block())

        @block.sync
        def _(sp):
            sp.dma_start(k.ident[:], io["c_ident"]).then_inc(landed, 16)
            at = 0
            for name in ("mix_norm", "ffn_norm", "ple_norm", "final_norm", "pool_scale", "lb_logits"):
                a = io[name]
                n = a.size() // P if callable(a.size) else a.size // P
                flat = a.rearrange("(n p) -> n p", p=P) if len(a.shape) == 1 else a.rearrange("l (n p) -> (l n) p", p=P)
                sp.dma_start(rows[at:at + n, :], flat).then_inc(landed, 16)
                at += n
            sp.wait_ge(landed, 16 * 7)

        @block.vector
        def _(dve):
            dve.memset(k.ones[:], 1.0)
            dve.memset(k.eps[:], EPS)
            dve.wait_ge(turned, 1)
            dve.tensor_copy(k.vec[:], k.ps[:, 0, 0:9 * KD])

        @block.tensor
        def _(pe):
            pe.wait_ge(landed, 16 * 7)
            pe.transpose(k.ps[:, 0, 0:9 * KD], rows[:], k.ident[0:9 * KD, 0:9 * KD]).then_inc(turned, 1)

    k.mix_w = [k.vec[:, i * KD:(i + 1) * KD] for i in range(2)]
    k.ffn_w = [k.vec[:, (2 + i) * KD:(3 + i) * KD] for i in range(2)]
    k.ple_w = [k.vec[:, (4 + i) * KD:(5 + i) * KD] for i in range(2)]
    k.final_w = k.vec[:, 6 * KD:7 * KD]
    k.pool_s = k.vec[:, 7 * KD:8 * KD]
    k.lb_logit = [k.vec[:, 8 * KD + i * BH:8 * KD + (i + 1) * BH] for i in range(2)]



def load_x(k):
    nc, io, ps = k.nc, k.io, k.ps
    with ExitStack() as ctx:
        rows = k.sb(ctx, "x_rows", [P, 3, D])
        landed = k.sem_ring(ctx, "x_landed", 3)
        turned, copied = k.sems(ctx, "turned", "copied")
        block = ctx.enter_context(nc.Block())

        @block.sync
        def _(sp):
            for r in range(NT + 1):
                n = rows_of(r)
                if r >= 3:
                    sp.wait_ge(turned, r - 2)
                src = io["x_prompt"][0, r * P:(r + 1) * P, :] if r < NT else io["x_sample"].rearrange("b t d -> (b t) d")
                sp.dma_start(rows[0:n, r % 3, :], src).then_inc(landed[r % 3], 16)

        @block.tensor
        def _(pe):
            for r in range(NT + 1):
                n = rows_of(r)
                pe.wait_ge(landed[r % 3], 16 * (r // 3 + 1))
                if r >= 2:
                    pe.wait_ge(copied, r - 1)
                for d in range(KD):
                    at = (d % 4) * P
                    m = pe.transpose(ps[:, 2 * (r % 2) + d // 4, at:at + n], rows[0:n, r % 3, d * P:(d + 1) * P],
                                     k.ident[0:n, 0:n])
                m.then_inc(turned, 1)

        @block.scalar
        def _(act):
            for r in range(NT + 1):
                n, b = rows_of(r), 2 * (r % 2)
                act.wait_ge(turned, r + 1)
                src = ps[:, b:b + 2, :].rearrange("p b (d n) -> p (b d) n", n=P)
                act.copy(k.xT[:, :, r * P:r * P + n], src[:, :, 0:n]).then_inc(copied, 1)


class Norm:

    def __init__(self, k, ctx, hT, weight, square=None, total=None):
        self.k, self.hT, self.weight = k, hT, weight
        self.square = k.sb(ctx, "norm_square", [P, 2, R]) if square is None else square
        self.total = k.sb(ctx, "norm_total", [P, R])[:] if total is None else total
        self.squared, self.summed, self.ssq, self.rooted, self.normed = k.sems(
            ctx, "norm_squared", "norm_summed", "norm_ssq", "norm_rooted", "normed")

    def scalar(self, act):
        k = self.k
        for d in range(KD):
            if d >= 2:
                act.wait_ge(self.summed, max(1, d - 2))
            act.activation(self.square[:, d % 2, :], k.xT[:, d, :], ACT.Square).then_inc(self.squared, 1)
        for g in range(G):
            act.wait_ge(self.ssq, g + 1)
            act.activation(self.square[:, 0, g * GC:(g + 1) * GC], k.ps[:, g, 0:GC], ACT.Sqrt,
                           bias=k.eps[:, 0:1], scale=1.0 / D).then_inc(self.rooted, 1)

    def tensor(self, pe):
        k = self.k
        pe.wait_ge(self.summed, KD - 1)
        for g in range(G):
            pe.matmul(k.ps[:, g, 0:GC], k.ones[:], self.total[:, g * GC:(g + 1) * GC],
                      start=True, stop=True).then_inc(self.ssq, 1)

    def vector(self, dve):
        k, total = self.k, self.total
        for d in range(1, KD):
            dve.wait_ge(self.squared, d + 1)
            first = self.square[:, 0, :] if d == 1 else total
            dve.tensor_tensor(total, first, self.square[:, d % 2, :], ALU.add).then_inc(self.summed, 1)
            dve.drain()
        for g in range(G):
            dve.wait_ge(self.rooted, g + 1)
            dve.reciprocal(total[:, g * GC:(g + 1) * GC], self.square[:, 0, g * GC:(g + 1) * GC])
        dve.drain()
        for d in range(KD):
            dve.scalar_tensor_tensor(self.hT[:, d, :], k.xT[:, d, :], self.weight[:, d:d + 1], total,
                                     ALU.mult, ALU.mult).then_inc(self.normed, 1)



def project_rows(k, chunks):
    nc, io, ps, hT = k.nc, k.io, k.ps, k.hT
    w_in = io["w_in"][0].rearrange("(k p) n -> p k n", p=P)
    jobs = [(c, r) for c in chunks for r in range(NT + 1)]
    rotated = {"aq", "ak", "iq", "ik"}
    width = {c: IK_COLS if c == "ik" else 512 for c in COL}
    turns = {"aq": k.qT, "ak": k.kT, "iq": k.iqT, "ik": k.ikT}
    RAW = 3
    LAG = 3
    nth_rot, nth_store = {}, {}
    for j, (c, r) in enumerate(jobs):
        if c in rotated:
            nth_rot[j] = len(nth_rot)
        if c in ("ak", "av", "ik", "bi", "bg") or r == NT:
            nth_store[j] = len(nth_store)

    def dest(c, r):
        if r == NT:
            return {"ak": io["k_sample"], "av": io["v_sample"], "ik": io["kidx_sample"], "aq": k.scratch["q_s"],
                    "iq": k.scratch["iq_s"], "bi": k.scratch["bi"][SEQ:R], "bg": k.scratch["bg"][SEQ:R]}[c]
        rows = slice(r * P, (r + 1) * P)
        return {"ak": io["k_prompt"], "av": io["v_prompt"], "ik": io["kidx_prompt"],
                "bi": k.scratch["bi"], "bg": k.scratch["bg"]}[c][rows]

    with ExitStack() as ctx:
        w = k.sb(ctx, "w_chunk", [P, 2, KD, 512])
        raw = k.sb(ctx, "raw", [P, RAW, 512])
        rot = k.sb(ctx, "rot", [P, RAW, 512])
        part = k.sb(ctx, "rope_part", [P, 2, 512])
        w_landed = k.sem_ring(ctx, "w_landed", 2)
        stored = k.sem_ring(ctx, "rows_stored", RAW)
        projected, taken, roped, turned, copied, iw_stored = k.sems(
            ctx, "projected", "taken", "roped", "turned", "copied", "iw_stored")
        block = ctx.enter_context(nc.Block())

        def stores_before(j):
            return sum(1 for i in nth_store if i < j and i % RAW == j % RAW)

        @block.sync
        def _(sp):
            def load(i):
                c = chunks[i]
                if i >= 2:
                    sp.wait_ge(projected, (NT + 1) * (i - 1))
                sp.dma_start(w[:, i % 2, :, 0:width[c]], w_in[:, :, COL[c]:COL[c] + width[c]]).then_inc(w_landed[i % 2], 16)

            load(0)
            for j, (c, r) in enumerate(jobs):
                i = j // (NT + 1)
                if r == 1 and i + 1 < len(chunks):
                    load(i + 1)
                if j in nth_store:
                    n = rows_of(r)
                    if c in rotated:
                        sp.wait_ge(roped, nth_rot[j] + 1)
                        cols = DH if c == "ik" else 512
                        sp.dma_start(dest(c, r), rot[0:n, j % RAW, 0:cols]).then_inc(stored[j % RAW], 16)
                    else:
                        sp.wait_ge(taken, j + 1)
                        sp.dma_start(dest(c, r), raw[0:n, j % RAW, :]).then_inc(stored[j % RAW], 16)
            if "ik" in chunks:
                sp.wait_ge(taken, len(jobs))
                sp.dma_start(k.scratch["iw_s"], k.iw[0:NS, NT, :]).then_inc(iw_stored, 16)
                sp.wait_ge(iw_stored, 16)
            for s in range(RAW):
                sp.wait_ge(stored[s], 16 * sum(1 for i in nth_store if i % RAW == s))

        @block.tensor
        def _(pe):
            turn_jobs = [j for j in range(len(jobs)) if jobs[j][0] in rotated]

            def turn(j):
                c, r = jobs[j]
                n, t = rows_of(r), nth_rot[j]
                pe.wait_ge(roped, t + 1)
                if t >= 4:
                    pe.wait_ge(copied, t - 3)
                for i in range(1 if c == "ik" else 4):
                    m = pe.transpose(ps[:, 4 + t % 4, i * P:i * P + n], rot[0:n, j % RAW, i * P:(i + 1) * P],
                                     k.ident[0:n, 0:n])
                m.then_inc(turned, 1)

            for j, (c, r) in enumerate(jobs):
                i, n = j // (NT + 1), rows_of(r)
                if r == 0:
                    pe.wait_ge(w_landed[i % 2], 16 * (i // 2 + 1))
                if j >= 4:
                    pe.wait_ge(taken, j - 3)
                for d in range(KD):
                    m = pe.matmul(ps[0:n, j % 4, 0:width[c]], hT[:, d, r * P:r * P + n], w[:, i % 2, d, 0:width[c]],
                                  start=d == 0, stop=d == KD - 1)
                m.then_inc(projected, 1)
                if j - LAG + 1 in nth_rot:
                    turn(j - LAG + 1)
            for j in range(len(jobs) - LAG + 1, len(jobs)):
                if j in nth_rot:
                    turn(j)

        @block.scalar
        def _(act):
            def take(j):
                c, r = jobs[j]
                n = rows_of(r)
                act.wait_ge(projected, j + 1)
                if j >= RAW:
                    if j - RAW in nth_rot:
                        act.wait_ge(roped, nth_rot[j - RAW] + 1)
                    if stores_before(j):
                        act.wait_ge(stored[j % RAW], 16 * stores_before(j))
                src, dst = ps[0:n, j % 4, 0:width[c]], raw[0:n, j % RAW, 0:width[c]]
                if c == "ik":
                    act.activation(k.iw[0:n, r, :], src[:, DH:IK_COLS], ACT.Copy, scale=float(np.float32(H ** -0.5) * DH ** -0.5))
                act.activation(dst, src, ACT.Silu if c == "bg" else ACT.Copy).then_inc(taken, 1)

            def copy_turned(j):
                c, r = jobs[j]
                n, t = rows_of(r), nth_rot[j]
                act.wait_ge(turned, t + 1)
                src = ps[:, 4 + t % 4, :].rearrange("p (i n) -> p i n", n=P)
                if c == "ik":
                    act.copy(k.ikT[:, r * P:r * P + n], src[:, 0, 0:n]).then_inc(copied, 1)
                else:
                    act.copy(turns[c][:, :, r * P:r * P + n], src[:, :, 0:n]).then_inc(copied, 1)

            for j in range(len(jobs)):
                take(j)
                if j - LAG in nth_rot:
                    copy_turned(j - LAG)
            for j in range(len(jobs) - LAG, len(jobs)):
                if j in nth_rot:
                    copy_turned(j)

        @block.gpsimd
        def _(pool):
            for j, (c, r) in enumerate(jobs):
                if c not in rotated:
                    continue
                n, t = rows_of(r), nth_rot[j]
                heads = 1 if c == "ik" else H
                cols = heads * DH
                pool.wait_ge(taken, j + 1)
                if t >= RAW:
                    pool.wait_ge(turned, t - RAW + 1)
                if stores_before(j):
                    pool.wait_ge(stored[j % RAW], 16 * stores_before(j))
                x = raw[0:n, j % RAW, 0:cols].rearrange("p (h t d) -> p h t d", h=heads, t=2)
                table = k.rope[0:n, r, :].rearrange("p (a t d) -> p a t d", a=2, t=2)
                for a, v in ((0, x), (1, x[:, :, ::-1, :])):
                    pool.tensor_tensor(part[0:n, a, 0:cols].rearrange("p (h t d) -> p h t d", h=heads, t=2), v,
                                       table[:, a, :, :][:, None, :, :].broadcast_to([n, heads, 2, DH // 2]), ALU.mult)
                pool.drain()
                if c == "ik":
                    pool.tensor_tensor(rot[0:n, j % RAW, cols:2 * cols], part[0:n, 0, 0:cols], part[0:n, 1, 0:cols], ALU.add)
                pool.tensor_tensor(rot[0:n, j % RAW, 0:cols], part[0:n, 0, 0:cols], part[0:n, 1, 0:cols],
                                   ALU.add).then_inc(roped, 1)
                pool.drain()



def project_gates(k):
    nc, io, ps, hT = k.nc, k.io, k.ps, k.hT
    w_in = io["w_in"][0].rearrange("(k p) n -> p k n", p=P)
    with ExitStack() as ctx:
        w = k.sb(ctx, "w_gate_chunk", [P, 2, KD, 512])
        out = k.sb(ctx, "gate_out", [P, 2, R])
        keyf = k.sb(ctx, "gate_key", [P, R])
        f = k.sb(ctx, "forget", [P, BH, R])
        reset = k.sb(ctx, "reset", [P, R])
        lb = k.sb(ctx, "lb", [P, 8, BH])
        w_landed, const_landed, stored_q, stored_k, stored_b = k.sems(
            ctx, "w_landed", "const_landed", "stored_q", "stored_k", "stored_b")
        multiplied, taken, lb_ready, exped, sig_taken, f_made, key_made, log_taken, scanned = k.sems(
            ctx, "multiplied", "taken", "lb_ready", "exped", "sig_taken", "f_made", "key_made", "log_taken", "scanned")
        block = ctx.enter_context(nc.Block())
        lb_value, lb_rest = lb[:, 0, :], lb[:, 1, :]

        @block.sync
        def _(sp):
            sp.dma_start(w[:, 0], w_in[:, :, COL["bq"]:COL["bq"] + 512]).then_inc(w_landed, 16)
            sp.dma_start(w[:, 1], w_in[:, :, COL["bf"]:COL["bf"] + 512]).then_inc(w_landed, 16)
            sp.dma_start(reset[:], io["c_reset"].broadcast_to([P, R])).then_inc(const_landed, 16)
            for i in range(BH):
                sp.wait_ge(taken, i + 1)
                sp.dma_start(k.scratch["gq"][i], out[:, i % 2, :]).then_inc(stored_q, 16)
                if i < BH - 1:
                    sp.wait_ge(stored_q, 16 * (i + 1))
            sp.wait_ge(stored_q, 16 * BH)
            for i in range(BH):
                sp.wait_ge(key_made, i + 1)
                sp.dma_start(k.scratch["gk"][i], keyf[:]).then_inc(stored_k, 16)
                sp.wait_ge(stored_k, 16 * (i + 1))
            for i in range(BH):
                sp.wait_ge(scanned, i + 1)
                sp.dma_start(k.scratch["gb"][i], out[:, i % 2, :]).then_inc(stored_b, 16)
                sp.wait_ge(stored_b, 16 * (i + 1))

        @block.tensor
        def _(pe):
            pe.wait_ge(w_landed, 32)
            for i in range(2 * BH):
                b = 4 * (i % 2)
                if i >= 2:
                    pe.wait_ge(taken, i - 1)
                for d in range(KD):
                    for g in range(G):
                        m = pe.matmul(ps[:, b + g, 0:GC], w[:, i // BH, d, (i % BH) * P:(i % BH + 1) * P],
                                      hT[:, d, g * GC:(g + 1) * GC], start=d == 0, stop=d == KD - 1)
                m.then_inc(multiplied, 1)

        @block.scalar
        def _(act):
            act.wait_ge(lb_ready, 1)
            for i in range(2):
                act.activation(lb[:, 2 + i, :], lb[:, 2 + i, :], ACT.Exp).then_inc(exped, 1)
            for i in range(BH):
                act.wait_ge(multiplied, i + 1)
                if i >= 2:
                    act.wait_ge(stored_q, 16 * (i - 1))
                act.activation(grouped(out[:, i % 2, :]), bank_cols(ps, 4 * (i % 2)), ACT.Silu).then_inc(taken, 1)
            for i in range(BH):
                act.wait_ge(multiplied, BH + i + 1)
                act.activation(grouped(f[:, i, :]), bank_cols(ps, 4 * (i % 2)), ACT.Sigmoid).then_inc(sig_taken, 1)
                if i >= 1:
                    act.wait_ge(stored_k, 16 * i)
                act.activation(grouped(keyf[:]), bank_cols(ps, 4 * (i % 2)), ACT.Sigmoid, scale=-1.0).then_inc(taken, 1)
            for i in range(BH):
                act.wait_ge(f_made, i + 1)
                act.activation(f[:, i, :], f[:, i, :], ACT.Ln).then_inc(log_taken, 1)

        @block.vector
        def _(dve):
            dve.tensor_tensor(lb[:, 4, :], k.lb_logit[0], k.lb_logit[1], ALU.max)
            dve.drain()
            for i in range(2):
                dve.tensor_tensor(lb[:, 2 + i, :], k.lb_logit[i], lb[:, 4, :], ALU.subtract)
            dve.drain()
            dve.tensor_copy(lb[:, 5, :], lb[:, 4, :]).then_inc(lb_ready, 1)
            dve.wait_ge(exped, 2)
            dve.tensor_tensor(lb[:, 6, :], lb[:, 2, :], lb[:, 3, :], ALU.add)
            dve.drain()
            dve.reciprocal(lb[:, 7, :], lb[:, 6, :])
            dve.drain()
            dve.tensor_tensor(lb_value, lb[:, 2, :], lb[:, 7, :], ALU.mult)
            dve.drain()
            dve.tensor_scalar(lb_rest, lb_value, -1.0, 1.0, ALU.mult, ALU.add)
            dve.drain()
            for i in range(BH):
                dve.wait_ge(sig_taken, i + 1)
                dve.tensor_scalar(f[:, i, :], f[:, i, :], lb_rest[:, i:i + 1], lb_value[:, i:i + 1],
                                  ALU.mult, ALU.add).then_inc(f_made, 1)
                dve.wait_ge(taken, BH + i + 1)
                dve.tensor_scalar(keyf[:], keyf[:], lb_rest[:, i:i + 1], None, ALU.mult).then_inc(key_made, 1)
            dve.wait_ge(const_landed, 16)
            for i in range(BH):
                dve.wait_ge(log_taken, i + 1)
                if i >= 2:
                    dve.wait_ge(stored_b, 16 * (i - 1))
                else:
                    dve.wait_ge(stored_q, 16 * BH)
                dve.tensor_tensor_scan(out[:, i % 2, :], reset[:], f[:, i, :], 0.0, ALU.mult, ALU.add).then_inc(scanned, 1)



def recurrence(k):
    nc, io, ps, mixT = k.nc, k.io, k.ps, k.hT
    tiles = NT + 1
    with ExitStack() as ctx:
        q = k.sb(ctx, "g_q", [P, 2, BH, P])
        key = k.sb(ctx, "g_key", [P, 2, BH, P])
        b = k.sb(ctx, "g_b", [P, 2, BH, P])
        val = k.sb(ctx, "g_val", [P, 2, BH, P])
        gate = k.sb(ctx, "g_gate", [P, 2, BH, P])
        dif = k.sb(ctx, "g_dif", [P, 2, BH * P])
        uq = k.sb(ctx, "g_uq", [P, 2, BH, P])
        uk = k.sb(ctx, "g_uk", [P, 2, BH, P])
        att = k.sb(ctx, "g_att", [P, BH, P])
        eb = k.sb(ctx, "g_eb", [P, BH, P])
        el = k.sb(ctx, "g_el", [P, BH, P])
        qe = k.sb(ctx, "g_qe", [P, BH, P])
        ke = k.sb(ctx, "g_ke", [P, BH, P])
        ker = k.sb(ctx, "g_ker", [P, BH, P])
        state = k.sb(ctx, "g_state", [P, BH, P])
        osq = k.sb(ctx, "g_osq", [P, BH, P])
        on = k.sb(ctx, "g_on", [P, BH, P])
        small = k.sb(ctx, "g_small", [P, 4, BH])
        normw = k.sb(ctx, "g_normw", [P, P])
        level = k.sb(ctx, "g_level", [P, LEVELS + 1, P], I32)
        s0 = k.sb(ctx, "g_s0", [P, BD * BH, P])
        snew = k.sb(ctx, "g_snew", [P, 2, BD, P])
        qm = k.sb(ctx, "g_qm", [P, BH, BD, NS])
        vm = k.sb(ctx, "g_vm", [NS, BH, BD, P])
        bcol = k.sb(ctx, "g_bcol", [P, BD * NS])
        brow = k.sb(ctx, "g_brow", [NS, BD])
        landed = k.sem_ring(ctx, "g_landed", 2)
        const, s0_landed, state_stored = k.sems(ctx, "g_const", "g_s0_landed", "g_state_stored")
        (dif_made, exped, scaled, multiplied, placed, edge_dif, edge_exp, qe_made, ke_turned, ke_copied, out_done,
         update_done, updated, squared, means, rstd_made, gated, out_turned, out_copied, s_update, snew_made,
         qm_made, tile_read) = k.sems(
            ctx, "g_dif_made", "g_exped", "g_scaled", "g_multiplied", "g_placed", "g_edge_dif", "g_edge_exp",
            "g_qe_made", "g_ke_turned", "g_ke_copied", "g_out_done", "g_update_done", "g_updated", "g_squared",
            "g_means", "g_rstd_made", "g_gated", "g_out_turned", "g_out_copied", "g_s_update", "g_snew_made",
            "g_qm_made", "g_tile_read")
        block = ctx.enter_context(nc.Block())

        def levels_of(c):
            return list(range(LEVELS)) if c < NT else list(range(int(math.log2(TD))))

        def level_count(c):
            return sum(len(levels_of(i)) for i in range(c))

        def product_count(c):
            return level_count(c) + c

        scr = k.scratch

        @block.sync
        def _(sp):
            sp.dma_start(normw[:], io["glr_norm"].broadcast_to([P, P])).then_inc(const, 16)
            sp.dma_start(level[:], io["c_level"]).then_inc(const, 16)
            sp.dma_start(bcol[:], io["c_batchcol"].broadcast_to([P, BD * NS])).then_inc(const, 16)
            sp.dma_start(brow[:], io["c_batchrow"]).then_inc(const, 16)
            sp.dma_start(s0[:], io["state_glr"][0].rearrange("b h d v -> d (b h) v")).then_inc(s0_landed, 16)
            for c in range(tiles):
                n = rows_of(c)
                if c >= 2:
                    sp.wait_ge(tile_read, c - 1)
                for buf, name in ((q, "gq"), (key, "gk"), (b, "gb")):
                    sp.dma_start(buf[:, c % 2, :, 0:n], scr[name].rearrange("h d t -> d h t")[:, :, c * P:c * P + n]
                                 ).then_inc(landed[c % 2], 16)
                for buf, name in ((val, "bi"), (gate, "bg")):
                    sp.dma_start(buf[0:n, c % 2], scr[name][c * P:c * P + n].rearrange("t (h v) -> t h v", h=BH)
                                 ).then_inc(landed[c % 2], 16)
            sp.wait_ge(updated, NT)
            sp.dma_start(io["glr_prompt"][0, 0].rearrange("h d v -> d h v"), state[:]).then_inc(state_stored, 16)
            for h in range(BH):
                sp.wait_ge(snew_made, h + 1)
                sp.dma_start(io["glr_sample"][0].rearrange("b h d v -> h d b v")[h], snew[:, h % 2]).then_inc(state_stored, 16)
                sp.wait_ge(state_stored, 16 * (h + 2))

        @block.vector
        def _(dve):
            dve.memset(att[:], 0.0)
            dve.memset(state[:], 0.0)
            dve.memset(uq[:], 0.0)
            dve.memset(uk[:], 0.0)
            dve.memset(dif[:], 0.0)
            dve.wait_ge(const, 64)
            dve.drain()
            for c in range(tiles):
                n, s = rows_of(c), c % 2
                lv = levels_of(c)
                dve.wait_ge(landed[s], 80 * (c // 2 + 1))
                bt, qt, kt = b[:, s, :, 0:n], q[:, s, :, 0:n], key[:, s, :, 0:n]

                def halves(ap, w):
                    return ap.rearrange("p h (m a w) -> p h m a w", a=2, w=w)

                def make_dif(i):
                    w = 1 << lv[i]
                    e = level_count(c) + i
                    if e >= 2:
                        dve.wait_ge(scaled, e - 1)
                    d4 = dif[:, e % 2, 0:BH * n].rearrange("p (h m a w) -> p h m a w", h=BH, a=2, w=w)
                    b4 = halves(bt, w)
                    ref = b4[:, :, :, 0, w - 1:w].broadcast_to([P, BH, n // (2 * w), w])
                    dve.tensor_tensor(d4[:, :, :, 0, :], ref, b4[:, :, :, 0, :], ALU.subtract)
                    dve.tensor_tensor(d4[:, :, :, 1, :], b4[:, :, :, 1, :], ref, ALU.subtract).then_inc(dif_made, 1)

                def scale(i):
                    w = 1 << lv[i]
                    e = level_count(c) + i
                    dve.wait_ge(exped, e + 1)
                    u = product_count(c) + i
                    if e >= 2:
                        before = u - 2 if i >= 2 else (product_count(c - 1) + len(levels_of(c - 1)) - 2 + i if c else 0)
                        dve.wait_ge(multiplied, before + 1)
                    d4 = dif[:, e % 2, 0:BH * n].rearrange("p (h m a w) -> p h m a w", h=BH, a=2, w=w)
                    dve.tensor_tensor(halves(uk[:, e % 2, :, 0:n], w)[:, :, :, 0, :], halves(kt, w)[:, :, :, 0, :],
                                      d4[:, :, :, 0, :], ALU.mult)
                    dve.tensor_tensor(halves(uq[:, e % 2, :, 0:n], w)[:, :, :, 1, :], halves(qt, w)[:, :, :, 1, :],
                                      d4[:, :, :, 1, :], ALU.mult).then_inc(scaled, 1)

                def place(i):
                    u = product_count(c) + i
                    lvl = lv[i] if i < len(lv) else LEVELS
                    dve.wait_ge(multiplied, u + 1)
                    if i == 0 and c:
                        dve.wait_ge(out_done, c)
                        if c == NT:
                            dve.memset(att[0:n, :, 0:n], 0.0)
                            dve.drain()
                    src = ps[0:n, u % 2, :].rearrange("p (h t) -> p h t", h=BH)[:, :, 0:n]
                    dve.copy_predicated(att[0:n, :, 0:n], level[0:n, lvl, 0:n][:, None, :].broadcast_to([n, BH, n]), src
                                        ).then_inc(placed, 1)
                    dve.drain()

                span = P if c < NT else TD
                if c:
                    dve.wait_ge(ke_turned, c)
                bs = bt.rearrange("p h (m w) -> p h m w", w=span)
                dve.tensor_tensor(el[:, :, 0:n].rearrange("p h (m w) -> p h m w", w=span),
                                  bs[:, :, :, span - 1:span].broadcast_to([P, BH, n // span, span]), bs, ALU.subtract
                                  ).then_inc(edge_dif, 1)
                make_dif(0)
                for i in range(len(lv)):
                    if i + 1 < len(lv):
                        make_dif(i + 1)
                    scale(i)
                    if i == 0:
                        dve.wait_ge(edge_exp, c + 1)
                        if c:
                            dve.wait_ge(out_done, c)
                        dve.tensor_tensor(ke[:, :, 0:n], kt, el[:, :, 0:n], ALU.mult)
                        dve.tensor_tensor(qe[:, :, 0:n], qt, eb[:, :, 0:n], ALU.mult).then_inc(qe_made, 1)
                        dve.drain()
                    if i:
                        place(i - 1)
                place(len(lv) - 1)
                place(len(lv))
                if c == NT:
                    for h in range(BH):
                        x = dve.tensor_tensor(qm[:, h], qe[:, h, 0:n][:, None, :].broadcast_to([P, BD, NS]),
                                              bcol[:].rearrange("p (b t) -> p b t", b=BD), ALU.mult)
                        y = dve.tensor_tensor(vm[:, h], val[0:NS, s, h, :][:, None, :].broadcast_to([NS, BD, P]),
                                              brow[:, :, None].broadcast_to([NS, BD, P]), ALU.mult)
                    y.then_inc(qm_made, 1)
                if c < NT:
                    dve.wait_ge(update_done, c + 1)
                    dve.wait_ge(out_done, c + 1)
                    for h in range(BH):
                        x = dve.scalar_tensor_tensor(state[:, h, :], state[:, h, :], eb[:, h, P - 1:P],
                                                     ps[:, 4, h * P:(h + 1) * P], ALU.mult, ALU.add)
                    x.then_inc(updated, 1)
                else:
                    dve.wait_ge(s0_landed, 16)
                    s0v = s0[:].rearrange("p (b h) v -> p b h v", h=BH)
                    for h in range(BH):
                        if h >= 2:
                            dve.wait_ge(state_stored, 16 * h)
                        last = eb[:, h, TD - 1:NS:TD]
                        dve.tensor_tensor(snew[:, h % 2], s0v[:, :, h, :], last[:, :, None].broadcast_to([P, BD, P]), ALU.mult)
                        dve.drain()
                        dve.wait_ge(s_update, h + 1)
                        dve.tensor_tensor(snew[:, h % 2], snew[:, h % 2],
                                          ps[:, 0:2, :].rearrange("p a (b v) -> p (a b) v", v=P), ALU.add).then_inc(snew_made, 1)
                        dve.drain()
                dve.wait_ge(squared, c + 1)
                dve.tensor_reduce(small[0:n, 0, :], osq[0:n], AX.X, ALU.add)
                dve.drain()
                dve.tensor_scalar(small[0:n, 1, :], small[0:n, 0, :], 1.0 / P, EPS, ALU.mult, ALU.add).then_inc(means, 1)
                dve.wait_ge(rstd_made, c + 1)
                if c:
                    dve.wait_ge(out_turned, c)
                dve.tensor_tensor(on[0:n], ps[0:n, 3, :].rearrange("p (h v) -> p h v", h=BH),
                                  small[0:n, 2, :][:, :, None].broadcast_to([n, BH, P]), ALU.mult)
                dve.drain()
                dve.tensor_tensor(on[0:n], on[0:n], normw[0:n][:, None, :].broadcast_to([n, BH, P]), ALU.mult)
                dve.drain()
                dve.tensor_tensor(on[0:n], on[0:n], gate[0:n, s], ALU.mult).then_inc(gated, 1)
                dve.drain()

        @block.scalar
        def _(act):
            for c in range(tiles):
                n, s = rows_of(c), c % 2
                lv = levels_of(c)
                act.wait_ge(edge_dif, c + 1)
                if c:
                    act.wait_ge(updated, c)
                act.activation(eb[:, :, 0:n], b[:, s, :, 0:n], ACT.Exp)
                act.activation(el[:, :, 0:n], el[:, :, 0:n], ACT.Exp).then_inc(edge_exp, 1)
                for i in range(len(lv)):
                    e = level_count(c) + i
                    act.wait_ge(dif_made, e + 1)
                    act.activation(dif[:, e % 2, 0:BH * n], dif[:, e % 2, 0:BH * n], ACT.Exp).then_inc(exped, 1)
                act.wait_ge(ke_turned, c + 1)
                act.copy(ker[0:n], ps[0:n, 2, :].rearrange("p (h d) -> p h d", h=BH)).then_inc(ke_copied, 1)
                act.wait_ge(out_done, c + 1)
                if c:
                    act.wait_ge(means, c)
                act.activation(osq[0:n], ps[0:n, 3, :].rearrange("p (h v) -> p h v", h=BH), ACT.Square).then_inc(squared, 1)
                act.wait_ge(out_turned, c + 1)
                src = ps[:, 5, :].rearrange("p (h t) -> p h t", h=BH)
                act.copy(mixT[:, BH:2 * BH, c * P:c * P + n], src[:, :, 0:n]).then_inc(out_copied, 1)

        @block.gpsimd
        def _(pool):
            pool.memset(small[:, 3, :], -0.5)
            pool.drain()
            for c in range(tiles):
                n = rows_of(c)
                pool.wait_ge(means, c + 1)
                if c:
                    pool.wait_ge(gated, c)
                pool.tensor_tensor(small[0:n, 2, :], small[0:n, 1, :], small[0:n, 3, :], ALU.pow).then_inc(rstd_made, 1)

        @block.tensor
        def _(pe):
            for c in range(tiles):
                n, s = rows_of(c), c % 2
                lv = levels_of(c)
                pe.wait_ge(landed[s], 80 * (c // 2 + 1))

                def product(i):
                    u = product_count(c) + i
                    if u >= 2:
                        pe.wait_ge(placed, u - 1)
                    e = level_count(c) + i
                    if i < len(lv):
                        pe.wait_ge(scaled, e + 1)
                    for h in range(BH):
                        lhs = uk[:, e % 2, h, 0:n] if i < len(lv) else key[:, s, h, 0:n]
                        rhs = uq[:, e % 2, h, 0:n] if i < len(lv) else q[:, s, h, 0:n]
                        m = pe.matmul(ps[0:n, u % 2, h * P:h * P + n], lhs, rhs, start=True, stop=True)
                    m.then_inc(multiplied, 1)

                for i in range(len(lv) + 1):
                    product(i)
                    if i == 0:
                        pe.wait_ge(qe_made, c + 1)
                        if c:
                            pe.wait_ge(ke_copied, c)
                        for h in range(BH):
                            m = pe.transpose(ps[0:n, 2, h * P:(h + 1) * P], ke[:, h, 0:n], k.ident[:])
                        m.then_inc(ke_turned, 1)
                pe.wait_ge(placed, product_count(c + 1))
                if c:
                    pe.wait_ge(updated, c)
                    pe.wait_ge(gated, c)
                if c == NT:
                    pe.wait_ge(qm_made, 1)
                    pe.wait_ge(s0_landed, 16)
                for h in range(BH):
                    o = ps[0:n, 3, h * P:(h + 1) * P]
                    pe.matmul(o, att[0:n, h, 0:n], val[0:n, s, h, :], start=True, stop=False)
                    if c < NT:
                        m = pe.matmul(o, qe[:, h, :], state[:, h, :], start=False, stop=True)
                    else:
                        for e in range(BD):
                            m = pe.matmul(o, qm[:, h, e, :], s0[:, e * BH + h, :], start=False, stop=e == BD - 1)
                m.then_inc(out_done, 1)
                pe.wait_ge(ke_copied, c + 1)
                if c < NT:
                    for h in range(BH):
                        m = pe.matmul(ps[:, 4, h * P:(h + 1) * P], ker[0:n, h, :], val[0:n, s, h, :], start=True, stop=True)
                    m.then_inc(update_done, 1)
                else:
                    for h in range(BH):
                        if h:
                            pe.wait_ge(snew_made, h)
                        for a in range(2):
                            m = pe.matmul(ps[:, a, :], ker[0:n, h, :], vm[:, h, a * 4:(a + 1) * 4, :].rearrange("p b v -> p (b v)"),
                                          start=True, stop=True)
                        m.then_inc(s_update, 1)
                pe.wait_ge(gated, c + 1)
                if c:
                    pe.wait_ge(out_copied, c)
                for h in range(BH):
                    m = pe.transpose(ps[:, 5, h * P:h * P + n], on[0:n, h, :], k.ident[0:n, 0:n])
                m.then_inc(out_turned, 1)
                pe.matmul(ps[0:1, 6, 0:1], k.ones[:, 0:1], k.ones[:, 0:1], start=True, stop=True).then_inc(tile_read, 1)



def mask_offset(i):
    return sum((j + 1) * P for j in range(2, i))


def select_prompt(k):
    nc, ps = k.nc, k.ps
    steps = [(i, h) for i in range(2, NT) for h in range(H)]
    with ExitStack() as ctx:
        relu = k.sb(ctx, "relu", [P, 2, SEQ])
        best = k.sb(ctx, "best", [P, 8])
        scored, rectified, summed, masked = k.sems(ctx, "scored", "rectified", "summed", "masked")
        block = ctx.enter_context(nc.Block())

        def scores(i):
            return k.masks[:, mask_offset(i):mask_offset(i) + (i + 1) * P]

        @block.tensor
        def _(pe):
            for u, (i, h) in enumerate(steps):
                w, row = (i + 1) * P, (h % 2) * DH
                if u >= 4:
                    pe.wait_ge(rectified, u - 3)
                for a in range(0, w, 512):
                    n = min(512, w - a)
                    m = pe.matmul(ps[:, 2 * (u % 4) + a // 512, 0:n], k.iqT[row:row + DH, h // 2, i * P:(i + 1) * P],
                                  k.ikT[row:row + DH, a:a + n], start=True, stop=True)
                m.then_inc(scored, 1)

        @block.scalar
        def _(act):
            for u, (i, h) in enumerate(steps):
                w = (i + 1) * P
                act.wait_ge(scored, u + 1)
                if u >= 2:
                    act.wait_ge(summed, u - 1)
                act.activation(relu[:, u % 2, 0:w], ps[:, 2 * (u % 4):2 * (u % 4) + 2, :].rearrange("p b n -> p (b n)")[:, 0:w],
                               ACT.Relu).then_inc(rectified, 1)

        @block.gpsimd
        def _(pool):
            for i in range(2, NT):
                pool.wait_ge(summed, (i - 1) * H)
                diag = scores(i)[:, i * P:(i + 1) * P]
                pool.affine_select(out=diag, in_=diag, compare_op=ALU.is_ge, fill=UNSEEN, base=0,
                                   pattern=[[-1, P]], channel_multiplier=1).then_inc(masked, 1)

        @block.vector
        def _(dve):
            for u, (i, h) in enumerate(steps):
                w = (i + 1) * P
                sc = scores(i)
                dve.wait_ge(rectified, u + 1)
                if h == 0:
                    dve.tensor_scalar(sc, relu[:, u % 2, 0:w], k.iw[:, i, 0:1], None, ALU.mult).then_inc(summed, 1)
                else:
                    dve.scalar_tensor_tensor(sc, relu[:, u % 2, 0:w], k.iw[:, i, h:h + 1], sc, ALU.mult, ALU.add
                                             ).then_inc(summed, 1)
                dve.drain()
                if h == H - 1:
                    dve.wait_ge(masked, i - 1)
                    with dve.Fori(0, ROUNDS):
                        dve.max(best[:], sc)
                        dve.drain()
                        dve.match_replace(sc, best[:], sc, TAKEN)
                        dve.drain()
                    dve.tensor_scalar(sc, sc, TAKEN, MASKED, ALU.is_gt, ALU.mult)



def attend_prompt(k):
    nc, io, ps, mixT = k.nc, k.io, k.ps, k.hT
    steps = [(i, h) for i in range(NT) for h in range(H)]
    scale = DH ** -0.5
    with ExitStack() as ctx:
        v = k.sb(ctx, "v_rows", [P, NT, H * DH])
        causal = k.sb(ctx, "causal", [P, 2, 2 * P])
        logit = k.sb(ctx, "logit", [P, 2, SEQ])
        prob = k.sb(ctx, "prob", [P, 2, SEQ])
        probT = k.sb(ctx, "probT", [P, 2, NT, P])
        top = k.sb(ctx, "top", [P, 2, 2])
        total = k.sb(ctx, "total", [P, 2, H])
        inv = k.sb(ctx, "inv", [P, H])
        att = k.sb(ctx, "att_rows", [P, 2, H * DH])
        v_landed, c_landed = k.sems(ctx, "v_landed", "c_landed")
        scored, biased, exped, turned, copied, weighed, normed, att_turned, att_copied = k.sems(
            ctx, "scored", "biased", "exped", "turned", "copied", "weighed", "normed", "att_turned", "att_copied")
        block = ctx.enter_context(nc.Block())

        def two_banks(b):
            return ps[:, b:b + 2, :].rearrange("p b n -> p (b n)")

        @block.sync
        def _(sp):
            sp.dma_start(causal[:, 0, 0:P], io["c_causal"]).then_inc(c_landed, 16)
            sp.dma_start(causal[:, 1, P:2 * P], io["c_causal"]).then_inc(c_landed, 16)
            sp.dma_start(v[:], io["v_prompt"].rearrange("(i p) n -> p i n", p=P)).then_inc(v_landed, 16)

        @block.tensor
        def _(pe):
            def score(u):
                i, h = steps[u]
                w, row = (i + 1) * P, (h % 2) * DH
                if u >= 2:
                    pe.wait_ge(biased, u - 1)
                for a in range(0, w, 512):
                    n = min(512, w - a)
                    m = pe.matmul(ps[:, 2 * (u % 2) + a // 512, 0:n], k.qT[row:row + DH, h // 2, i * P:(i + 1) * P],
                                  k.kT[row:row + DH, h // 2, a:a + n], start=True, stop=True)
                m.then_inc(scored, 1)

            def turn(u):
                i, h = steps[u]
                pe.wait_ge(exped, u + 1)
                if u:
                    pe.wait_ge(copied, u)
                for j in range(i + 1):
                    m = pe.transpose(ps[:, 4 + j // 4, (j % 4) * P:(j % 4 + 1) * P], prob[:, u % 2, j * P:(j + 1) * P], k.ident[:])
                m.then_inc(turned, 1)

            def weigh(u):
                i, h = steps[u]
                pe.wait_ge(copied, u + 1)
                if h == 0:
                    pe.wait_ge(v_landed, 16)
                    if i:
                        pe.wait_ge(normed, i)
                for j in range(i + 1):
                    m = pe.matmul(ps[:, 6, h * DH:(h + 1) * DH], probT[:, u % 2, j, :], v[:, j, h * DH:(h + 1) * DH],
                                  start=j == 0, stop=j == i)
                m.then_inc(weighed, 1)

            def turn_att(i):
                pe.wait_ge(normed, i + 1)
                if i:
                    pe.wait_ge(att_copied, i)
                for f in range(4):
                    m = pe.transpose(ps[:, 7, f * P:(f + 1) * P], att[:, i % 2, f * P:(f + 1) * P], k.ident[:])
                m.then_inc(att_turned, 1)

            score(0)
            for u in range(len(steps) + 1):
                if u + 1 < len(steps):
                    score(u + 1)
                if u < len(steps):
                    turn(u)
                if u:
                    weigh(u - 1)
                if u >= 10 and (u - 10) % H == 0:
                    turn_att((u - 10) // H)
            turn_att(NT - 1)

        @block.vector
        def _(dve):
            dve.memset(causal[:, 1, 0:P], 0.0)
            dve.wait_ge(c_landed, 32)
            dve.drain()

            def bias(u):
                i, h = steps[u]
                w = (i + 1) * P
                mask = causal[:, i, 0:w] if i < 2 else k.masks[:, mask_offset(i):mask_offset(i) + w]
                dve.wait_ge(scored, u + 1)
                if u >= 2:
                    dve.wait_ge(exped, u - 1)
                dve.tensor_tensor_reduce(logit[:, u % 2, 0:w], two_banks(2 * (u % 2))[:, 0:w], mask, 1.0, UNSEEN,
                                         ALU.add, ALU.max, top[:, u % 2, 0:1])
                dve.drain()
                dve.tensor_scalar(top[:, u % 2, 1:2], top[:, u % 2, 0:1], -scale, None, ALU.mult).then_inc(biased, 1)

            def normalise(i):
                dve.wait_ge(weighed, (i + 1) * H)
                if i >= 2:
                    dve.wait_ge(att_turned, i - 1)
                dve.reciprocal(inv[:], total[:, i % 2, :])
                dve.drain()
                dve.tensor_tensor(att[:, i % 2].rearrange("p (h d) -> p h d", h=H), ps[:, 6, :].rearrange("p (h d) -> p h d", h=H),
                                  inv[:][:, :, None].broadcast_to([P, H, DH]), ALU.mult).then_inc(normed, 1)
                dve.drain()

            for u in range(len(steps)):
                bias(u)
                if u >= H and u % H == 1:
                    normalise(u // H - 1)
            normalise(NT - 1)

        @block.scalar
        def _(act):
            def exp(u):
                i, h = steps[u]
                w = (i + 1) * P
                act.wait_ge(biased, u + 1)
                if u >= 2:
                    act.wait_ge(turned, u - 1)
                if h == 0 and i >= 2:
                    act.wait_ge(normed, i - 1)
                act.activation(prob[:, u % 2, 0:w], logit[:, u % 2, 0:w], ACT.Exp, bias=top[:, u % 2, 1:2], scale=scale,
                               accum_out=total[:, i % 2, h:h + 1])
                act.drain()
                act.copy(top[0:1, u % 2, 0:1], top[0:1, u % 2, 1:2]).then_inc(exped, 1)

            def copy(u):
                i, h = steps[u]
                act.wait_ge(turned, u + 1)
                if u >= 2:
                    act.wait_ge(weighed, u - 1)
                act.copy(probT[:, u % 2].rearrange("p j n -> p (j n)")[:, 0:(i + 1) * P], two_banks(4)[:, 0:(i + 1) * P]
                         ).then_inc(copied, 1)

            def copy_att(i):
                act.wait_ge(att_turned, i + 1)
                act.copy(mixT[:, 0:4, i * P:(i + 1) * P], ps[:, 7, :].rearrange("p (f n) -> p f n", f=4)).then_inc(att_copied, 1)

            exp(0)
            for u in range(len(steps)):
                copy(u)
                if u + 1 < len(steps):
                    exp(u + 1)
                if u >= 11 and (u - 11) % H == 0:
                    copy_att((u - 11) // H)
            copy_att(NT - 1)



def score_sample(k):
    nc, io, ps = k.nc, k.io, k.ps
    N = BD * 4
    E16 = PAGE // 8
    with ExitStack() as ctx:
        pages = k.sb(ctx, "pages", [P, N], I32)
        index = k.sb(ctx, "index", [P, N], I32)
        keys = k.sb(ctx, "keys", [P, 4, E16 * DH])
        keysT = k.sb(ctx, "keysT", [P, 2, 8, P])
        part = k.sb(ctx, "part", [P, 2, 8 * 2 * TD * H])
        iq2 = k.sb(ctx, "iq_twice", [NS, H, 2, DH])
        bd = k.sb(ctx, "iq_blocks", [P, BD, 2, TD, H])
        wb = k.sb(ctx, "iw_all", [P, NS, H])
        sc = k.sb(ctx, "key_scores", [P, E16, 4, NS])
        newp = k.sb(ctx, "new_part", [NS, NS * H])
        news = k.sb(ctx, "new_scores", [NS, NS])
        newt = k.sb(ctx, "new_turned", [NS, NS])
        newb = k.sb(ctx, "new_bias", [NS, NS])
        newq = k.sb(ctx, "new_query", [NS, TD])
        g_landed = k.sem_ring(ctx, "keys_landed", 4)
        pt_landed, small_landed, placed = k.sems(ctx, "pt_landed", "small_landed", "placed")
        (indexed, turned, copied, multiplied, weighted, iq_turned, blocks_made, new_scored, new_summed, new_turned,
         new_ready, sc_turned, sc_copied, zeroed, reduced) = k.sems(
            ctx, "indexed", "turned", "copied", "multiplied", "weighted", "iq_turned", "blocks_made", "new_scored",
            "new_summed", "new_turned", "new_ready", "sc_turned", "sc_copied", "zeroed", "reduced")
        block = ctx.enter_context(nc.Block())

        @block.sync
        def _(sp):
            src = io["page_table"].rearrange("b (k i) -> i b k", i=16)
            for s in range(8):
                sp.dma_start(pages[s:P:8, :].rearrange("p (b k) -> p b k", b=BD), src,
                             allow_slow_non_contiguous=True).then_inc(pt_landed, 16)
            iq = k.scratch["iq_s"].rearrange("r (h d) -> r h d", h=H)
            for a in range(2):
                sp.dma_start(iq2[:, :, a, :], iq).then_inc(small_landed, 16)
            sp.dma_start(wb[:].rearrange("p q h -> p (q h)"),
                         k.scratch["iw_s"].rearrange("(o q) h -> o (q h)", o=1).broadcast_to([P, NS * H])).then_inc(small_landed, 16)
            sp.dma_start(newb[:], io["c_newbias"]).then_inc(small_landed, 16)
            sp.wait_ge(new_ready, 1)
            sp.wait_ge(zeroed, 1)
            sp.dma_start(k.found[3 * NS:P, QUARTER:QUARTER + TD], newq[:]).then_inc(placed, 16)
            sp.wait_ge(placed, 16)

        @block.gpsimd
        def _(pool):
            view = io["cache_kidx"][0].rearrange("g (s e) d -> (g s) (e d)", s=8)
            pool.wait_ge(indexed, 1)
            for j in range(N):
                if j >= 4:
                    pool.wait_ge(turned, 2 * (j - 3))
                pool.indirect_dma_start(keys[:, j % 4], None, view,
                                        bass.IndirectOffsetOnAxis(ap=index[:, j:j + 1].bitcast(U32), axis=0)
                                        ).then_inc(g_landed[j % 4], 16)

        @block.tensor
        def _(pe):
            pe.wait_ge(small_landed, 64)
            for h in range(H):
                m = pe.transpose(ps[:, 7, h * NS:(h + 1) * NS], iq2[:, h].rearrange("p a d -> p (a d)"), k.ident[0:NS, 0:NS])
            m.then_inc(iq_turned, 1)
            pe.wait_ge(blocks_made, 1)
            pe.matmul(ps[0:NS, 6, 0:NS * H].rearrange("p (b q) -> p b q", b=BD), k.ikT[0:DH, SEQ:R],
                      bd[0:DH, :, 0].rearrange("p b t h -> p b (t h)"), start=True, stop=True).then_inc(new_scored, 1)

            def turn(j):
                pe.wait_ge(g_landed[j % 4], 16 * (j // 4 + 1))
                for a in range(2):
                    if j:
                        pe.wait_ge(copied, 2 * j + a - 1)
                    for e in range(4):
                        x = 2 * (4 * a + e) * DH
                        m = pe.transpose(ps[:, a, e * P:(e + 1) * P], keys[:, j % 4, x:x + 2 * DH], k.ident[:])
                    m.then_inc(turned, 1)

            def multiply(j):
                if j >= 2:
                    pe.wait_ge(weighted, j - 1)
                pe.wait_ge(copied, 2 * j + 2)
                for e in range(8):
                    m = pe.matmul(ps[:, 2 + j % 2, e * 64:(e + 1) * 64], keysT[:, j % 2, e, :],
                                  bd[:, j // 4].rearrange("p a t h -> p (a t h)"), start=True, stop=True)
                m.then_inc(multiplied, 1)

            for j in range(N + 1):
                if j < N:
                    turn(j)
                if j:
                    multiply(j - 1)
            pe.wait_ge(new_summed, 1)
            pe.transpose(ps[0:NS, 7, 0:NS], news[:], k.ident[0:NS, 0:NS]).then_inc(new_turned, 1)
            pe.wait_ge(reduced, 1)
            for e in range(E16):
                if e % 4 == 0 and e >= 8:
                    pe.wait_ge(sc_copied, e // 4 - 1)
                m = pe.transpose(ps[:, 4 + (e // 4) % 2, (e % 4) * P:(e % 4 + 1) * P], sc[:, e].rearrange("p a q -> p (a q)"), k.ident[:])
                if e % 4 == 3:
                    m.then_inc(sc_turned, 1)

        @block.scalar
        def _(act):
            for j in range(N):
                for a in range(2):
                    act.wait_ge(turned, 2 * j + a + 1)
                    if j >= 2 and a == 0:
                        act.wait_ge(multiplied, j - 1)
                    act.copy(keysT[:, j % 2, 4 * a:4 * a + 4, :], ps[:, a, :].rearrange("p (e n) -> p e n", n=P)).then_inc(copied, 1)

        @block.vector
        def _(dve):
            dve.wait_ge(pt_landed, 128)
            dve.tensor_scalar(index[:], pages[:], 8.0, k.part[:, 0:1], ALU.mult, ALU.add).then_inc(indexed, 1)
            dve.memset(bd[:], 0.0)
            dve.memset(k.found[:, QUARTER:QUARTER + TD], UNSEEN)
            dve.drain()
            dve.memset(newp[0:1, 0:1], 0.0).then_inc(zeroed, 1)
            dve.wait_ge(iq_turned, 1)
            for a in range(2):
                rows = slice(a * DH, (a + 1) * DH)
                src = ps[rows, 7, 0:H * NS].rearrange("p (h b t) -> p h b t", h=H, b=BD)
                for t in range(TD):
                    x = dve.tensor_copy(bd[rows, :, a, t, :], src[:, :, :, t].rearrange("p h b -> p b h"))
            dve.drain()
            dve.memset(newp[0:1, 0:1], 0.0).then_inc(blocks_made, 1)
            dve.wait_ge(new_scored, 1)
            dve.wait_ge(small_landed, 64)
            dve.drain()
            dve.scalar_tensor_tensor(newp[:], ps[0:NS, 6, 0:NS * H], 0.0, wb[0:NS].rearrange("p q h -> p (q h)"), ALU.max, ALU.mult)
            dve.drain()
            dve.tensor_reduce(news[:], newp[:].rearrange("p (q h) -> p q h", h=H), AX.X, ALU.add).then_inc(new_summed, 1)
            for j in range(N):
                b, a = j // 4, j % 4
                dve.wait_ge(multiplied, j + 1)
                w = wb[:, b * TD:(b + 1) * TD, :].rearrange("p t h -> p (t h)")
                dve.scalar_tensor_tensor(part[:, j % 2].rearrange("p (e n) -> p e n", n=TD * H),
                                         ps[:, 2 + j % 2, :].rearrange("p (e n) -> p e n", n=TD * H), 0.0,
                                         w[:, None, :].broadcast_to([P, E16, TD * H]), ALU.max, ALU.mult).then_inc(weighted, 1)
                dve.drain()
                dve.tensor_reduce(sc[:, :, a, b * TD:(b + 1) * TD], part[:, j % 2].rearrange("p (e t h) -> p e t h", e=E16, h=H),
                                  AX.X, ALU.add)
            dve.drain()
            dve.memset(newp[0:1, 0:1], 0.0).then_inc(reduced, 1)
            dve.wait_ge(new_turned, 1)
            dve.tensor_tensor(newt[:], ps[0:NS, 7, 0:NS], newb[:], ALU.add)
            dve.drain()
            dve.tensor_reduce(newq[:], newt[:].rearrange("p (b s) -> p s b", b=BD), AX.X, ALU.max).then_inc(new_ready, 1)
            for g in range(4):
                dve.wait_ge(sc_turned, g + 1)
                dst = k.found[:, 0:QUARTER].rearrange("p (n e) -> p e n", e=E16)
                dve.tensor_copy(dst[:, 4 * g:4 * g + 4, :], ps[:, 4 + g % 2, :].rearrange("p (e n) -> p e n", n=P)).then_inc(sc_copied, 1)


def select_sample(k):
    nc, io, ps = k.nc, k.io, k.ps
    F = k.found
    FIRST_NEW = k.n_pool * PAGE
    with ExitStack() as ctx:
        best = k.sb(ctx, "best", [P, TOPK])
        where = k.sb(ctx, "where", [P, TOPK], U32)
        tabi = k.sb(ctx, "table_i", [P, 16], I32)
        tab = k.sb(ctx, "table", [P, 16])
        pagef = k.sb(ctx, "page_f", [P, TOPK])
        blk = k.sb(ctx, "block_u", [P, TOPK], U32)
        offu = k.sb(ctx, "offset_u", [P, TOPK], U32)
        hit = k.sb(ctx, "hit", [P, TOPK])
        row = k.sb(ctx, "row", [P, 2, 2 * TOPK])
        iota = k.sb(ctx, "iota", [P, TOPK])
        cand = k.sb(ctx, "cand", [NS, 4, TOPK])
        cbest = k.sb(ctx, "cand_best", [NS, 8])
        ceq = k.sb(ctx, "cand_taken", [NS, 4, TOPK])
        span = k.sb(ctx, "span", [NS, 4, 2])
        cnt = k.sb(ctx, "cnt", [NS, 4])
        sp4 = k.sb(ctx, "span_of_part", [P, 2])
        bitsu = k.sb(ctx, "bits_u", [P, 10], I32)
        bits = k.sb(ctx, "bits", [P, 10])
        fold = k.sb(ctx, "fold", [P, NS])
        newc = k.sb(ctx, "new_count", [P, TD])
        newq = k.sb(ctx, "new_by_query", [NS, TD])
        newm = k.sb(ctx, "new_matrix", [NS, BD, TD])
        same = k.sb(ctx, "same_entry", [NS, NS])
        slots = k.sb(ctx, "slots", [P, 2, NS])
        landed, cand_landed, span_landed = k.sems(ctx, "landed", "cand_landed", "span_landed")
        found, counted, placed, folded, new_made, new_turned = k.sems(
            ctx, "found", "counted", "placed", "folded", "new_made", "new_turned")
        block = ctx.enter_context(nc.Block())

        @block.sync
        def _(sp):
            pt = io["page_table"].rearrange("b (a i) -> a b i", a=4)
            for a in range(4):
                sp.dma_start(tabi[a * NS:(a + 1) * NS, :],
                             pt[a][:, None, :].broadcast_to([BD, TD, 16])).then_inc(landed, 16)
            sp.dma_start(iota[:], io["c_iota"].broadcast_to([P, TOPK])).then_inc(landed, 16)
            sp.dma_start(fold[:], io["c_fold"]).then_inc(landed, 16)
            sp.dma_start(same[:], io["c_same"]).then_inc(landed, 16)
            sp.wait_ge(found, 1)
            for a in range(4):
                sp.dma_start(cand[:, a, :], best[a * NS:(a + 1) * NS, :]).then_inc(cand_landed, 16)
            sp.wait_ge(counted, 1)
            for a in range(4):
                sp.dma_start(sp4[a * NS:(a + 1) * NS, :], span[:, a, :]).then_inc(span_landed, 16)

        @block.vector
        def _(dve):
            for i in range(ROUNDS):
                b8 = best[:, 8 * i:8 * i + 8]
                dve.max(b8, F[:])
                dve.drain()
                dve.max_index(where[:, 8 * i:8 * i + 8], b8, F[:])
                dve.drain()
                dve.match_replace(F[:], b8, F[:], TAKEN)
                dve.drain()
            dve.tensor_copy(tab[0:1, 0:1], best[0:1, 0:1]).then_inc(found, 1)
            dve.wait_ge(landed, 112)
            dve.drain()
            dve.tensor_copy(tab[:], tabi[:])
            dve.tensor_scalar(blk[:], where[:], 7, None, ALU.logical_shift_right)
            dve.tensor_scalar(offu[:], where[:], PAGE - 1, None, ALU.bitwise_and)
            dve.memset(row[:], 0.0)
            dve.drain()
            dve.tensor_copy(pagef[:], blk[:])
            dve.drain()
            data = row[:, 0, TOPK:2 * TOPK]
            dve.tensor_scalar(data, pagef[:], 16.0, float(k.n_pool), ALU.is_equal, ALU.mult)
            dve.drain()
            for i in range(16):
                dve.tensor_scalar(hit[:], pagef[:], float(i), tab[:, i:i + 1], ALU.is_equal, ALU.mult)
                dve.drain()
                dve.tensor_tensor(data, data, hit[:], ALU.add)
                dve.drain()
            dve.scalar_tensor_tensor(data, data, float(PAGE), offu[:], ALU.mult, ALU.add)
            dve.wait_ge(cand_landed, 64)
            c = cand[:].rearrange("p a n -> p (a n)")
            with dve.Fori(0, ROUNDS):
                dve.max(cbest[:], c)
                dve.drain()
                dve.match_replace(c, cbest[:], c, TAKEN)
                dve.drain()
            dve.tensor_scalar(ceq[:], cand[:], TAKEN, None, ALU.is_equal)
            dve.drain()
            dve.tensor_reduce(cnt[:], ceq[:], AX.X, ALU.add)
            dve.memset(span[:, 0, 0:1], 0.0)
            dve.drain()
            for a in range(4):
                dve.tensor_tensor(span[:, a, 1:2], span[:, a, 0:1], cnt[:, a:a + 1], ALU.add)
                dve.drain()
                if a < 3:
                    dve.tensor_copy(span[:, a + 1, 0:1], span[:, a, 1:2])
                    dve.drain()
            dve.tensor_copy(cbest[:, 0:1], cnt[:, 0:1]).then_inc(counted, 1)
            dve.wait_ge(span_landed, 64)
            dve.tensor_copy(bitsu[:, 9:10], sp4[:, 0:1])
            dve.drain()
            for i in range(9):
                dve.tensor_scalar(bitsu[:, i:i + 1], bitsu[:, 9:10], i, 1, ALU.arith_shift_right, ALU.bitwise_and)
            dve.drain()
            dve.tensor_copy(bits[:, 0:9], bitsu[:, 0:9])
            dve.drain()
            for i in range(9):
                x, y = row[:, i % 2], row[:, (i + 1) % 2]
                dve.tensor_tensor(hit[:], x[:, TOPK - (1 << i):2 * TOPK - (1 << i)], x[:, TOPK:2 * TOPK], ALU.subtract)
                dve.drain()
                dve.scalar_tensor_tensor(y[:, TOPK:2 * TOPK], hit[:], bits[:, i:i + 1], x[:, TOPK:2 * TOPK], ALU.mult, ALU.add)
                dve.drain()
            y = row[:, 1, TOPK:2 * TOPK]
            dve.scalar_tensor_tensor(hit[:], iota[:], sp4[:, 0:1], y, ALU.is_ge, ALU.mult)
            dve.drain()
            dve.scalar_tensor_tensor(y, iota[:], sp4[:, 1:2], hit[:], ALU.is_lt, ALU.mult)
            dve.drain()
            for s in range(TD):
                dve.tensor_scalar(hit[:], y, float(FIRST_NEW + s), None, ALU.is_equal)
                dve.drain()
                dve.tensor_reduce(newc[:, s:s + 1], hit[:], AX.X, ALU.add)
                dve.drain()
            dve.tensor_copy(bits[0:1, 9:10], bits[0:1, 8:9]).then_inc(placed, 1)
            dve.wait_ge(folded, 1)
            dve.tensor_copy(slots[:], ps[:, 0, 0:2 * NS].rearrange("p (a q) -> p a q", a=2))
            dve.tensor_copy(newq[:], ps[0:NS, 1, 0:TD])
            dve.drain()
            dve.tensor_scalar(k.slot_bias[:], slots[:], float(FIRST_NEW), MASKED, ALU.is_ge, ALU.mult)
            dve.tensor_scalar(k.slot_row[:], slots[:], float(FIRST_NEW - 1), None, ALU.min)
            dve.tensor_tensor(newm[:], newq[:][:, None, :].broadcast_to([NS, BD, TD]), same[:].rearrange("p (b s) -> p b s", b=BD),
                              ALU.mult).then_inc(new_made, 1)
            dve.wait_ge(new_turned, 1)
            dve.tensor_scalar(k.new_bias[:], ps[0:NS, 1, 0:NS], -1.0, -MASKED, ALU.add, ALU.mult)

        @block.tensor
        def _(pe):
            pe.wait_ge(placed, 1)
            pe.wait_ge(landed, 112)
            for a in range(2):
                pe.matmul(ps[:, 0, a * NS:(a + 1) * NS], row[:, 1, TOPK + a * P:TOPK + (a + 1) * P], fold[:], start=True, stop=True)
            pe.matmul(ps[0:NS, 1, 0:TD], fold[:], newc[:], start=True, stop=True).then_inc(folded, 1)
            pe.wait_ge(new_made, 1)
            pe.transpose(ps[0:NS, 1, 0:NS], newm[:].rearrange("p b s -> p (b s)"), k.ident[0:NS, 0:NS]).then_inc(new_turned, 1)



def attend_sample(k):
    nc, io, ps, mixT = k.nc, k.io, k.ps, k.hT
    RING = 6
    scale = DH ** -0.5
    pairs = [(q, a) for q in range(NS) for a in range(2)]
    HALF = NS // 2
    SLOTS = TOPK + NS
    with ExitStack() as ctx:
        got = k.sb(ctx, "gathered", [P, RING, H * DH])
        qb = k.sb(ctx, "q_everywhere", [P, 2, H * DH])
        prod = k.sb(ctx, "prod", [P, 2, H * DH])
        lg = k.sb(ctx, "slot_logits", [P, 2, NS, H])
        lgn = k.sb(ctx, "new_logits", [NS, NS, H])
        prob = k.sb(ctx, "prob_rows", [P, 2, SLOTS])
        pr = k.sb(ctx, "slot_probs", [P, 2, NS, H])
        prn = k.sb(ctx, "new_probs", [NS, NS, H])
        vnew = k.sb(ctx, "v_new", [NS, H * DH])
        top = k.sb(ctx, "top", [P, 2, 2])
        total = k.sb(ctx, "total", [P, 2, 2])
        g_landed = k.sem_ring(ctx, "g_landed", RING)
        q_landed = k.sem_ring(ctx, "q_landed", 2)
        (v_landed,) = k.sems(ctx, "v_landed")
        (scored_new, multiplied, summed, biased, turned, topped, exped, scaled, returned, probs_copied, weighed) = k.sems(
            ctx, "scored_new", "multiplied", "summed", "biased", "turned", "topped", "exped", "scaled", "returned",
            "probs_copied", "weighed")
        block = ctx.enter_context(nc.Block())

        @block.sync
        def _(sp):
            for q in range(NS):
                if q >= 2:
                    sp.wait_ge(multiplied, 2 * (q - 1))
                sp.dma_start(qb[:, q % 2, :], k.scratch["q_s"][q:q + 1, :].broadcast_to([P, H * DH])).then_inc(q_landed[q % 2], 16)
            sp.dma_start(vnew[:], io["v_sample"]).then_inc(v_landed, 16)

        @block.gpsimd
        def _(pool):
            for n, (name, used) in enumerate((("cache_k", multiplied), ("cache_v", weighed))):
                view = io[name][0].rearrange("g r h d -> (g r) (h d)")
                for j, (q, a) in enumerate(pairs):
                    i = n * len(pairs) + j
                    if i >= RING:
                        before = i - RING
                        if before < len(pairs):
                            pool.wait_ge(multiplied, before + 1)
                        else:
                            pool.wait_ge(weighed, (before - len(pairs)) // 2 + 1)
                    pool.indirect_dma_start(got[:, i % RING, :], None, view,
                                            bass.IndirectOffsetOnAxis(ap=k.slot_row[:, a, q:q + 1], axis=0)
                                            ).then_inc(g_landed[i % RING], 16)

        @block.vector
        def _(dve):
            dve.wait_ge(scored_new, 1)
            for a in range(2):
                dve.tensor_tensor(lgn[:, :, a:H:2], ps[0:NS, 6 + a, 0:NS * H // 2].rearrange("p (f q) -> p q f", q=NS),
                                  k.new_bias[:][:, :, None].broadcast_to([NS, NS, H // 2]), ALU.add)
            for j, (q, a) in enumerate(pairs):
                dve.wait_ge(g_landed[j % RING], 16 * (j // RING + 1))
                dve.wait_ge(q_landed[q % 2], 16 * (q // 2 + 1))
                dve.tensor_tensor(prod[:, a, :], got[:, j % RING, :], qb[:, q % 2, :], ALU.mult).then_inc(multiplied, 1)
                dve.drain()
                dve.tensor_reduce(lg[:, a, q, :], prod[:, a, :].rearrange("p (h d) -> p h d", h=H), AX.X, ALU.add)
            dve.drain()
            dve.tensor_tensor(lg[:], lg[:], k.slot_bias[:][:, :, :, None].broadcast_to([P, 2, NS, H]), ALU.add).then_inc(biased, 1)
            for g in range(2):
                dve.wait_ge(turned, g + 1)
                dve.tensor_reduce(top[:, g, 0:1], ps[:, g, 0:SLOTS], AX.X, ALU.max)
                dve.drain()
                dve.tensor_scalar(top[:, g, 1:2], top[:, g, 0:1], -scale, None, ALU.mult).then_inc(topped, 1)
            for g in range(2):
                dve.wait_ge(exped, g + 1)
                dve.reciprocal(total[:, g, 1:2], total[:, g, 0:1])
                dve.drain()
                dve.tensor_scalar(prob[:, g, :], prob[:, g, :], total[:, g, 1:2], None, ALU.mult).then_inc(scaled, 1)
            for g in range(2):
                dve.wait_ge(returned, g + 1)
                qs = slice(g * HALF, (g + 1) * HALF)
                dve.tensor_copy(pr[:, :, qs, :], ps[:, 2 + g, 0:TOPK].rearrange("p (a q h) -> p a q h", a=2, h=H))
                dve.tensor_copy(prn[:, qs, :], ps[0:NS, 2 + g, TOPK:TOPK + P].rearrange("p (q h) -> p q h", h=H)).then_inc(probs_copied, 1)
            dve.wait_ge(weighed, NS)
            out = ps[:, 4:6, :].rearrange("p b (q f h) -> p (b q) f h", f=4, h=H)
            for a in range(2):
                rows = slice(a * DH, (a + 1) * DH)
                for f in range(4):
                    dve.tensor_copy(mixT[rows, f, SEQ:R], out[rows, :, f, 2 * f + a])

        @block.scalar
        def _(act):
            for g in range(2):
                act.wait_ge(topped, g + 1)
                act.activation(prob[:, g, :], ps[:, g, 0:SLOTS], ACT.Exp, bias=top[:, g, 1:2], scale=scale,
                               accum_out=total[:, g, 0:1])
                act.drain()
                act.copy(top[0:1, g, 0:1], top[0:1, g, 1:2]).then_inc(exped, 1)

        @block.tensor
        def _(pe):
            for h in range(H):
                row = (h % 2) * DH
                m = pe.matmul(ps[0:NS, 6 + h % 2, (h // 2) * NS:(h // 2 + 1) * NS], k.kT[row:row + DH, h // 2, SEQ:R],
                              k.qT[row:row + DH, h // 2, SEQ:R], start=True, stop=True)
            m.then_inc(scored_new, 1)
            pe.wait_ge(biased, 1)
            for g in range(2):
                qs = slice(g * HALF, (g + 1) * HALF)
                for a in range(2):
                    pe.transpose(ps[:, g, a * P:(a + 1) * P], lg[:, a, qs, :].rearrange("p q h -> p (q h)"), k.ident[:])
                pe.transpose(ps[:, g, TOPK:SLOTS], lgn[:, qs, :].rearrange("p q h -> p (q h)"), k.ident[0:NS, 0:NS]).then_inc(turned, 1)
            for g in range(2):
                pe.wait_ge(scaled, g + 1)
                for a in range(2):
                    pe.transpose(ps[:, 2 + g, a * P:(a + 1) * P], prob[:, g, a * P:(a + 1) * P], k.ident[:])
                pe.transpose(ps[0:NS, 2 + g, TOPK:TOPK + P], prob[:, g, TOPK:SLOTS], k.ident[:]).then_inc(returned, 1)
            pe.wait_ge(probs_copied, 2)
            pe.wait_ge(v_landed, 16)
            for q in range(NS):
                i = len(pairs) + 2 * q
                for x in (i, i + 1):
                    pe.wait_ge(g_landed[x % RING], 16 * (x // RING + 1))
                for f in range(4):
                    at = (q % HALF) * 4 * H + f * H
                    o = ps[:, 4 + q // HALF, at:at + H]
                    fs = slice(f * P, (f + 1) * P)
                    for a in range(2):
                        pe.matmul(o, got[:, (i + a) % RING, fs], pr[:, a, q, :], start=a == 0, stop=False)
                    m = pe.matmul(o, vnew[:, fs], prn[:, q, :], start=False, stop=True)
                m.then_inc(weighed, 1)



def project_out(k):
    nc, ps = k.nc, k.ps
    w_out = k.io["w_out"][0].rearrange("(k p) n -> p k n", p=P)
    with ExitStack() as ctx:
        w = k.sb(ctx, "w_out_tile", [P, 2, KD, P])
        landed = k.sem_ring(ctx, "landed", 2)
        multiplied, banks_free = k.sems(ctx, "multiplied", "banks_free")
        block = ctx.enter_context(nc.Block())

        @block.sync
        def _(sp):
            for s in range(2):
                sp.dma_start(w[:, s], w_out[:, :, s * P:(s + 1) * P]).then_inc(landed[s], 16)
            with sp.Fori(0, KD // 2 - 1) as t:
                for s in range(2):
                    sp.wait_ge(multiplied, 2 * t + s + 1)
                    sp.dma_start(w[:, s], w_out[:, :, bass.ds((2 * t + 2 + s) * P, P)]).then_inc(landed[s], 16)

        @block.tensor
        def _(pe):
            with pe.Fori(0, KD // 2) as t:
                for s in range(2):
                    pe.wait_ge(landed[s], 16 * t + 16)
                    pe.wait_ge(banks_free, 2 * t + s + 1)
                    for d in range(KD):
                        for g in range(G):
                            m = pe.matmul(ps[:, 4 * s + g, 0:GC], w[:, s, d, :], k.hT[:, d, g * GC:(g + 1) * GC],
                                          start=d == 0, stop=d == KD - 1)
                    m.then_inc(multiplied, 1)

        @block.vector
        def _(dve):
            dve.sem_inc(banks_free, 2)
            with dve.Fori(0, KD // 2) as t:
                for s in range(2):
                    dve.wait_ge(multiplied, 2 * t + s + 1)
                    x = grouped(k.xT[:, 2 * t + s, :])
                    dve.tensor_tensor(x, x, bank_cols(ps, 4 * s), ALU.add).then_inc(banks_free, 1)


def ffn(k, layer):
    nc, ps = k.nc, k.ps
    w_up = k.io["w_up"][layer].rearrange("(k p) n -> p k n", p=P)
    w_down = k.io["w_down"][layer].rearrange("(k p) n -> p k n", p=P)
    with ExitStack() as ctx:
        hidden = k.sb(ctx, "hidden", [P, KF, R])
        wu = k.sb(ctx, "w_up_tile", [P, 2, 2, KD, P])
        wd = k.sb(ctx, "w_down_tile", [P, 2, KF, P])
        act_gate = k.sb(ctx, "act_gate", [P, R])
        up_landed, down_landed = k.sem_ring(ctx, "up_landed", 2), k.sem_ring(ctx, "down_landed", 2)
        gate_done, up_done, silu_done, hidden_done, down_done, banks_free = k.sems(
            ctx, "gate_done", "up_done", "silu_done", "hidden_done", "down_done", "banks_free")
        norm_ctx = ctx.enter_context(ExitStack())
        norm = Norm(k, norm_ctx, k.hT, k.ffn_w[layer], square=hidden[:, 0:2, :], total=hidden[:, 2, :])
        block = ctx.enter_context(nc.Block())

        @block.sync
        def _(sp):
            def load_up(s, n):
                for half in range(2):
                    sp.dma_start(wu[:, s, half], w_up[:, :, bass.ds(n * P + half * FF, P)]).then_inc(up_landed[s], 16)

            for s in range(2):
                load_up(s, s)
            for s in range(2):
                sp.dma_start(wd[:, s], w_down[:, :, s * P:(s + 1) * P]).then_inc(down_landed[s], 16)
            with sp.Fori(0, KF // 2 - 1) as t:
                for s in range(2):
                    sp.wait_ge(up_done, 2 * t + s + 1)
                    load_up(s, 2 * t + 2 + s)
            with sp.Fori(0, KD // 2 - 1) as t:
                for s in range(2):
                    sp.wait_ge(down_done, 2 * t + s + 1)
                    sp.dma_start(wd[:, s], w_down[:, :, bass.ds((2 * t + 2 + s) * P, P)]).then_inc(down_landed[s], 16)

        @block.tensor
        def _(pe):
            norm.tensor(pe)
            pe.wait_ge(norm.normed, KD)
            with pe.Fori(0, KF // 2) as t:
                for s in range(2):
                    pe.wait_ge(up_landed[s], 32 * t + 32)
                    for half, free, done in ((0, silu_done, gate_done), (1, hidden_done, up_done)):
                        pe.wait_ge(free, 2 * t + s)
                        for d in range(KD):
                            for g in range(G):
                                m = pe.matmul(ps[:, 4 * half + g, 0:GC], wu[:, s, half, d, :], k.hT[:, d, g * GC:(g + 1) * GC],
                                              start=d == 0, stop=d == KD - 1)
                        m.then_inc(done, 1)
            pe.wait_ge(hidden_done, KF)
            with pe.Fori(0, KD // 2) as t:
                for s in range(2):
                    pe.wait_ge(down_landed[s], 16 * t + 16)
                    pe.wait_ge(banks_free, 2 * t + s + 1)
                    for f in range(KF):
                        for g in range(G):
                            m = pe.matmul(ps[:, 4 * s + g, 0:GC], wd[:, s, f, :], hidden[:, f, g * GC:(g + 1) * GC],
                                          start=f == 0, stop=f == KF - 1)
                    m.then_inc(down_done, 1)

        @block.scalar
        def _(act):
            norm.scalar(act)
            with act.Fori(0, KF) as n:
                act.wait_ge(gate_done, n + 1)
                act.wait_ge(hidden_done, n)
                act.activation(grouped(act_gate[:]), bank_cols(ps, 0), ACT.Silu).then_inc(silu_done, 1)

        @block.vector
        def _(dve):
            norm.vector(dve)
            dve.drain()
            with dve.Fori(0, KF) as n:
                dve.wait_ge(silu_done, n + 1)
                dve.wait_ge(up_done, n + 1)
                dve.tensor_tensor(grouped(hidden[:, n, :]), grouped(act_gate[:]), bank_cols(ps, 4), ALU.mult).then_inc(hidden_done, 1)
            dve.sem_inc(banks_free, 2)
            with dve.Fori(0, KD // 2) as t:
                for s in range(2):
                    dve.wait_ge(down_done, 2 * t + s + 1)
                    x = grouped(k.xT[:, 2 * t + s, :])
                    dve.tensor_tensor(x, x, bank_cols(ps, 4 * s), ALU.add).then_inc(banks_free, 1)


def layer_embedding(k, layer):
    nc, io, ps = k.nc, k.io, k.ps
    wg = io["w_ple_gate"][layer].rearrange("(k p) n -> p k n", p=P)
    wp = io["w_ple"][layer].rearrange("(k p) n -> p k n", p=P)
    KP = PLE // P
    with ExitStack() as ctx:
        rows = k.sb(ctx, "p_rows", [P, NT + 1, PLE])
        pT = k.sb(ctx, "pT", [P, KP, R])
        w = k.sb(ctx, "w_ple_tile", [P, 2, KD + KP, P])
        gate = k.sb(ctx, "gate", [P, R])
        term = k.sb(ctx, "term", [P, R])
        landed = k.sem_ring(ctx, "w_landed", 2)
        (p_landed,) = k.sems(ctx, "p_landed")
        turned, copied, gate_done, ple_done, gated, added = k.sems(
            ctx, "turned", "copied", "gate_done", "ple_done", "gated", "added")
        norm = Norm(k, ctx, k.hT, k.ple_w[layer])
        block = ctx.enter_context(nc.Block())

        @block.sync
        def _(sp):
            sp.dma_start(rows[:, 0:NT, :], io["p_prompt"][layer, 0].rearrange("(r p) n -> p r n", p=P)).then_inc(p_landed, 16)
            sp.dma_start(rows[0:NS, NT, :], io["p_sample"][layer].rearrange("b t n -> (b t) n")).then_inc(p_landed, 16)

            def load(s, n):
                sp.dma_start(w[:, s, 0:KD, :], wg[:, :, bass.ds(n * P, P)]).then_inc(landed[s], 16)
                sp.dma_start(w[:, s, KD:KD + KP, :], wp[:, :, bass.ds(n * P, P)]).then_inc(landed[s], 16)

            for s in range(2):
                load(s, s)
            with sp.Fori(0, KD // 2 - 1) as t:
                for s in range(2):
                    sp.wait_ge(ple_done, 2 * t + s + 1)
                    load(s, 2 * t + 2 + s)

        @block.tensor
        def _(pe):
            pe.wait_ge(p_landed, 32)
            for r in range(NT + 1):
                n = rows_of(r)
                if r >= 2:
                    pe.wait_ge(copied, r - 1)
                for i in range(KP):
                    m = pe.transpose(ps[:, 6 + r % 2, i * P:i * P + n], rows[0:n, r, i * P:(i + 1) * P], k.ident[0:n, 0:n])
                m.then_inc(turned, 1)
            norm.tensor(pe)
            pe.wait_ge(copied, NT + 1)
            pe.wait_ge(norm.normed, KD)
            with pe.Fori(0, KD // 2) as t:
                for s in range(2):
                    pe.wait_ge(landed[s], 32 * t + 32)
                    pe.wait_ge(gated, 2 * t + s)
                    for d in range(KD):
                        for g in range(G):
                            m = pe.matmul(ps[:, g, 0:GC], w[:, s, d, :], k.hT[:, d, g * GC:(g + 1) * GC],
                                          start=d == 0, stop=d == KD - 1)
                    m.then_inc(gate_done, 1)
                    pe.wait_ge(added, 2 * t + s)
                    for i in range(KP):
                        for g in range(G):
                            m = pe.matmul(ps[:, 4 + g, 0:GC], w[:, s, KD + i, :], pT[:, i, g * GC:(g + 1) * GC],
                                          start=i == 0, stop=i == KP - 1)
                    m.then_inc(ple_done, 1)

        @block.scalar
        def _(act):
            for r in range(NT + 1):
                n = rows_of(r)
                act.wait_ge(turned, r + 1)
                act.copy(pT[:, :, r * P:r * P + n], ps[:, 6 + r % 2, 0:PLE].rearrange("p (i n) -> p i n", n=P)[:, :, 0:n]).then_inc(copied, 1)
            norm.scalar(act)
            with act.Fori(0, KD) as n:
                act.wait_ge(gate_done, n + 1)
                act.wait_ge(added, n)
                act.activation(grouped(gate[:]), bank_cols(ps, 0), ACT.Sigmoid).then_inc(gated, 1)

        @block.vector
        def _(dve):
            norm.vector(dve)
            dve.drain()
            with dve.Fori(0, KD) as n:
                dve.wait_ge(gated, n + 1)
                dve.wait_ge(ple_done, n + 1)
                dve.tensor_tensor(grouped(term[:]), grouped(gate[:]), bank_cols(ps, 4), ALU.mult)
                dve.drain()
                x = k.xT[:, n, :]
                dve.tensor_tensor(x, x, term[:], ALU.add).then_inc(added, 1)
                dve.drain()



def pool_mix(k):
    nc, io, ps, hT = k.nc, k.io, k.ps, k.hT
    SEG = POOL_BUF + TD
    HEAD = POOL_BUF + SEQ
    LEN = HEAD + BD * SEG
    BUF = BD * POOL_BUF
    OUT = POOL_BUF + NS
    with ExitStack() as ctx:
        z = k.sb(ctx, "z", [P, KD, R])
        ext = k.sb(ctx, "ext", [P, 2, LEN])
        sums = k.sb(ctx, "sums", [P, 2, LEN])
        inv = k.sb(ctx, "inv_count", [P, len(WINDOWS), 16])
        w = k.sb(ctx, "pool_w", [P, len(WINDOWS), 2, 2 * P])
        buf = k.sb(ctx, "buf_rows", [BUF, D])
        bufT = k.sb(ctx, "bufT", [P, KD, BUF])
        last = k.sb(ctx, "last_rows", [OUT, D])
        fix = k.sb(ctx, "first_means", [P, 16])
        w_landed, buf_landed, out_stored = k.sems(ctx, "w_landed", "buf_landed", "out_stored")
        turned, copied, last_turned, last_copied, z_made, multiplied, added = k.sems(
            ctx, "turned", "copied", "last_turned", "last_copied", "z_made", "multiplied", "added")
        norm = Norm(k, ctx, hT, k.mix_w[1], square=z[:, 0:2, :], total=z[:, 2, :])
        block = ctx.enter_context(nc.Block())

        @block.sync
        def _(sp):
            sp.dma_start(buf[:], io["state_pool"][0].rearrange("b r n -> (b r) n")).then_inc(buf_landed, 16)
            sp.dma_start(w[:], io["pool_w"][0].rearrange("g (k p) n -> p g k n", p=P)).then_inc(w_landed, 16)
            sp.dma_start(inv[:].rearrange("p w n -> p (w n)"), io["c_invcnt"].broadcast_to([P, 16 * len(WINDOWS)])).then_inc(w_landed, 16)
            sp.dma_start(io["pool_sample"][0][:, 0:POOL_BUF - TD, :], io["state_pool"][0][:, TD:POOL_BUF, :]).then_inc(out_stored, 16)
            sp.wait_ge(last_copied, 1)
            sp.dma_start(io["pool_prompt"][0, 0], last[0:POOL_BUF, :]).then_inc(out_stored, 16)
            for b in range(BD):
                at = POOL_BUF + b * TD
                sp.dma_start(io["pool_sample"][0, b, POOL_BUF - TD:POOL_BUF, :], last[at:at + TD, :]).then_inc(out_stored, 16)
            sp.wait_ge(out_stored, 16 * (BD + 2))

        @block.tensor
        def _(pe):
            pe.wait_ge(buf_landed, 16)
            for d in range(KD):
                m = pe.transpose(ps[:, 4 + d // 4, (d % 4) * P:(d % 4) * P + BUF], buf[:, d * P:(d + 1) * P], k.ident[0:BUF, 0:BUF])
            m.then_inc(turned, 1)
            norm.tensor(pe)
            pe.wait_ge(norm.normed, KD)
            for d in range(KD):
                m = pe.transpose(ps[0:OUT, 6 + d // 4, (d % 4) * P:(d % 4 + 1) * P], hT[:, d, R - OUT:R], k.ident[:])
            m.then_inc(last_turned, 1)
            pe.wait_ge(w_landed, 32)
            pe.wait_ge(copied, 1)
            for d in range(KD):
                b = 3 * (d % 2)
                pe.wait_ge(z_made, 2 * (d // 2 + 1))
                if d >= 2:
                    pe.wait_ge(added, d - 1)
                for i in range(2):
                    for g in range(G):
                        m = pe.matmul(ps[:, b + g, 0:GC], w[:, d // 2, i, (d % 2) * P:(d % 2 + 1) * P],
                                      z[:, 2 * (d // 2) + i, g * GC:(g + 1) * GC], start=i == 0, stop=i == 1)
                m.then_inc(multiplied, 1)

        @block.scalar
        def _(act):
            act.wait_ge(turned, 1)
            act.copy(bufT[:], ps[:, 4:6, :].rearrange("p b (d n) -> p (b d) n", n=P)[:, :, 0:BUF]).then_inc(copied, 1)
            norm.scalar(act)
            act.wait_ge(last_turned, 1)
            act.copy(last[:].rearrange("p (b n) -> p b n", b=2), ps[0:OUT, 6:8, :]).then_inc(last_copied, 1)

        @block.vector
        def _(dve):
            norm.vector(dve)
            dve.memset(ext[:, :, 0:POOL_BUF], 0.0)
            dve.memset(sums[:], 0.0)
            dve.wait_ge(copied, 1)
            dve.wait_ge(w_landed, 32)
            dve.drain()
            for d in range(KD):
                e = ext[:, d % 2, :]
                wi = d // 2
                seg = e[:, HEAD:LEN].rearrange("p (b r) -> p b r", r=SEG)
                dve.tensor_copy(e[:, POOL_BUF:HEAD], hT[:, d, 0:SEQ])
                dve.tensor_copy(seg[:, :, 0:POOL_BUF], bufT[:, d, :].rearrange("p (b r) -> p b r", r=POOL_BUF))
                dve.tensor_copy(seg[:, :, POOL_BUF:SEG], hT[:, d, SEQ:R].rearrange("p (b t) -> p b t", t=TD))
                dve.drain()
                src, reach = e, 1
                for n in range(wi + 1):
                    dst = sums[:, n % 2, :]
                    dve.tensor_tensor(dst[:, reach:LEN], src[:, reach:LEN], src[:, 0:LEN - reach], ALU.add)
                    dve.drain()
                    src, reach = dst, 2 * reach
                zp, zs = z[:, d, 0:SEQ], z[:, d, SEQ:R].rearrange("p (b t) -> p b t", t=TD)
                dve.scalar_tensor_tensor(zp, src[:, POOL_BUF:HEAD], 1.0 / reach, e[:, POOL_BUF:HEAD], ALU.mult, ALU.subtract)
                sseg = src[:, HEAD:LEN].rearrange("p (b r) -> p b r", r=SEG)
                dve.scalar_tensor_tensor(zs, sseg[:, :, POOL_BUF:SEG], 1.0 / reach, seg[:, :, POOL_BUF:SEG], ALU.mult, ALU.subtract)
                dve.tensor_tensor(fix[:], src[:, POOL_BUF:POOL_BUF + 16], inv[:, wi, :], ALU.mult)
                dve.drain()
                dve.tensor_tensor(zp[:, 0:16], fix[:], e[:, POOL_BUF:POOL_BUF + 16], ALU.subtract).then_inc(z_made, 1)
                dve.drain()
            for d in range(KD):
                dve.wait_ge(multiplied, d + 1)
                x = grouped(k.xT[:, d, :])
                dve.scalar_tensor_tensor(x, bank_cols(ps, 3 * (d % 2)), k.pool_s[:, d:d + 1], x, ALU.mult, ALU.add).then_inc(added, 1)



def finish(k):
    nc, io, ps, hT = k.nc, k.io, k.ps, k.hT
    with ExitStack() as ctx:
        rows = k.sb(ctx, "y_rows", [P, 3, D])
        stored = k.sem_ring(ctx, "y_stored", 3)
        turned, copied = k.sems(ctx, "turned", "copied")
        norm = Norm(k, ctx, hT, k.final_w)
        block = ctx.enter_context(nc.Block())

        @block.tensor
        def _(pe):
            norm.tensor(pe)
            pe.wait_ge(norm.normed, KD)
            for r in range(NT + 1):
                n, b = rows_of(r), 2 * (r % 2)
                if r >= 2:
                    pe.wait_ge(copied, r - 1)
                for d in range(KD):
                    m = pe.transpose(ps[0:n, b + d // 4, (d % 4) * P:(d % 4 + 1) * P], hT[:, d, r * P:r * P + n], k.ident[:])
                m.then_inc(turned, 1)

        @block.scalar
        def _(act):
            norm.scalar(act)
            for r in range(NT + 1):
                n, b = rows_of(r), 2 * (r % 2)
                act.wait_ge(turned, r + 1)
                if r >= 3:
                    act.wait_ge(stored[r % 3], 16 * (r // 3))
                act.copy(rows[0:n, r % 3, :].rearrange("p (b n) -> p b n", b=2), ps[0:n, b:b + 2, :]).then_inc(copied, 1)

        block.vector(norm.vector)

        @block.sync
        def _(sp):
            for r in range(NT + 1):
                n = rows_of(r)
                sp.wait_ge(copied, r + 1)
                dst = io["y_prompt"][0, r * P:(r + 1) * P, :] if r < NT else io["y_sample"].rearrange("b t d -> (b t) d")
                sp.dma_start(dst, rows[0:n, r % 3, :]).then_inc(stored[r % 3], 16)
            for s in range(3):
                sp.wait_ge(stored[s], 16 * ((NT + 1 - s + 2) // 3))



def build(nc, io):
    scratch = {}
    for name, shape in dict(q_s=(NS, 512), iq_s=(NS, 512), iw_s=(NS, H), bi=(R, 512), bg=(R, 512),
                            gq=(BH, P, R), gk=(BH, P, R), gb=(BH, P, R)).items():
        scratch[name] = nc.dram_tensor(f"scratch_{name}", shape, F32, kind="Internal").ap()
    k = Program(nc, io, scratch)
    k.n_pool = io["cache_kidx"].shape[1]
    io["k_prompt"] = io["k_prompt"].rearrange("l b t h d -> (l b t) (h d)")
    io["v_prompt"] = io["v_prompt"].rearrange("l b t h d -> (l b t) (h d)")
    io["kidx_prompt"] = io["kidx_prompt"].rearrange("l b t d -> (l b t) d")
    io["k_sample"] = io["k_sample"].rearrange("l b t h d -> (l b t) (h d)")
    io["v_sample"] = io["v_sample"].rearrange("l b t h d -> (l b t) (h d)")
    io["kidx_sample"] = io["kidx_sample"].rearrange("l b t d -> (l b t) d")
    with k.keep:
        load_constants(k)
        k.hT = k.sb(k.keep, "hT", [P, KD, R])
        load_x(k)
        with ExitStack() as mix:
            k.qT, k.kT, k.iqT = (k.sb(mix, n, [P, 4, R]) for n in ("qT", "kT", "iqT"))
            k.ikT = k.sb(mix, "ikT", [P, R])
            k.iw = k.sb(mix, "iw", [P, NT + 1, H])
            k.slot_row = k.sb(mix, "slot_row", [P, 2, NS], U32)
            k.slot_bias = k.sb(mix, "slot_bias", [P, 2, NS])
            k.new_bias = k.sb(mix, "new_bias_t", [NS, NS])
            with ExitStack() as proj:
                k.rope = k.sb(proj, "rope", [P, NT + 1, 2 * DH])
                k.part = k.sb(proj, "part_const", [P, 2])
                norm_into_features(k)
                project_rows(k, ["iq", "ik", "aq", "ak", "av", "bi", "bg"])
                project_gates(k)
                with ExitStack() as sample:
                    k.found = k.sb(sample, "found", [P, QUARTER + TD])
                    score_sample(k)
                    select_sample(k)
            with ExitStack() as prompt:
                k.masks = k.sb(prompt, "masks", [P, mask_offset(NT)])
                select_prompt(k)
                attend_prompt(k)
            attend_sample(k)
        recurrence(k)
        project_out(k)
        ffn(k, 0)
        layer_embedding(k, 0)
        pool_mix(k)
        ffn(k, 1)
        layer_embedding(k, 1)
        finish(k)


def norm_into_features(k):
    with ExitStack() as ctx:
        (landed,) = k.sems(ctx, "landed")
        norm = Norm(k, ctx, k.hT, k.mix_w[0])
        block = ctx.enter_context(k.nc.Block())

        @block.sync
        def _(sp):
            table = k.io["c_rope"].rearrange("t a d -> t (a d)")
            sp.dma_start(k.rope[:, 0:NT, :], table[0:SEQ].rearrange("(r p) n -> p r n", p=P)).then_inc(landed, 16)
            sp.dma_start(k.rope[0:NS, NT, :], table[SEQ:R]).then_inc(landed, 16)
            sp.dma_start(k.part[:], k.io["c_part"]).then_inc(landed, 16)
            sp.wait_ge(landed, 48)

        block.scalar(norm.scalar)
        block.tensor(norm.tensor)
        block.vector(norm.vector)



_OUTS = dict(
    y_prompt=(1, SEQ, D), y_sample=(BD, TD, D),
    k_prompt=(1, 1, SEQ, H, DH), v_prompt=(1, 1, SEQ, H, DH), kidx_prompt=(1, 1, SEQ, DH),
    glr_prompt=(1, 1, BH, BK, BK), pool_prompt=(1, 1, POOL_BUF, D),
    k_sample=(1, BD, TD, H, DH), v_sample=(1, BD, TD, H, DH), kidx_sample=(1, BD, TD, DH),
    glr_sample=(1, BD, BH, BK, BK), pool_sample=(1, BD, POOL_BUF, D),
)


def kernel(**inputs):
    import concourse.bacc as _bacc
    from concourse.bass_utils import run_bass_kernel_spmd as _run

    nc = _bacc.Bacc("TRN2", target_bir_lowering=False, num_devices=1)
    arrays, io = {}, {}
    for name, a in {**inputs, **constants()}.items():
        a = np.ascontiguousarray(a)
        arrays[f"in_{name}"] = a
        io[name] = nc.dram_tensor(f"in_{name}", a.shape, mybir.dt.from_np(a.dtype), kind="ExternalInput").ap()
    for name, shape in _OUTS.items():
        io[name] = nc.dram_tensor(f"out_{name}", shape, F32, kind="ExternalOutput").ap()
    build(nc, io)
    r = _run(nc, [arrays], core_ids=[0])
    return tuple(r.results[0][f"out_{name}"] for name in _OUTS)
```

```python
from contextlib import ExitStack
import math

import numpy as np

import concourse.bass as bass
from concourse import mybir

F32, F32R, I32, U32 = mybir.dt.float32, mybir.dt.float32r, mybir.dt.int32, mybir.dt.uint32
ALU, ACT, AX = mybir.AluOpType, mybir.ActivationFunctionType, mybir.AxisListType

P = 128
D = 1024
SEQ = 1024
BD, TD = 8, 4
NS = BD * TD
R = SEQ + NS
PAGE, NPAGES = 128, 64
PAST = PAGE * NPAGES
H, DH = 8, 64
TOPK = 256
BH, BK = 4, 128
FF = 2816
PLE = 256
POOL_BUF = 15
WINDOWS = (2, 4, 8, 16)
EPS = 1e-6

KD = D // P
KF = FF // P
NT = SEQ // P
G, GC = 3, R // 3
COL = dict(aq=0, ak=512, av=1024, iq=1536, ik=2048, bq=2120, bf=2632, bi=3144, bg=3656)
IK_COLS = DH + H
QUARTER = PAST // 4
ROUNDS = TOPK // 8
MASKED = -1e30
UNSEEN = -3.0e38
TAKEN = -3.39e38
LEVELS = int(math.log2(P))


def rows_of(r):
    return P if r < NT else NS


def constants():
    half = DH // 2
    inv = (10000.0 ** (-np.arange(half) / half)).astype(np.float32)
    pos = np.concatenate([np.arange(SEQ), np.tile(PAST + np.arange(TD), BD)]).astype(np.float32)
    ang = pos[:, None] * inv[None, :]
    c, s = np.cos(ang), np.sin(ang)
    rope = np.stack([np.concatenate([c, c], 1), np.concatenate([-s, s], 1)], 1).astype(np.float32)
    a, b = np.arange(P)[:, None], np.arange(P)[None, :]
    level = [((a // (2 * w)) == (b // (2 * w))) & (a % (2 * w) < w) & (b % (2 * w) >= w)
             for w in (1 << n for n in range(LEVELS))] + [a == b]
    t = np.arange(R)
    reset = np.where(t < SEQ, t % P != 0, (t - SEQ) % TD != 0)
    q, n = np.arange(NS)[:, None], np.arange(NS)[None, :]
    same = q // TD == n // TD
    w = np.array(WINDOWS)[:, None]
    return dict(
        c_ident=np.eye(P, dtype=np.float32),
        c_rope=rope,
        c_level=np.stack(level, 1).astype(np.int32),
        c_causal=np.where(b <= a, 0.0, MASKED).astype(np.float32),
        c_reset=reset[None].astype(np.float32),
        c_batchcol=(n[0][None, :] // TD == np.arange(BD)[:, None]).reshape(1, BD * NS).astype(np.float32),
        c_batchrow=(np.arange(NS)[:, None] // TD == np.arange(BD)[None, :]).astype(np.float32),
        c_fold=(a % NS == n).astype(np.float32),
        c_newbias=np.where(same & (n % TD <= q % TD), 0.0, UNSEEN).astype(np.float32),
        c_same=same.astype(np.float32),
        c_iota=np.arange(TOPK)[None].astype(np.float32),
        c_part=np.concatenate([a % 8, (a // NS) * QUARTER], 1).astype(np.float32),
        c_invcnt=(1.0 / np.minimum(np.arange(16)[None] + 1, w)).reshape(1, -1).astype(np.float32),
    )


class Program:

    def __init__(self, nc, io, scratch):
        self.nc, self.io, self.scratch = nc, io, scratch
        self.keep = ExitStack()
        self.used = {}
        self.in_use = []

    def numbered(self, name):
        self.used[name] = self.used.get(name, 0) + 1
        return name if self.used[name] == 1 else f"{name}_{self.used[name]}"

    def sb(self, ctx, name, shape, dt=F32):
        return ctx.enter_context(self.nc.sbuf_tensor(self.numbered(name), shape, dt))

    def sems(self, ctx, *names):
        sems = [self.nc.alloc_semaphore(self.numbered("s_" + n)) for n in names]
        self.in_use += sems
        ctx.callback(self.clear_sems)
        return sems

    def sem_ring(self, ctx, name, n):
        return self.sems(ctx, *(f"{name}{i}" for i in range(n)))

    def stage(self, *parts):
        with ExitStack() as ctx:
            with self.nc.Block() as block:
                later = [part(self, ctx, block, *args) for part, *args in parts]
                for part in later:
                    if part is not None:
                        part(self, ctx, block)

    def clear_sems(self):
        if self.in_use:
            self.nc.clear_and_free_semaphores(self.in_use)
            self.in_use = []
            self.nc.all_engine_barrier()


def bank_cols(ps, b, n=G):
    return ps[:, b:b + n, 0:GC]


def grouped(ap):
    return ap.rearrange("p (g n) -> p g n", g=G)



def load_constants(k, ctx, block):
    nc, io = k.nc, k.io
    rows = k.sb(ctx, "vec_rows", [9 * KD, P])
    landed, turned = k.sems(ctx, "landed", "turned")

    @block.sync
    def _(sp):
        sp.dma_start(k.ident[:], io["c_ident"]).then_inc(landed, 16)
        at = 0
        for name in ("mix_norm", "ffn_norm", "ple_norm", "final_norm", "pool_scale", "lb_logits"):
            a = io[name]
            n = a.size() // P if callable(a.size) else a.size // P
            flat = a.rearrange("(n p) -> n p", p=P) if len(a.shape) == 1 else a.rearrange("l (n p) -> (l n) p", p=P)
            sp.dma_start(rows[at:at + n, :], flat).then_inc(landed, 16)
            at += n
        sp.wait_ge(landed, 16 * 7)

    @block.vector
    def _(dve):
        dve.memset(k.ones[:], 1.0)
        dve.memset(k.eps[:], EPS)
        dve.wait_ge(turned, 1)
        dve.tensor_copy(k.vec[:], k.ps[:, 0, 0:9 * KD])

    @block.tensor
    def _(pe):
        pe.wait_ge(landed, 16 * 7)
        pe.transpose(k.ps[:, 0, 0:9 * KD], rows[:], k.ident[0:9 * KD, 0:9 * KD]).then_inc(turned, 1)

    k.mix_w = [k.vec[:, i * KD:(i + 1) * KD] for i in range(2)]
    k.ffn_w = [k.vec[:, (2 + i) * KD:(3 + i) * KD] for i in range(2)]
    k.ple_w = [k.vec[:, (4 + i) * KD:(5 + i) * KD] for i in range(2)]
    k.final_w = k.vec[:, 6 * KD:7 * KD]
    k.pool_s = k.vec[:, 7 * KD:8 * KD]
    k.lb_logit = [k.vec[:, 8 * KD + i * BH:8 * KD + (i + 1) * BH] for i in range(2)]



def load_x(k, ctx, block):
    nc, io, ps = k.nc, k.io, k.ps
    rows = k.sb(ctx, "x_rows", [P, 3, D])
    landed = k.sem_ring(ctx, "x_landed", 3)
    turned, copied = k.sems(ctx, "turned", "copied")

    @block.sync
    def _(sp):
        for r in range(NT + 1):
            n = rows_of(r)
            if r >= 3:
                sp.wait_ge(turned, r - 2)
            src = io["x_prompt"][0, r * P:(r + 1) * P, :] if r < NT else io["x_sample"].rearrange("b t d -> (b t) d")
            sp.dma_start(rows[0:n, r % 3, :], src).then_inc(landed[r % 3], 16)

    @block.tensor
    def _(pe):
        for r in range(NT + 1):
            n = rows_of(r)
            pe.wait_ge(landed[r % 3], 16 * (r // 3 + 1))
            if r >= 2:
                pe.wait_ge(copied, r - 1)
            for d in range(KD):
                at = (d % 4) * P
                m = pe.transpose(ps[:, 2 * (r % 2) + d // 4, at:at + n], rows[0:n, r % 3, d * P:(d + 1) * P],
                                 k.ident[0:n, 0:n])
            m.then_inc(turned, 1)

    @block.scalar
    def _(act):
        for r in range(NT + 1):
            n, b = rows_of(r), 2 * (r % 2)
            act.wait_ge(turned, r + 1)
            src = ps[:, b:b + 2, :].rearrange("p b (d n) -> p (b d) n", n=P)
            act.copy(k.xT[:, :, r * P:r * P + n], src[:, :, 0:n]).then_inc(copied, 1)


class Norm:

    def __init__(self, k, ctx, hT, weight, square=None, total=None):
        self.k, self.hT, self.weight = k, hT, weight
        self.square = k.sb(ctx, "norm_square", [P, 2, R]) if square is None else square
        self.total = k.sb(ctx, "norm_total", [P, R])[:] if total is None else total
        self.squared, self.summed, self.ssq, self.rooted, self.normed = k.sems(
            ctx, "norm_squared", "norm_summed", "norm_ssq", "norm_rooted", "normed")

    def scalar(self, act):
        k = self.k
        for d in range(KD):
            if d >= 2:
                act.wait_ge(self.summed, max(1, d - 2))
            act.activation(self.square[:, d % 2, :], k.xT[:, d, :], ACT.Square).then_inc(self.squared, 1)
        for g in range(G):
            act.wait_ge(self.ssq, g + 1)
            act.activation(self.square[:, 0, g * GC:(g + 1) * GC], k.ps[:, g, 0:GC], ACT.Sqrt,
                           bias=k.eps[:, 0:1], scale=1.0 / D).then_inc(self.rooted, 1)

    def tensor(self, pe):
        k = self.k
        pe.wait_ge(self.summed, KD - 1)
        for g in range(G):
            pe.matmul(k.ps[:, g, 0:GC], k.ones[:], self.total[:, g * GC:(g + 1) * GC],
                      start=True, stop=True).then_inc(self.ssq, 1)

    def sum_up(self, dve):
        k, total = self.k, self.total
        for d in range(1, KD):
            dve.wait_ge(self.squared, d + 1)
            first = self.square[:, 0, :] if d == 1 else total
            dve.tensor_tensor(total, first, self.square[:, d % 2, :], ALU.add).then_inc(self.summed, 1)
            dve.drain()
        for g in range(G):
            dve.wait_ge(self.rooted, g + 1)
            dve.reciprocal(total[:, g * GC:(g + 1) * GC], self.square[:, 0, g * GC:(g + 1) * GC])
        dve.drain()

    def vector(self, dve):
        k, total = self.k, self.total
        self.sum_up(dve)
        for d in range(KD):
            dve.scalar_tensor_tensor(self.hT[:, d, :], k.xT[:, d, :], self.weight[:, d:d + 1], total,
                                     ALU.mult, ALU.mult).then_inc(self.normed, 1)


class SplitNorm(Norm):

    def __init__(self, k, ctx, h, weight, square=None, total=None):
        super().__init__(k, ctx, h, weight, square, total)
        self.exact = self.square
        self.scaled, self.high, self.even_low = k.sems(ctx, "norm_scaled", "norm_high", "norm_even_low")

    def round(self, act):
        for d in range(KD):
            act.wait_ge(self.scaled, d + 1)
            act.copy(self.hT[:, 0, d, :], self.exact[:, d % 2, :]).then_inc(self.high, 1)

    def low(self, eng, d):
        eng.wait_ge(self.high, d + 1)
        return eng.tensor_tensor(self.hT[:, 1, d, :], self.exact[:, d % 2, :], self.hT[:, 0, d, :].bitcast(F32), ALU.subtract)

    def pool(self, pool):
        for d in range(1, KD, 2):
            pool.wait_ge(self.even_low, d // 2 + 1)
            self.low(pool, d).then_inc(self.normed, 2)

    def vector(self, dve):
        self.sum_up(dve)
        for d in range(KD):
            if d >= 2:
                dve.wait_ge(self.even_low if d % 2 == 0 else self.normed, d // 2 if d % 2 == 0 else d - 1)
            dve.scalar_tensor_tensor(self.exact[:, d % 2, :], self.k.xT[:, d, :], self.weight[:, d:d + 1], self.total,
                                     ALU.mult, ALU.mult).then_inc(self.scaled, 1)
            if d % 2:
                self.low(dve, d - 1).then_inc(self.even_low, 1)
        dve.wait_ge(self.normed, KD)



def project_rows(k, ctx, block, chunks, scores=False, moves=None):
    nc, io, ps, hT = k.nc, k.io, k.ps, k.hT
    w_in = io["w_in"][0].rearrange("(k p) n -> p k n", p=P)
    jobs = [(c, r) for c in chunks for r in range(NT + 1)]
    rotated = {"aq", "ak", "iq", "ik"}
    width = {c: IK_COLS if c == "ik" else 512 for c in COL}
    turns = {"aq": k.qT, "ak": k.kT, "iq": k.iqT, "ik": k.ikT}
    RAW = 3
    LAG = 3
    if scores:
        index = PromptScores(k, ctx)
        first = sum(c in rotated for c in chunks) * (NT + 1) + LAG - 1
        assert all(c not in rotated for c, _ in jobs[first:]) and 2 * (len(jobs) - first) >= len(index.steps)

    def score_steps(j):
        at = 2 * (j - first) if scores else 0
        return range(at, min(at + 2, len(index.steps))) if scores and j >= first else range(0)

    nth_rot, nth_store = {}, {}
    for j, (c, r) in enumerate(jobs):
        if c in rotated:
            nth_rot[j] = len(nth_rot)
        if c in ("ak", "av", "ik", "bi", "bg") or r == NT:
            nth_store[j] = len(nth_store)

    def dest(c, r):
        if r == NT:
            return {"ak": io["k_sample"], "av": io["v_sample"], "ik": io["kidx_sample"], "aq": k.scratch["q_s"],
                    "iq": k.scratch["iq_s"], "bi": k.scratch["bi"][SEQ:R], "bg": k.scratch["bg"][SEQ:R]}[c]
        rows = slice(r * P, (r + 1) * P)
        return {"ak": io["k_prompt"], "av": io["v_prompt"], "ik": io["kidx_prompt"],
                "bi": k.scratch["bi"], "bg": k.scratch["bg"]}[c][rows]

    w = k.sb(ctx, "w_chunk", [P, 2, KD, 512])
    raw = k.sb(ctx, "raw", [P, RAW, 512])
    rot = k.sb(ctx, "rot", [P, RAW, 512])
    part = k.sb(ctx, "rope_part", [P, 2, 512])
    w_landed = k.sem_ring(ctx, "w_landed", 2)
    stored = k.sem_ring(ctx, "rows_stored", RAW)
    projected, taken, roped, turned, copied, iw_stored = k.sems(
        ctx, "projected", "taken", "roped", "turned", "copied", "iw_stored")

    def stores_before(j):
        return sum(1 for i in nth_store if i < j and i % RAW == j % RAW)

    @block.sync
    def _(sp):
        def load(i):
            c = chunks[i]
            if i >= 2:
                sp.wait_ge(projected, (NT + 1) * (i - 1))
            sp.dma_start(w[:, i % 2, :, 0:width[c]], w_in[:, :, COL[c]:COL[c] + width[c]]).then_inc(w_landed[i % 2], 16)

        load(0)
        for j, (c, r) in enumerate(jobs):
            i = j // (NT + 1)
            if r == 1 and i + 1 < len(chunks):
                load(i + 1)
            if j in nth_store:
                n = rows_of(r)
                if c in rotated:
                    sp.wait_ge(roped, nth_rot[j] + 1)
                    cols = DH if c == "ik" else 512
                    sp.dma_start(dest(c, r), rot[0:n, j % RAW, 0:cols]).then_inc(stored[j % RAW], 16)
                else:
                    sp.wait_ge(taken, j + 1)
                    sp.dma_start(dest(c, r), raw[0:n, j % RAW, :]).then_inc(stored[j % RAW], 16)
        if "ik" in chunks:
            sp.wait_ge(taken, len(jobs))
            sp.dma_start(k.scratch["iw_s"], k.iw[0:NS, NT, :]).then_inc(iw_stored, 16)
            sp.wait_ge(iw_stored, 16)
        for s in range(RAW):
            sp.wait_ge(stored[s], 16 * sum(1 for i in nth_store if i % RAW == s))

    @block.tensor
    def _(pe):
        turn_jobs = [j for j in range(len(jobs)) if jobs[j][0] in rotated]

        def turn(j):
            c, r = jobs[j]
            n, t = rows_of(r), nth_rot[j]
            pe.wait_ge(roped, t + 1)
            if t >= 4:
                pe.wait_ge(copied, t - 3)
            for i in range(1 if c == "ik" else 4):
                m = pe.transpose(ps[:, 4 + t % 4, i * P:i * P + n], rot[0:n, j % RAW, i * P:(i + 1) * P],
                                 k.ident[0:n, 0:n])
            m.then_inc(turned, 1)

        for j, (c, r) in enumerate(jobs):
            i, n = j // (NT + 1), rows_of(r)
            if r == 0:
                pe.wait_ge(w_landed[i % 2], 16 * (i // 2 + 1))
            if j >= 4:
                pe.wait_ge(taken, j - 3)
            for d in range(KD):
                m = pe.matmul(ps[0:n, j % 4, 0:width[c]], hT[:, d, r * P:r * P + n], w[:, i % 2, d, 0:width[c]],
                              start=d == 0, stop=d == KD - 1)
            m.then_inc(projected, 1)
            if j - LAG + 1 in nth_rot:
                turn(j - LAG + 1)
            for u in score_steps(j):
                if u == 0:
                    pe.wait_ge(copied, len(nth_rot))
                index.tensor(pe, u)
        for j in range(len(jobs) - LAG + 1, len(jobs)):
            if j in nth_rot:
                turn(j)

    @block.scalar
    def _(act):
        def take(j):
            c, r = jobs[j]
            n = rows_of(r)
            act.wait_ge(projected, j + 1)
            if j >= RAW:
                if j - RAW in nth_rot:
                    act.wait_ge(roped, nth_rot[j - RAW] + 1)
                if stores_before(j):
                    act.wait_ge(stored[j % RAW], 16 * stores_before(j))
            src, dst = ps[0:n, j % 4, 0:width[c]], raw[0:n, j % RAW, 0:width[c]]
            if c == "ik":
                act.activation(k.iw[0:n, r, :], src[:, DH:IK_COLS], ACT.Copy, scale=float(np.float32(H ** -0.5) * DH ** -0.5))
            act.activation(dst, src, ACT.Silu if c == "bg" else ACT.Copy).then_inc(taken, 1)

        def copy_turned(j):
            c, r = jobs[j]
            n, t = rows_of(r), nth_rot[j]
            act.wait_ge(turned, t + 1)
            src = ps[:, 4 + t % 4, :].rearrange("p (i n) -> p i n", n=P)
            if c == "ik":
                act.copy(k.ikT[:, r * P:r * P + n], src[:, 0, 0:n]).then_inc(copied, 1)
            else:
                act.copy(turns[c][:, :, r * P:r * P + n], src[:, :, 0:n]).then_inc(copied, 1)

        k.banks_taken = (taken, len(jobs))
        for j in range(len(jobs)):
            take(j)
            if j - LAG in nth_rot:
                copy_turned(j - LAG)
            for u in score_steps(j):
                index.scalar(act, u)
        for j in range(len(jobs) - LAG, len(jobs)):
            if j in nth_rot:
                copy_turned(j)

    @block.gpsimd
    def _(pool):
        for j, (c, r) in enumerate(jobs):
            if c not in rotated:
                continue
            n, t = rows_of(r), nth_rot[j]
            heads = 1 if c == "ik" else H
            cols = heads * DH
            pool.wait_ge(taken, j + 1)
            if t >= RAW:
                pool.wait_ge(turned, t - RAW + 1)
            if stores_before(j):
                pool.wait_ge(stored[j % RAW], 16 * stores_before(j))
            x = raw[0:n, j % RAW, 0:cols].rearrange("p (h t d) -> p h t d", h=heads, t=2)
            table = k.rope[0:n, r, :].rearrange("p (a t d) -> p a t d", a=2, t=2)
            for a, v in ((0, x), (1, x[:, :, ::-1, :])):
                pool.tensor_tensor(part[0:n, a, 0:cols].rearrange("p (h t d) -> p h t d", h=heads, t=2), v,
                                   table[:, a, :, :][:, None, :, :].broadcast_to([n, heads, 2, DH // 2]), ALU.mult)
            pool.drain()
            if c == "ik":
                pool.tensor_tensor(rot[0:n, j % RAW, cols:2 * cols], part[0:n, 0, 0:cols], part[0:n, 1, 0:cols], ALU.add)
            pool.tensor_tensor(rot[0:n, j % RAW, 0:cols], part[0:n, 0, 0:cols], part[0:n, 1, 0:cols],
                               ALU.add).then_inc(roped, 1)
            pool.drain()
        if scores:
            for u in range(len(index.steps)):
                if u in moves:
                    moves[u](pool)
                index.pool(pool, u)



def lower_bound(k, ctx, block):
    t = k.sb(ctx, "lb_terms", [P, 5, BH])
    lb_ready, exped = k.sems(ctx, "lb_ready", "exped")

    @block.scalar
    def _(act):
        act.wait_ge(lb_ready, 1)
        for i in range(2):
            act.activation(t[:, i, :], t[:, i, :], ACT.Exp).then_inc(exped, 1)

    @block.vector
    def _(dve):
        dve.tensor_tensor(t[:, 2, :], k.lb_logit[0], k.lb_logit[1], ALU.max)
        dve.drain()
        for i in range(2):
            dve.tensor_tensor(t[:, i, :], k.lb_logit[i], t[:, 2, :], ALU.subtract)
        dve.drain()
        dve.tensor_copy(t[:, 3, :], t[:, 2, :]).then_inc(lb_ready, 1)
        dve.wait_ge(exped, 2)
        dve.tensor_tensor(t[:, 3, :], t[:, 0, :], t[:, 1, :], ALU.add)
        dve.drain()
        dve.reciprocal(t[:, 4, :], t[:, 3, :])
        dve.drain()
        dve.tensor_tensor(k.lb[:, 0, :], t[:, 0, :], t[:, 4, :], ALU.mult)
        dve.drain()
        dve.tensor_scalar(k.lb[:, 1, :], k.lb[:, 0, :], -1.0, 1.0, ALU.mult, ALU.add)


def project_gates(k, ctx, block):
    nc, io, ps, hT = k.nc, k.io, k.ps, k.hT
    w_in = io["w_in"][0].rearrange("(k p) n -> p k n", p=P)
    w = k.sb(ctx, "w_gate_tile", [P, 2, KD, P])
    out = k.sb(ctx, "gate_out", [P, 2, R])
    keyf = k.sb(ctx, "gate_key", [P, 2, R])
    f = k.xT[:, KD - BH:KD, :]
    reset = k.sb(ctx, "reset", [P, R])
    w_landed, stored_q, stored_k, stored_b = (k.sem_ring(ctx, n, 2) for n in ("w_landed", "stored_q", "stored_k", "stored_b"))
    (const_landed,) = k.sems(ctx, "const_landed")
    multiplied, taken, sig_taken, f_made, key_made, log_taken, scanned = k.sems(
        ctx, "multiplied", "taken", "sig_taken", "f_made", "key_made", "log_taken", "scanned")
    lb_value, lb_rest = k.lb[:, 0, :], k.lb[:, 1, :]
    banks_taken = k.banks_taken
    k.banks_taken = (taken, 2 * BH)

    @block.sync
    def _(sp):
        def load(i):
            at = COL["bq" if i < BH else "bf"] + (i % BH) * P
            sp.dma_start(w[:, i % 2], w_in[:, :, at:at + P]).then_inc(w_landed[i % 2], 16)

        sp.dma_start(reset[:], io["c_reset"].broadcast_to([P, R])).then_inc(const_landed, 16)
        load(0)
        load(1)
        for i in range(2 * BH):
            if i + 2 < 2 * BH:
                sp.wait_ge(multiplied, i + 1)
                load(i + 2)
            if i < BH:
                sp.wait_ge(taken, i + 1)
                sp.dma_start(k.scratch["gq"][i], out[:, i % 2, :]).then_inc(stored_q[i % 2], 16)
            else:
                sp.wait_ge(key_made, i - BH + 1)
                sp.dma_start(k.scratch["gk"][i - BH], keyf[:, i % 2, :]).then_inc(stored_k[i % 2], 16)
        for i in range(BH):
            sp.wait_ge(scanned, i + 1)
            sp.dma_start(k.scratch["gb"][i], out[:, i % 2, :]).then_inc(stored_b[i % 2], 16)
        for s in range(2):
            sp.wait_ge(stored_k[s], 16 * BH // 2)
            sp.wait_ge(stored_b[s], 16 * BH // 2)

    @block.tensor
    def _(pe):
        pe.wait_ge(*banks_taken)
        for i in range(2 * BH):
            b = 4 * (i % 2)
            pe.wait_ge(w_landed[i % 2], 16 * (i // 2 + 1))
            if i >= 2:
                pe.wait_ge(taken, i - 1)
            for d in range(KD):
                for g in range(G):
                    m = pe.matmul(ps[:, b + g, 0:GC], w[:, i % 2, d, :], hT[:, d, g * GC:(g + 1) * GC],
                                  start=d == 0, stop=d == KD - 1)
            m.then_inc(multiplied, 1)

    @block.scalar
    def _(act):
        for i in range(BH):
            act.wait_ge(multiplied, i + 1)
            if i >= 2:
                act.wait_ge(stored_q[i % 2], 16 * (i // 2))
            act.activation(grouped(out[:, i % 2, :]), bank_cols(ps, 4 * (i % 2)), ACT.Silu).then_inc(taken, 1)
        for i in range(BH):
            act.wait_ge(multiplied, BH + i + 1)
            act.activation(grouped(f[:, i, :]), bank_cols(ps, 4 * (i % 2)), ACT.Sigmoid).then_inc(sig_taken, 1)
            if i >= 2:
                act.wait_ge(stored_k[i % 2], 16 * (i // 2))
            act.activation(grouped(keyf[:, i % 2, :]), bank_cols(ps, 4 * (i % 2)), ACT.Sigmoid, scale=-1.0).then_inc(taken, 1)
        for i in range(BH):
            act.wait_ge(f_made, i + 1)
            act.activation(f[:, i, :], f[:, i, :], ACT.Ln).then_inc(log_taken, 1)

    @block.gpsimd
    def _(pool):
        for i in range(BH):
            pool.wait_ge(sig_taken, i + 1)
            pool.tensor_scalar(f[:, i, :], f[:, i, :], lb_rest[:, i:i + 1], lb_value[:, i:i + 1],
                               ALU.mult, ALU.add).then_inc(f_made, 1)
            pool.wait_ge(taken, BH + i + 1)
            pool.tensor_scalar(keyf[:, i % 2, :], keyf[:, i % 2, :], lb_rest[:, i:i + 1], None, ALU.mult).then_inc(key_made, 1)

    @block.vector
    def _(dve):
        dve.wait_ge(const_landed, 16)
        for i in range(BH):
            dve.wait_ge(log_taken, i + 1)
            dve.wait_ge(*((stored_q[i % 2], 16 * BH // 2) if i < 2 else (stored_b[i % 2], 16 * (i // 2))))
            dve.tensor_tensor_scan(out[:, i % 2, :], reset[:], f[:, i, :], 0.0, ALU.mult, ALU.add).then_inc(scanned, 1)



def recurrence(k, ctx, block):
    nc, io, ps, mixT = k.nc, k.io, k.ps, k.hT
    tiles = NT + 1
    q = k.sb(ctx, "g_q", [P, 2, BH, P])
    key = k.sb(ctx, "g_key", [P, 2, BH, P])
    b = k.sb(ctx, "g_b", [P, 2, BH, P])
    val = k.sb(ctx, "g_val", [P, 2, BH, P])
    gate = k.sb(ctx, "g_gate", [P, 2, BH, P])
    dif = k.sb(ctx, "g_dif", [P, 2, BH * P])
    uq = k.sb(ctx, "g_uq", [P, 2, BH, P])
    uk = k.sb(ctx, "g_uk", [P, 2, BH, P])
    att = k.sb(ctx, "g_att", [P, BH, P])
    eb = k.sb(ctx, "g_eb", [P, BH, P])
    el = k.sb(ctx, "g_el", [P, BH, P])
    qe = k.sb(ctx, "g_qe", [P, BH, P])
    ke = k.sb(ctx, "g_ke", [P, BH, P])
    ker = k.sb(ctx, "g_ker", [P, BH, P])
    state = k.sb(ctx, "g_state", [P, BH, P])
    osq = k.sb(ctx, "g_osq", [P, BH, P])
    on = k.sb(ctx, "g_on", [P, BH, P])
    small = k.sb(ctx, "g_small", [P, 4, BH])
    normw = k.sb(ctx, "g_normw", [P, P])
    level = k.sb(ctx, "g_level", [P, LEVELS + 1, P], I32)
    s0 = k.sb(ctx, "g_s0", [P, BD * BH, P])
    snew = k.sb(ctx, "g_snew", [P, 2, BD, P])
    qm = k.sb(ctx, "g_qm", [P, BH, BD, NS])
    vm = k.sb(ctx, "g_vm", [NS, BH, BD, P])
    bcol = k.sb(ctx, "g_bcol", [P, BD * NS])
    brow = k.sb(ctx, "g_brow", [NS, BD])
    x_rows = k.sb(ctx, "x_rows", [P, 2, D])
    x_landed = k.sem_ring(ctx, "x_landed", 2)
    x_turned, x_copied = k.sems(ctx, "x_turned", "x_copied")
    landed = k.sem_ring(ctx, "g_landed", 2)
    const, s0_landed, state_stored = k.sems(ctx, "g_const", "g_s0_landed", "g_state_stored")
    (dif_made, exped, scaled, multiplied, placed, edge_dif, edge_exp, qe_made, ke_turned, ke_copied, out_done,
     update_done, updated, squared, means, rstd_made, gated, out_turned, out_copied, s_update, snew_made,
     qm_made, tile_read) = k.sems(
        ctx, "g_dif_made", "g_exped", "g_scaled", "g_multiplied", "g_placed", "g_edge_dif", "g_edge_exp",
        "g_qe_made", "g_ke_turned", "g_ke_copied", "g_out_done", "g_update_done", "g_updated", "g_squared",
        "g_means", "g_rstd_made", "g_gated", "g_out_turned", "g_out_copied", "g_s_update", "g_snew_made",
        "g_qm_made", "g_tile_read")

    def levels_of(c):
        return list(range(LEVELS)) if c < NT else list(range(int(math.log2(TD))))

    def level_count(c):
        return sum(len(levels_of(i)) for i in range(c))

    def product_count(c):
        return level_count(c) + c

    def turn_x(pe, c, half):
        n = rows_of(c)
        pe.wait_ge(x_landed[c % 2], 16 * (c // 2 + 1))
        if c or half:
            pe.wait_ge(x_copied, 2 * c + half)
        for d in range(4):
            at = (4 * half + d) * P
            m = pe.transpose(ps[:, 7, d * P:d * P + n], x_rows[0:n, c % 2, at:at + P], k.ident[0:n, 0:n])
        m.then_inc(x_turned, 1)

    def copy_x(act, c, half):
        n = rows_of(c)
        act.wait_ge(x_turned, 2 * c + half + 1)
        act.copy(k.xT[:, 4 * half:4 * half + 4, c * P:c * P + n], ps[:, 7, :].rearrange("p (d n) -> p d n", n=P)[:, :, 0:n]
                 ).then_inc(x_copied, 1)

    scr = k.scratch

    @block.sync
    def _(sp):
        sp.dma_start(normw[:], io["glr_norm"].broadcast_to([P, P])).then_inc(const, 16)
        sp.dma_start(level[:], io["c_level"]).then_inc(const, 16)
        sp.dma_start(bcol[:], io["c_batchcol"].broadcast_to([P, BD * NS])).then_inc(const, 16)
        sp.dma_start(brow[:], io["c_batchrow"]).then_inc(const, 16)
        sp.dma_start(s0[:], io["state_glr"][0].rearrange("b h d v -> d (b h) v")).then_inc(s0_landed, 16)
        for c in range(tiles):
            n = rows_of(c)
            if c >= 2:
                sp.wait_ge(tile_read, c - 1)
            for buf, name in ((q, "gq"), (key, "gk"), (b, "gb")):
                sp.dma_start(buf[:, c % 2, :, 0:n], scr[name].rearrange("h d t -> d h t")[:, :, c * P:c * P + n]
                             ).then_inc(landed[c % 2], 16)
            src = io["x_prompt"][0, c * P:(c + 1) * P, :] if c < NT else io["x_sample"].rearrange("b t d -> (b t) d")
            if c >= 2:
                sp.wait_ge(x_turned, 2 * (c - 1))
            sp.dma_start(x_rows[0:n, c % 2, :], src).then_inc(x_landed[c % 2], 16)
            for buf, name in ((val, "bi"), (gate, "bg")):
                sp.dma_start(buf[0:n, c % 2], scr[name][c * P:c * P + n].rearrange("t (h v) -> t h v", h=BH)
                             ).then_inc(landed[c % 2], 16)
        sp.wait_ge(updated, NT)
        sp.dma_start(io["glr_prompt"][0, 0].rearrange("h d v -> d h v"), state[:]).then_inc(state_stored, 16)
        for h in range(BH):
            sp.wait_ge(snew_made, h + 1)
            sp.dma_start(io["glr_sample"][0].rearrange("b h d v -> h d b v")[h], snew[:, h % 2]).then_inc(state_stored, 16)
            sp.wait_ge(state_stored, 16 * (h + 2))

    @block.vector
    def _(dve):
        dve.memset(att[:], 0.0)
        dve.memset(state[:], 0.0)
        dve.memset(uq[:], 0.0)
        dve.memset(uk[:], 0.0)
        dve.memset(dif[:], 0.0)
        dve.wait_ge(const, 64)
        dve.drain()
        for c in range(tiles):
            n, s = rows_of(c), c % 2
            lv = levels_of(c)
            dve.wait_ge(landed[s], 80 * (c // 2 + 1))
            bt, qt, kt = b[:, s, :, 0:n], q[:, s, :, 0:n], key[:, s, :, 0:n]

            def halves(ap, w):
                return ap.rearrange("p h (m a w) -> p h m a w", a=2, w=w)

            def make_dif(i):
                w = 1 << lv[i]
                e = level_count(c) + i
                if e >= 2:
                    dve.wait_ge(scaled, e - 1)
                d4 = dif[:, e % 2, 0:BH * n].rearrange("p (h m a w) -> p h m a w", h=BH, a=2, w=w)
                b4 = halves(bt, w)
                ref = b4[:, :, :, 0, w - 1:w].broadcast_to([P, BH, n // (2 * w), w])
                dve.tensor_tensor(d4[:, :, :, 0, :], ref, b4[:, :, :, 0, :], ALU.subtract)
                dve.tensor_tensor(d4[:, :, :, 1, :], b4[:, :, :, 1, :], ref, ALU.subtract).then_inc(dif_made, 1)

            def scale(i):
                w = 1 << lv[i]
                e = level_count(c) + i
                dve.wait_ge(exped, e + 1)
                u = product_count(c) + i
                if e >= 2:
                    before = u - 2 if i >= 2 else (product_count(c - 1) + len(levels_of(c - 1)) - 2 + i if c else 0)
                    dve.wait_ge(multiplied, before + 1)
                d4 = dif[:, e % 2, 0:BH * n].rearrange("p (h m a w) -> p h m a w", h=BH, a=2, w=w)
                dve.tensor_tensor(halves(uk[:, e % 2, :, 0:n], w)[:, :, :, 0, :], halves(kt, w)[:, :, :, 0, :],
                                  d4[:, :, :, 0, :], ALU.mult)
                dve.tensor_tensor(halves(uq[:, e % 2, :, 0:n], w)[:, :, :, 1, :], halves(qt, w)[:, :, :, 1, :],
                                  d4[:, :, :, 1, :], ALU.mult).then_inc(scaled, 1)

            def place(i):
                u = product_count(c) + i
                lvl = lv[i] if i < len(lv) else LEVELS
                dve.wait_ge(multiplied, u + 1)
                if i == 0 and c:
                    dve.wait_ge(out_done, c)
                    if c == NT:
                        dve.memset(att[0:n, :, 0:n], 0.0)
                        dve.drain()
                src = ps[0:n, u % 2, :].rearrange("p (h t) -> p h t", h=BH)[:, :, 0:n]
                dve.copy_predicated(att[0:n, :, 0:n], level[0:n, lvl, 0:n][:, None, :].broadcast_to([n, BH, n]), src
                                    ).then_inc(placed, 1)
                dve.drain()

            span = P if c < NT else TD
            if c:
                dve.wait_ge(ke_turned, c)
            bs = bt.rearrange("p h (m w) -> p h m w", w=span)
            dve.tensor_tensor(el[:, :, 0:n].rearrange("p h (m w) -> p h m w", w=span),
                              bs[:, :, :, span - 1:span].broadcast_to([P, BH, n // span, span]), bs, ALU.subtract
                              ).then_inc(edge_dif, 1)
            make_dif(0)
            for i in range(len(lv)):
                if i + 1 < len(lv):
                    make_dif(i + 1)
                scale(i)
                if i == 0:
                    dve.wait_ge(edge_exp, c + 1)
                    if c:
                        dve.wait_ge(out_done, c)
                    dve.tensor_tensor(ke[:, :, 0:n], kt, el[:, :, 0:n], ALU.mult)
                    dve.tensor_tensor(qe[:, :, 0:n], qt, eb[:, :, 0:n], ALU.mult).then_inc(qe_made, 1)
                    dve.drain()
                if i:
                    place(i - 1)
            place(len(lv) - 1)
            place(len(lv))
            if c == NT:
                for h in range(BH):
                    x = dve.tensor_tensor(qm[:, h], qe[:, h, 0:n][:, None, :].broadcast_to([P, BD, NS]),
                                          bcol[:].rearrange("p (b t) -> p b t", b=BD), ALU.mult)
                    y = dve.tensor_tensor(vm[:, h], val[0:NS, s, h, :][:, None, :].broadcast_to([NS, BD, P]),
                                          brow[:, :, None].broadcast_to([NS, BD, P]), ALU.mult)
                y.then_inc(qm_made, 1)
            if c < NT:
                dve.wait_ge(update_done, c + 1)
                dve.wait_ge(out_done, c + 1)
                for h in range(BH):
                    x = dve.scalar_tensor_tensor(state[:, h, :], state[:, h, :], eb[:, h, P - 1:P],
                                                 ps[:, 4, h * P:(h + 1) * P], ALU.mult, ALU.add)
                x.then_inc(updated, 1)
            else:
                dve.wait_ge(s0_landed, 16)
                s0v = s0[:].rearrange("p (b h) v -> p b h v", h=BH)
                for h in range(BH):
                    if h >= 2:
                        dve.wait_ge(state_stored, 16 * h)
                    last = eb[:, h, TD - 1:NS:TD]
                    dve.tensor_tensor(snew[:, h % 2], s0v[:, :, h, :], last[:, :, None].broadcast_to([P, BD, P]), ALU.mult)
                    dve.drain()
                    dve.wait_ge(s_update, h + 1)
                    dve.tensor_tensor(snew[:, h % 2], snew[:, h % 2],
                                      ps[:, 0:2, :].rearrange("p a (b v) -> p (a b) v", v=P), ALU.add).then_inc(snew_made, 1)
                    dve.drain()
            dve.wait_ge(squared, c + 1)
            dve.tensor_reduce(small[0:n, 0, :], osq[0:n], AX.X, ALU.add)
            dve.drain()
            dve.tensor_scalar(small[0:n, 1, :], small[0:n, 0, :], 1.0 / P, EPS, ALU.mult, ALU.add).then_inc(means, 1)
            dve.wait_ge(rstd_made, c + 1)
            if c:
                dve.wait_ge(out_turned, c)
            dve.tensor_tensor(on[0:n], ps[0:n, 3, :].rearrange("p (h v) -> p h v", h=BH),
                              small[0:n, 2, :][:, :, None].broadcast_to([n, BH, P]), ALU.mult)
            dve.drain()
            dve.tensor_tensor(on[0:n], on[0:n], normw[0:n][:, None, :].broadcast_to([n, BH, P]), ALU.mult)
            dve.drain()
            dve.tensor_tensor(on[0:n], on[0:n], gate[0:n, s], ALU.mult).then_inc(gated, 1)
            dve.drain()

    @block.scalar
    def _(act):
        for c in range(tiles):
            n, s = rows_of(c), c % 2
            lv = levels_of(c)
            copy_x(act, c, 0)
            act.wait_ge(edge_dif, c + 1)
            if c:
                act.wait_ge(updated, c)
            act.activation(eb[:, :, 0:n], b[:, s, :, 0:n], ACT.Exp)
            act.activation(el[:, :, 0:n], el[:, :, 0:n], ACT.Exp).then_inc(edge_exp, 1)
            for i in range(len(lv)):
                e = level_count(c) + i
                act.wait_ge(dif_made, e + 1)
                act.activation(dif[:, e % 2, 0:BH * n], dif[:, e % 2, 0:BH * n], ACT.Exp).then_inc(exped, 1)
            act.wait_ge(ke_turned, c + 1)
            act.copy(ker[0:n], ps[0:n, 2, :].rearrange("p (h d) -> p h d", h=BH)).then_inc(ke_copied, 1)
            act.wait_ge(out_done, c + 1)
            if c:
                act.wait_ge(means, c)
            act.activation(osq[0:n], ps[0:n, 3, :].rearrange("p (h v) -> p h v", h=BH), ACT.Square).then_inc(squared, 1)
            act.wait_ge(out_turned, c + 1)
            src = ps[:, 5, :].rearrange("p (h t) -> p h t", h=BH)
            act.copy(mixT[:, BH:2 * BH, c * P:c * P + n], src[:, :, 0:n]).then_inc(out_copied, 1)
            copy_x(act, c, 1)

    @block.gpsimd
    def _(pool):
        pool.memset(small[:, 3, :], -0.5)
        pool.drain()
        for c in range(tiles):
            n = rows_of(c)
            pool.wait_ge(means, c + 1)
            if c:
                pool.wait_ge(gated, c)
            pool.tensor_tensor(small[0:n, 2, :], small[0:n, 1, :], small[0:n, 3, :], ALU.pow).then_inc(rstd_made, 1)

    @block.tensor
    def _(pe):
        for c in range(tiles):
            n, s = rows_of(c), c % 2
            lv = levels_of(c)
            turn_x(pe, c, 0)
            pe.wait_ge(landed[s], 80 * (c // 2 + 1))

            def product(i):
                u = product_count(c) + i
                if u >= 2:
                    pe.wait_ge(placed, u - 1)
                e = level_count(c) + i
                if i < len(lv):
                    pe.wait_ge(scaled, e + 1)
                for h in range(BH):
                    lhs = uk[:, e % 2, h, 0:n] if i < len(lv) else key[:, s, h, 0:n]
                    rhs = uq[:, e % 2, h, 0:n] if i < len(lv) else q[:, s, h, 0:n]
                    m = pe.matmul(ps[0:n, u % 2, h * P:h * P + n], lhs, rhs, start=True, stop=True)
                m.then_inc(multiplied, 1)

            for i in range(len(lv) + 1):
                product(i)
                if i == 0:
                    pe.wait_ge(qe_made, c + 1)
                    if c:
                        pe.wait_ge(ke_copied, c)
                    for h in range(BH):
                        m = pe.transpose(ps[0:n, 2, h * P:(h + 1) * P], ke[:, h, 0:n], k.ident[:])
                    m.then_inc(ke_turned, 1)
            pe.wait_ge(placed, product_count(c + 1))
            if c:
                pe.wait_ge(updated, c)
                pe.wait_ge(gated, c)
            if c == NT:
                pe.wait_ge(qm_made, 1)
                pe.wait_ge(s0_landed, 16)
            for h in range(BH):
                o = ps[0:n, 3, h * P:(h + 1) * P]
                pe.matmul(o, att[0:n, h, 0:n], val[0:n, s, h, :], start=True, stop=False)
                if c < NT:
                    m = pe.matmul(o, qe[:, h, :], state[:, h, :], start=False, stop=True)
                else:
                    for e in range(BD):
                        m = pe.matmul(o, qm[:, h, e, :], s0[:, e * BH + h, :], start=False, stop=e == BD - 1)
            m.then_inc(out_done, 1)
            pe.wait_ge(ke_copied, c + 1)
            if c < NT:
                for h in range(BH):
                    m = pe.matmul(ps[:, 4, h * P:(h + 1) * P], ker[0:n, h, :], val[0:n, s, h, :], start=True, stop=True)
                m.then_inc(update_done, 1)
            else:
                for h in range(BH):
                    if h:
                        pe.wait_ge(snew_made, h)
                    for a in range(2):
                        m = pe.matmul(ps[:, a, :], ker[0:n, h, :], vm[:, h, a * 4:(a + 1) * 4, :].rearrange("p b v -> p (b v)"),
                                      start=True, stop=True)
                    m.then_inc(s_update, 1)
            pe.wait_ge(gated, c + 1)
            if c:
                pe.wait_ge(out_copied, c)
            for h in range(BH):
                m = pe.transpose(ps[:, 5, h * P:h * P + n], on[0:n, h, :], k.ident[0:n, 0:n])
            m.then_inc(out_turned, 1)
            turn_x(pe, c, 1)
            pe.matmul(ps[0:1, 6, 0:1], k.ones[:, 0:1], k.ones[:, 0:1], start=True, stop=True).then_inc(tile_read, 1)



def mask_offset(i):
    return sum((j + 1) * P for j in range(2, i))


def mask_of(k, i):
    at = mask_offset(i)
    return k.xT[:, 0:4, :].rearrange("p d n -> p (d n)")[:, at:at + (i + 1) * P]


class PromptScores:

    def __init__(self, k, ctx):
        self.k = k
        self.steps = [(i, h) for i in range(2, NT) for h in range(H)]
        self.relu = k.xT[:, 4:6, :]
        self.spare = k.sb(ctx, "spare", [1, 1])
        self.scored, self.rectified, self.weighted, self.summed = k.sems(ctx, "scored", "rectified", "weighted", "summed")

    def tensor(self, pe, u):
        k, (i, h) = self.k, self.steps[u]
        w, row = (i + 1) * P, (h % 2) * DH
        if u >= 2:
            pe.wait_ge(self.rectified, u - 1)
        for a in range(0, w, 512):
            n = min(512, w - a)
            m = pe.matmul(k.ps[:, 4 + 2 * (u % 2) + a // 512, 0:n], k.iqT[row:row + DH, h // 2, i * P:(i + 1) * P],
                          k.ikT[row:row + DH, a:a + n], start=True, stop=True)
        m.then_inc(self.scored, 1)

    def scalar(self, act, u):
        k, (i, h) = self.k, self.steps[u]
        w, b = (i + 1) * P, 4 + 2 * (u % 2)
        relu = self.relu[:, u % 2, 0:w]
        act.wait_ge(self.scored, u + 1)
        if u >= 2:
            act.wait_ge(self.summed, u - 1)
        act.activation(relu, k.ps[:, b:b + 2, :].rearrange("p b n -> p (b n)")[:, 0:w], ACT.Relu).then_inc(self.rectified, 1)
        act.drain()
        act.activation(mask_of(k, i) if h == 0 else relu, relu, ACT.Copy, scale=k.iw[:, i, h:h + 1]).then_inc(self.weighted, 1)

    def pool(self, pool, u):
        k, (i, h) = self.k, self.steps[u]
        sc = mask_of(k, i)
        pool.wait_ge(self.weighted, u + 1)
        if h == 0:
            pool.tensor_copy(self.spare[:], k.ones[0:1, 0:1]).then_inc(self.summed, 1)
        else:
            pool.tensor_tensor(sc, sc, self.relu[:, u % 2, 0:(i + 1) * P], ALU.add).then_inc(self.summed, 1)
        pool.drain()
        if h == H - 1:
            diag = sc[:, i * P:(i + 1) * P]
            pool.affine_select(out=diag, in_=diag, compare_op=ALU.is_ge, fill=UNSEEN, base=0,
                               pattern=[[-1, P]], channel_multiplier=1)


def take_best(k, dve, best, i, first, rounds):
    sc = mask_of(k, i)
    with dve.Fori(0, rounds):
        dve.max(best[:], sc)
        dve.drain()
        dve.match_replace(sc, best[:], sc, TAKEN)
        dve.drain()
    if first + rounds == ROUNDS:
        dve.tensor_scalar(sc, sc, TAKEN, MASKED, ALU.is_gt, ALU.mult)
        dve.drain()



def attend_prompt(k, ctx, block):
    nc, io, ps, mixT = k.nc, k.io, k.ps, k.hT
    steps = [(i, h) for i in range(NT) for h in range(H)]
    scale = DH ** -0.5
    v = k.sb(ctx, "v_rows", [P, NT, H * DH])
    causal = k.sb(ctx, "causal", [P, 2, 2 * P])
    logit = k.sb(ctx, "logit", [P, 2, SEQ])
    prob = k.sb(ctx, "prob", [P, 2, SEQ])
    probT = k.sb(ctx, "probT", [P, 2, NT, P])
    top = k.sb(ctx, "top", [P, 2, 2])
    total = k.sb(ctx, "total", [P, 2, H])
    inv = k.sb(ctx, "inv", [P, H])
    att = k.sb(ctx, "att_rows", [P, 2, H * DH])
    best = k.sb(ctx, "best", [P, 8])
    v_landed, c_landed = k.sems(ctx, "v_landed", "c_landed")
    scored, biased, exped, turned, copied, weighed, normed, att_turned, att_copied = k.sems(
        ctx, "scored", "biased", "exped", "turned", "copied", "weighed", "normed", "att_turned", "att_copied")

    def two_banks(b):
        return ps[:, b:b + 2, :].rearrange("p b n -> p (b n)")

    @block.sync
    def _(sp):
        sp.dma_start(causal[:, 0, 0:P], io["c_causal"]).then_inc(c_landed, 16)
        sp.dma_start(causal[:, 1, P:2 * P], io["c_causal"]).then_inc(c_landed, 16)
        sp.dma_start(v[:], io["v_prompt"].rearrange("(i p) n -> p i n", p=P)).then_inc(v_landed, 16)

    @block.tensor
    def _(pe):
        def score(u):
            i, h = steps[u]
            w, row = (i + 1) * P, (h % 2) * DH
            if u >= 2:
                pe.wait_ge(biased, u - 1)
            for a in range(0, w, 512):
                n = min(512, w - a)
                m = pe.matmul(ps[:, 2 * (u % 2) + a // 512, 0:n], k.qT[row:row + DH, h // 2, i * P:(i + 1) * P],
                              k.kT[row:row + DH, h // 2, a:a + n], start=True, stop=True)
            m.then_inc(scored, 1)

        def turn(u):
            i, h = steps[u]
            pe.wait_ge(exped, u + 1)
            if u:
                pe.wait_ge(copied, u)
            for j in range(i + 1):
                m = pe.transpose(ps[:, 4 + j // 4, (j % 4) * P:(j % 4 + 1) * P], prob[:, u % 2, j * P:(j + 1) * P], k.ident[:])
            m.then_inc(turned, 1)

        def weigh(u):
            i, h = steps[u]
            pe.wait_ge(copied, u + 1)
            if h == 0:
                pe.wait_ge(v_landed, 16)
                if i:
                    pe.wait_ge(normed, i)
            for j in range(i + 1):
                m = pe.matmul(ps[:, 6, h * DH:(h + 1) * DH], probT[:, u % 2, j, :], v[:, j, h * DH:(h + 1) * DH],
                              start=j == 0, stop=j == i)
            m.then_inc(weighed, 1)

        def turn_att(i):
            pe.wait_ge(normed, i + 1)
            if i:
                pe.wait_ge(att_copied, i)
            for f in range(4):
                m = pe.transpose(ps[:, 7, f * P:(f + 1) * P], att[:, i % 2, f * P:(f + 1) * P], k.ident[:])
            m.then_inc(att_turned, 1)

        score(0)
        for u in range(len(steps) + 1):
            if u + 1 < len(steps):
                score(u + 1)
            if u < len(steps):
                turn(u)
            if u:
                weigh(u - 1)
            if u >= 10 and (u - 10) % H == 0:
                turn_att((u - 10) // H)
        turn_att(NT - 1)

    @block.vector
    def _(dve):
        dve.memset(causal[:, 1, 0:P], 0.0)
        dve.wait_ge(c_landed, 32)
        dve.drain()

        def bias(u):
            i, h = steps[u]
            w = (i + 1) * P
            mask = causal[:, i, 0:w] if i < 2 else mask_of(k, i)
            dve.wait_ge(scored, u + 1)
            if u >= 2:
                dve.wait_ge(exped, u - 1)
            dve.tensor_tensor_reduce(logit[:, u % 2, 0:w], two_banks(2 * (u % 2))[:, 0:w], mask, 1.0, UNSEEN,
                                     ALU.add, ALU.max, top[:, u % 2, 0:1])
            dve.drain()
            dve.tensor_scalar(top[:, u % 2, 1:2], top[:, u % 2, 0:1], -scale, None, ALU.mult).then_inc(biased, 1)

        def normalise(i):
            dve.wait_ge(weighed, (i + 1) * H)
            if i >= 2:
                dve.wait_ge(att_turned, i - 1)
            dve.reciprocal(inv[:], total[:, i % 2, :])
            dve.drain()
            dve.tensor_tensor(att[:, i % 2].rearrange("p (h d) -> p h d", h=H), ps[:, 6, :].rearrange("p (h d) -> p h d", h=H),
                              inv[:][:, :, None].broadcast_to([P, H, DH]), ALU.mult).then_inc(normed, 1)
            dve.drain()

        for u, (i, h) in enumerate(steps):
            bias(u)
            if u >= H and h == 1:
                normalise(i - 1)
            if 1 <= i <= 4:
                take_best(k, dve, best, 6, u - H, 1)
            elif i in (5, 6):
                take_best(k, dve, best, 7, 2 * (u - 5 * H), 2)
        normalise(NT - 1)

    @block.scalar
    def _(act):
        def exp(u):
            i, h = steps[u]
            w = (i + 1) * P
            act.wait_ge(biased, u + 1)
            if u >= 2:
                act.wait_ge(turned, u - 1)
            if h == 0 and i >= 2:
                act.wait_ge(normed, i - 1)
            act.activation(prob[:, u % 2, 0:w], logit[:, u % 2, 0:w], ACT.Exp, bias=top[:, u % 2, 1:2], scale=scale,
                           accum_out=total[:, i % 2, h:h + 1])
            act.drain()
            act.copy(top[0:1, u % 2, 0:1], top[0:1, u % 2, 1:2]).then_inc(exped, 1)

        def copy(u):
            i, h = steps[u]
            act.wait_ge(turned, u + 1)
            if u >= 2:
                act.wait_ge(weighed, u - 1)
            act.copy(probT[:, u % 2].rearrange("p j n -> p (j n)")[:, 0:(i + 1) * P], two_banks(4)[:, 0:(i + 1) * P]
                     ).then_inc(copied, 1)

        def copy_att(i):
            act.wait_ge(att_turned, i + 1)
            act.copy(mixT[:, 0:4, i * P:(i + 1) * P], ps[:, 7, :].rearrange("p (f n) -> p f n", f=4)).then_inc(att_copied, 1)

        exp(0)
        for u in range(len(steps)):
            copy(u)
            if u + 1 < len(steps):
                exp(u + 1)
            if u >= 11 and (u - 11) % H == 0:
                copy_att((u - 11) // H)
        copy_att(NT - 1)



def score_sample(k, ctx, block):
    nc, io, ps = k.nc, k.io, k.ps
    N = BD * 4
    E16 = PAGE // 8
    pages = k.sb(ctx, "pages", [P, N], I32)
    index = k.sb(ctx, "index", [P, N], I32)
    keys = k.sb(ctx, "keys", [P, 4, E16 * DH])
    keysT = k.sb(ctx, "keysT", [P, 2, 8, P])
    part = k.sb(ctx, "part", [P, 2, 8 * 2 * TD * H])
    iq2 = k.sb(ctx, "iq_twice", [NS, H, 2, DH])
    bd = k.sb(ctx, "iq_blocks", [P, BD, 2, TD, H])
    wb = k.sb(ctx, "iw_all", [P, NS, H])
    sc = k.sb(ctx, "key_scores", [P, E16, 4, NS])
    newp = k.sb(ctx, "new_part", [NS, NS * H])
    news = k.sb(ctx, "new_scores", [NS, NS])
    newt = k.sb(ctx, "new_turned", [NS, NS])
    newb = k.sb(ctx, "new_bias", [NS, NS])
    newq = k.sb(ctx, "new_query", [NS, TD])
    g_landed = k.sem_ring(ctx, "keys_landed", 4)
    pt_landed, small_landed, placed = k.sems(ctx, "pt_landed", "small_landed", "placed")
    (indexed, turned, copied, multiplied, weighted, iq_turned, blocks_made, new_scored, new_summed, new_turned,
     new_ready, sc_turned, sc_copied, zeroed, reduced) = k.sems(
        ctx, "indexed", "turned", "copied", "multiplied", "weighted", "iq_turned", "blocks_made", "new_scored",
        "new_summed", "new_turned", "new_ready", "sc_turned", "sc_copied", "zeroed", "reduced")

    @block.sync
    def _(sp):
        src = io["page_table"].rearrange("b (k i) -> i b k", i=16)
        for s in range(8):
            sp.dma_start(pages[s:P:8, :].rearrange("p (b k) -> p b k", b=BD), src,
                         allow_slow_non_contiguous=True).then_inc(pt_landed, 16)
        iq = k.scratch["iq_s"].rearrange("r (h d) -> r h d", h=H)
        for a in range(2):
            sp.dma_start(iq2[:, :, a, :], iq).then_inc(small_landed, 16)
        sp.dma_start(wb[:].rearrange("p q h -> p (q h)"),
                     k.scratch["iw_s"].rearrange("(o q) h -> o (q h)", o=1).broadcast_to([P, NS * H])).then_inc(small_landed, 16)
        sp.dma_start(newb[:], io["c_newbias"]).then_inc(small_landed, 16)
        sp.wait_ge(new_ready, 1)
        sp.wait_ge(zeroed, 1)
        sp.dma_start(k.found[3 * NS:P, QUARTER:QUARTER + TD], newq[:]).then_inc(placed, 16)
        sp.wait_ge(placed, 16)

    @block.gpsimd
    def _(pool):
        view = io["cache_kidx"][0].rearrange("g (s e) d -> (g s) (e d)", s=8)
        pool.wait_ge(indexed, 1)
        for j in range(N):
            if j >= 4:
                pool.wait_ge(turned, 2 * (j - 3))
            pool.indirect_dma_start(keys[:, j % 4], None, view,
                                    bass.IndirectOffsetOnAxis(ap=index[:, j:j + 1].bitcast(U32), axis=0)
                                    ).then_inc(g_landed[j % 4], 16)

    @block.tensor
    def _(pe):
        pe.wait_ge(small_landed, 64)
        for h in range(H):
            m = pe.transpose(ps[:, 7, h * NS:(h + 1) * NS], iq2[:, h].rearrange("p a d -> p (a d)"), k.ident[0:NS, 0:NS])
        m.then_inc(iq_turned, 1)
        pe.wait_ge(blocks_made, 1)
        pe.matmul(ps[0:NS, 6, 0:NS * H].rearrange("p (b q) -> p b q", b=BD), k.ikT[0:DH, SEQ:R],
                  bd[0:DH, :, 0].rearrange("p b t h -> p b (t h)"), start=True, stop=True).then_inc(new_scored, 1)

        def turn(j):
            pe.wait_ge(g_landed[j % 4], 16 * (j // 4 + 1))
            for a in range(2):
                if j:
                    pe.wait_ge(copied, 2 * j + a - 1)
                for e in range(4):
                    x = 2 * (4 * a + e) * DH
                    m = pe.transpose(ps[:, a, e * P:(e + 1) * P], keys[:, j % 4, x:x + 2 * DH], k.ident[:])
                m.then_inc(turned, 1)

        def multiply(j):
            if j >= 2:
                pe.wait_ge(weighted, j - 1)
            pe.wait_ge(copied, 2 * j + 2)
            for e in range(8):
                m = pe.matmul(ps[:, 2 + j % 2, e * 64:(e + 1) * 64], keysT[:, j % 2, e, :],
                              bd[:, j // 4].rearrange("p a t h -> p (a t h)"), start=True, stop=True)
            m.then_inc(multiplied, 1)

        for j in range(N + 1):
            if j < N:
                turn(j)
            if j:
                multiply(j - 1)
        pe.wait_ge(new_summed, 1)
        pe.transpose(ps[0:NS, 7, 0:NS], news[:], k.ident[0:NS, 0:NS]).then_inc(new_turned, 1)
        pe.wait_ge(reduced, 1)
        for e in range(E16):
            if e % 4 == 0 and e >= 8:
                pe.wait_ge(sc_copied, e // 4 - 1)
            m = pe.transpose(ps[:, 4 + (e // 4) % 2, (e % 4) * P:(e % 4 + 1) * P], sc[:, e].rearrange("p a q -> p (a q)"), k.ident[:])
            if e % 4 == 3:
                m.then_inc(sc_turned, 1)

    @block.scalar
    def _(act):
        for j in range(N):
            for a in range(2):
                act.wait_ge(turned, 2 * j + a + 1)
                if j >= 2 and a == 0:
                    act.wait_ge(multiplied, j - 1)
                act.copy(keysT[:, j % 2, 4 * a:4 * a + 4, :], ps[:, a, :].rearrange("p (e n) -> p e n", n=P)).then_inc(copied, 1)

    @block.vector
    def _(dve):
        dve.wait_ge(pt_landed, 128)
        dve.tensor_scalar(index[:], pages[:], 8.0, k.part[:, 0:1], ALU.mult, ALU.add).then_inc(indexed, 1)
        dve.memset(bd[:], 0.0)
        dve.memset(k.found[:, QUARTER:QUARTER + TD], UNSEEN)
        dve.drain()
        dve.memset(newp[0:1, 0:1], 0.0).then_inc(zeroed, 1)
        dve.wait_ge(iq_turned, 1)
        for a in range(2):
            rows = slice(a * DH, (a + 1) * DH)
            src = ps[rows, 7, 0:H * NS].rearrange("p (h b t) -> p h b t", h=H, b=BD)
            for t in range(TD):
                x = dve.tensor_copy(bd[rows, :, a, t, :], src[:, :, :, t].rearrange("p h b -> p b h"))
        dve.drain()
        dve.memset(newp[0:1, 0:1], 0.0).then_inc(blocks_made, 1)
        dve.wait_ge(new_scored, 1)
        dve.wait_ge(small_landed, 64)
        dve.drain()
        dve.scalar_tensor_tensor(newp[:], ps[0:NS, 6, 0:NS * H], 0.0, wb[0:NS].rearrange("p q h -> p (q h)"), ALU.max, ALU.mult)
        dve.drain()
        dve.tensor_reduce(news[:], newp[:].rearrange("p (q h) -> p q h", h=H), AX.X, ALU.add).then_inc(new_summed, 1)
        for j in range(N):
            b, a = j // 4, j % 4
            dve.wait_ge(multiplied, j + 1)
            w = wb[:, b * TD:(b + 1) * TD, :].rearrange("p t h -> p (t h)")
            dve.scalar_tensor_tensor(part[:, j % 2].rearrange("p (e n) -> p e n", n=TD * H),
                                     ps[:, 2 + j % 2, :].rearrange("p (e n) -> p e n", n=TD * H), 0.0,
                                     w[:, None, :].broadcast_to([P, E16, TD * H]), ALU.max, ALU.mult).then_inc(weighted, 1)
            dve.drain()
            dve.tensor_reduce(sc[:, :, a, b * TD:(b + 1) * TD], part[:, j % 2].rearrange("p (e t h) -> p e t h", e=E16, h=H),
                              AX.X, ALU.add)
        dve.drain()
        dve.memset(newp[0:1, 0:1], 0.0).then_inc(reduced, 1)
        dve.wait_ge(new_turned, 1)
        dve.tensor_tensor(newt[:], ps[0:NS, 7, 0:NS], newb[:], ALU.add)
        dve.drain()
        dve.tensor_reduce(newq[:], newt[:].rearrange("p (b s) -> p s b", b=BD), AX.X, ALU.max).then_inc(new_ready, 1)
        for g in range(4):
            dve.wait_ge(sc_turned, g + 1)
            dst = k.found[:, 0:QUARTER].rearrange("p (n e) -> p e n", e=E16)
            dve.tensor_copy(dst[:, 4 * g:4 * g + 4, :], ps[:, 4 + g % 2, :].rearrange("p (e n) -> p e n", n=P)).then_inc(sc_copied, 1)


def select_sample(k, ctx, block, chunks):
    nc, io, ps = k.nc, k.io, k.ps
    F = k.found
    FIRST_NEW = k.n_pool * PAGE
    best = k.sb(ctx, "best", [P, TOPK])
    where = k.sb(ctx, "where", [P, TOPK], U32)
    tabi = k.sb(ctx, "table_i", [P, 16], I32)
    tab = k.sb(ctx, "table", [P, 16])
    pagef = k.sb(ctx, "page_f", [P, TOPK])
    blk = k.sb(ctx, "block_u", [P, TOPK], U32)
    offu = k.sb(ctx, "offset_u", [P, TOPK], U32)
    hit = k.sb(ctx, "hit", [P, TOPK])
    row = k.sb(ctx, "row", [P, 2, 2 * TOPK])
    iota = k.sb(ctx, "iota", [P, TOPK])
    cand = k.sb(ctx, "cand", [NS, 4, TOPK])
    cbest = k.sb(ctx, "cand_best", [NS, 8])
    ceq = k.sb(ctx, "cand_taken", [NS, 4, TOPK])
    span = k.sb(ctx, "span", [NS, 4, 2])
    cnt = k.sb(ctx, "cnt", [NS, 4])
    sp4 = k.sb(ctx, "span_of_part", [P, 2])
    bitsu = k.sb(ctx, "bits_u", [P, 10], I32)
    bits = k.sb(ctx, "bits", [P, 10])
    fold = k.sb(ctx, "fold", [P, NS])
    newc = k.sb(ctx, "new_count", [P, TD])
    newq = k.sb(ctx, "new_by_query", [NS, TD])
    newm = k.sb(ctx, "new_matrix", [NS, BD, TD])
    same = k.sb(ctx, "same_entry", [NS, NS])
    slots = k.sb(ctx, "slots", [P, 2, NS])
    landed, cand_landed, span_landed = k.sems(ctx, "landed", "cand_landed", "span_landed")
    found, counted, placed, folded, new_made, new_turned = k.sems(
        ctx, "found", "counted", "placed", "folded", "new_made", "new_turned")

    @block.sync
    def _(sp):
        pt = io["page_table"].rearrange("b (a i) -> a b i", a=4)
        for a in range(4):
            sp.dma_start(tabi[a * NS:(a + 1) * NS, :],
                         pt[a][:, None, :].broadcast_to([BD, TD, 16])).then_inc(landed, 16)
        sp.dma_start(iota[:], io["c_iota"].broadcast_to([P, TOPK])).then_inc(landed, 16)
        sp.dma_start(fold[:], io["c_fold"]).then_inc(landed, 16)
        sp.dma_start(same[:], io["c_same"]).then_inc(landed, 16)

    def gather_candidates(pool):
        pool.wait_ge(found, 1)
        for a in range(4):
            pool.dma_start(cand[:, a, :], best[a * NS:(a + 1) * NS, :]).then_inc(cand_landed, 16)

    def spread_spans(pool):
        pool.wait_ge(counted, 1)
        for a in range(4):
            pool.dma_start(sp4[a * NS:(a + 1) * NS, :], span[:, a, :]).then_inc(span_landed, 16)

    project_rows(k, ctx, block, chunks, scores=True, moves={22: gather_candidates, 38: spread_spans})

    @block.vector
    def _(dve):
        for i in range(ROUNDS):
            b8 = best[:, 8 * i:8 * i + 8]
            dve.max(b8, F[:])
            dve.drain()
            dve.max_index(where[:, 8 * i:8 * i + 8], b8, F[:])
            dve.drain()
            dve.match_replace(F[:], b8, F[:], TAKEN)
            dve.drain()
        dve.tensor_copy(tab[0:1, 0:1], best[0:1, 0:1]).then_inc(found, 1)
        dve.wait_ge(landed, 112)
        dve.drain()
        dve.tensor_copy(tab[:], tabi[:])
        dve.tensor_scalar(blk[:], where[:], 7, None, ALU.logical_shift_right)
        dve.tensor_scalar(offu[:], where[:], PAGE - 1, None, ALU.bitwise_and)
        dve.memset(row[:], 0.0)
        dve.drain()
        dve.tensor_copy(pagef[:], blk[:])
        dve.drain()
        data = row[:, 0, TOPK:2 * TOPK]
        dve.tensor_scalar(data, pagef[:], 16.0, float(k.n_pool), ALU.is_equal, ALU.mult)
        dve.drain()
        for i in range(16):
            dve.tensor_scalar(hit[:], pagef[:], float(i), tab[:, i:i + 1], ALU.is_equal, ALU.mult)
            dve.drain()
            dve.tensor_tensor(data, data, hit[:], ALU.add)
            dve.drain()
        dve.scalar_tensor_tensor(data, data, float(PAGE), offu[:], ALU.mult, ALU.add)
        dve.wait_ge(cand_landed, 64)
        c = cand[:].rearrange("p a n -> p (a n)")
        with dve.Fori(0, ROUNDS):
            dve.max(cbest[:], c)
            dve.drain()
            dve.match_replace(c, cbest[:], c, TAKEN)
            dve.drain()
        dve.tensor_scalar(ceq[:], cand[:], TAKEN, None, ALU.is_equal)
        dve.drain()
        dve.tensor_reduce(cnt[:], ceq[:], AX.X, ALU.add)
        dve.memset(span[:, 0, 0:1], 0.0)
        dve.drain()
        for a in range(4):
            dve.tensor_tensor(span[:, a, 1:2], span[:, a, 0:1], cnt[:, a:a + 1], ALU.add)
            dve.drain()
            if a < 3:
                dve.tensor_copy(span[:, a + 1, 0:1], span[:, a, 1:2])
                dve.drain()
        dve.tensor_copy(cbest[:, 0:1], cnt[:, 0:1]).then_inc(counted, 1)
        dve.wait_ge(span_landed, 64)
        dve.tensor_copy(bitsu[:, 9:10], sp4[:, 0:1])
        dve.drain()
        for i in range(9):
            dve.tensor_scalar(bitsu[:, i:i + 1], bitsu[:, 9:10], i, 1, ALU.arith_shift_right, ALU.bitwise_and)
        dve.drain()
        dve.tensor_copy(bits[:, 0:9], bitsu[:, 0:9])
        dve.drain()
        for i in range(9):
            x, y = row[:, i % 2], row[:, (i + 1) % 2]
            dve.tensor_tensor(hit[:], x[:, TOPK - (1 << i):2 * TOPK - (1 << i)], x[:, TOPK:2 * TOPK], ALU.subtract)
            dve.drain()
            dve.scalar_tensor_tensor(y[:, TOPK:2 * TOPK], hit[:], bits[:, i:i + 1], x[:, TOPK:2 * TOPK], ALU.mult, ALU.add)
            dve.drain()
        y = row[:, 1, TOPK:2 * TOPK]
        dve.scalar_tensor_tensor(hit[:], iota[:], sp4[:, 0:1], y, ALU.is_ge, ALU.mult)
        dve.drain()
        dve.scalar_tensor_tensor(y, iota[:], sp4[:, 1:2], hit[:], ALU.is_lt, ALU.mult)
        dve.drain()
        for s in range(TD):
            dve.tensor_scalar(hit[:], y, float(FIRST_NEW + s), None, ALU.is_equal)
            dve.drain()
            dve.tensor_reduce(newc[:, s:s + 1], hit[:], AX.X, ALU.add)
            dve.drain()
        dve.tensor_copy(bits[0:1, 9:10], bits[0:1, 8:9]).then_inc(placed, 1)
        dve.wait_ge(folded, 1)
        dve.tensor_copy(slots[:], ps[:, 0, 0:2 * NS].rearrange("p (a q) -> p a q", a=2))
        dve.tensor_copy(newq[:], ps[0:NS, 1, 0:TD])
        dve.drain()
        dve.tensor_scalar(k.slot_bias[:], slots[:], float(FIRST_NEW), MASKED, ALU.is_ge, ALU.mult)
        dve.tensor_scalar(k.slot_row[:], slots[:], float(FIRST_NEW - 1), None, ALU.min)
        dve.tensor_tensor(newm[:], newq[:][:, None, :].broadcast_to([NS, BD, TD]), same[:].rearrange("p (b s) -> p b s", b=BD),
                          ALU.mult).then_inc(new_made, 1)
        dve.wait_ge(new_turned, 1)
        dve.tensor_scalar(k.new_bias[:], ps[0:NS, 1, 0:NS], -1.0, -MASKED, ALU.add, ALU.mult)

    @block.tensor
    def _(pe):
        pe.wait_ge(placed, 1)
        pe.wait_ge(landed, 112)
        pe.wait_ge(*k.banks_taken)
        for a in range(2):
            pe.matmul(ps[:, 0, a * NS:(a + 1) * NS], row[:, 1, TOPK + a * P:TOPK + (a + 1) * P], fold[:], start=True, stop=True)
        pe.matmul(ps[0:NS, 1, 0:TD], fold[:], newc[:], start=True, stop=True).then_inc(folded, 1)
        pe.wait_ge(new_made, 1)
        pe.transpose(ps[0:NS, 1, 0:NS], newm[:].rearrange("p b s -> p (b s)"), k.ident[0:NS, 0:NS]).then_inc(new_turned, 1)



def attend_sample(k, ctx, block):
    nc, io, ps, mixT = k.nc, k.io, k.ps, k.hT
    RING = 12
    scale = DH ** -0.5
    pairs = [(q, a) for q in range(NS) for a in range(2)]
    HALF = NS // 2
    SLOTS = TOPK + NS
    got = k.sb(ctx, "gathered", [P, RING, H * DH])
    qb = k.sb(ctx, "q_everywhere", [P, 2, H * DH])
    prod = k.sb(ctx, "prod", [P, 2, H * DH])
    lg = k.sb(ctx, "slot_logits", [P, 2, NS, H])
    lgn = k.sb(ctx, "new_logits", [NS, NS, H])
    prob = k.sb(ctx, "prob_rows", [P, 2, SLOTS])
    pr = k.sb(ctx, "slot_probs", [P, 2, NS, H])
    prn = k.sb(ctx, "new_probs", [NS, NS, H])
    vnew = k.sb(ctx, "v_new", [NS, H * DH])
    best = k.sb(ctx, "best", [P, 8])
    top = k.sb(ctx, "top", [P, 2, 2])
    total = k.sb(ctx, "total", [P, 2, 2])
    g_landed = k.sem_ring(ctx, "g_landed", RING)
    q_landed = k.sem_ring(ctx, "q_landed", 2)
    (v_landed,) = k.sems(ctx, "v_landed")
    (scored_new, new_read, multiplied, biased, turned, topped, exped, scaled, returned, probs_copied, weighed) = k.sems(
        ctx, "scored_new", "new_read", "multiplied", "biased", "turned", "topped", "exped", "scaled", "returned",
        "probs_copied", "weighed")
    k.banks_taken = (new_read, 1)

    @block.sync
    def _(sp):
        sp.dma_start(vnew[:], io["v_sample"]).then_inc(v_landed, 16)

    def gather(pool, i):
        n, (q, a) = i // len(pairs), pairs[i % len(pairs)]
        before = i - RING
        if before >= len(pairs):
            pool.wait_ge(weighed, (before - len(pairs)) // 2 + 1)
        elif before >= 0:
            pool.wait_ge(multiplied, before + 1)
        view = io[("cache_k", "cache_v")[n]][0].rearrange("g r h d -> (g r) (h d)")
        pool.indirect_dma_start(got[:, i % RING, :], None, view,
                                bass.IndirectOffsetOnAxis(ap=k.slot_row[:, a, q:q + 1], axis=0)
                                ).then_inc(g_landed[i % RING], 16)

    @block.gpsimd
    def _(pool):
        for i, (q, a) in enumerate(pairs):
            if a == 0:
                if q >= 2:
                    pool.wait_ge(multiplied, 2 * (q - 1))
                pool.dma_start(qb[:, q % 2, :], k.scratch["q_s"][q:q + 1, :].broadcast_to([P, H * DH])).then_inc(q_landed[q % 2], 16)
            gather(pool, i)
        for i in range(len(pairs), len(pairs) + RING):
            gather(pool, i)

    @block.vector
    def _(dve):
        dve.wait_ge(scored_new, 1)
        for a in range(2):
            x = dve.tensor_tensor(lgn[:, :, a:H:2], ps[0:NS, 6 + a, 0:NS * H // 2].rearrange("p (f q) -> p q f", q=NS),
                                  k.new_bias[:][:, :, None].broadcast_to([NS, NS, H // 2]), ALU.add)
        x.then_inc(new_read, 1)
        for j, (q, a) in enumerate(pairs):
            dve.wait_ge(g_landed[j % RING], 16 * (j // RING + 1))
            dve.wait_ge(q_landed[q % 2], 16 * (q // 2 + 1))
            dve.tensor_tensor(prod[:, a, :], got[:, j % RING, :], qb[:, q % 2, :], ALU.mult).then_inc(multiplied, 1)
            dve.drain()
            dve.tensor_reduce(lg[:, a, q, :], prod[:, a, :].rearrange("p (h d) -> p h d", h=H), AX.X, ALU.add)
            take_best(k, dve, best, 2 + j // ROUNDS, j % ROUNDS, 1)
        dve.drain()
        dve.tensor_tensor(lg[:], lg[:], k.slot_bias[:][:, :, :, None].broadcast_to([P, 2, NS, H]), ALU.add).then_inc(biased, 1)

    @block.tensor
    def _(pe):
        for h in range(H):
            row = (h % 2) * DH
            m = pe.matmul(ps[0:NS, 6 + h % 2, (h // 2) * NS:(h // 2 + 1) * NS], k.kT[row:row + DH, h // 2, SEQ:R],
                          k.qT[row:row + DH, h // 2, SEQ:R], start=True, stop=True)
        m.then_inc(scored_new, 1)

    def weigh_values(k, ctx, block):
        @block.gpsimd
        def _(pool):
            for i in range(len(pairs) + RING, 2 * len(pairs)):
                gather(pool, i)

        @block.vector
        def _(dve):
            for g in range(2):
                dve.wait_ge(turned, g + 1)
                dve.tensor_reduce(top[:, g, 0:1], ps[:, g, 0:SLOTS], AX.X, ALU.max)
                dve.drain()
                dve.tensor_scalar(top[:, g, 1:2], top[:, g, 0:1], -scale, None, ALU.mult).then_inc(topped, 1)
            for g in range(2):
                dve.wait_ge(exped, g + 1)
                dve.reciprocal(total[:, g, 1:2], total[:, g, 0:1])
                dve.drain()
                dve.tensor_scalar(prob[:, g, :], prob[:, g, :], total[:, g, 1:2], None, ALU.mult).then_inc(scaled, 1)
            for g in range(2):
                dve.wait_ge(returned, g + 1)
                qs = slice(g * HALF, (g + 1) * HALF)
                dve.tensor_copy(pr[:, :, qs, :], ps[:, 2 + g, 0:TOPK].rearrange("p (a q h) -> p a q h", a=2, h=H))
                dve.tensor_copy(prn[:, qs, :], ps[0:NS, 2 + g, TOPK:TOPK + P].rearrange("p (q h) -> p q h", h=H)).then_inc(probs_copied, 1)
            for i in (4, 5):
                take_best(k, dve, best, i, 0, ROUNDS)
            dve.wait_ge(weighed, NS)
            out = ps[:, 4:6, :].rearrange("p b (q f h) -> p (b q) f h", f=4, h=H)
            for a in range(2):
                rows = slice(a * DH, (a + 1) * DH)
                for f in range(4):
                    dve.tensor_copy(mixT[rows, f, SEQ:R], out[rows, :, f, 2 * f + a])

        @block.scalar
        def _(act):
            for g in range(2):
                act.wait_ge(topped, g + 1)
                act.activation(prob[:, g, :], ps[:, g, 0:SLOTS], ACT.Exp, bias=top[:, g, 1:2], scale=scale,
                               accum_out=total[:, g, 0:1])
                act.drain()
                act.copy(top[0:1, g, 0:1], top[0:1, g, 1:2]).then_inc(exped, 1)

        @block.tensor
        def _(pe):
            pe.wait_ge(*k.banks_taken)
            pe.wait_ge(biased, 1)
            for g in range(2):
                qs = slice(g * HALF, (g + 1) * HALF)
                for a in range(2):
                    pe.transpose(ps[:, g, a * P:(a + 1) * P], lg[:, a, qs, :].rearrange("p q h -> p (q h)"), k.ident[:])
                pe.transpose(ps[:, g, TOPK:SLOTS], lgn[:, qs, :].rearrange("p q h -> p (q h)"), k.ident[0:NS, 0:NS]).then_inc(turned, 1)
            for g in range(2):
                pe.wait_ge(scaled, g + 1)
                for a in range(2):
                    pe.transpose(ps[:, 2 + g, a * P:(a + 1) * P], prob[:, g, a * P:(a + 1) * P], k.ident[:])
                pe.transpose(ps[0:NS, 2 + g, TOPK:TOPK + P], prob[:, g, TOPK:SLOTS], k.ident[:]).then_inc(returned, 1)
            pe.wait_ge(probs_copied, 2)
            pe.wait_ge(v_landed, 16)
            for q in range(NS):
                i = len(pairs) + 2 * q
                for x in (i, i + 1):
                    pe.wait_ge(g_landed[x % RING], 16 * (x // RING + 1))
                for f in range(4):
                    at = (q % HALF) * 4 * H + f * H
                    o = ps[:, 4 + q // HALF, at:at + H]
                    fs = slice(f * P, (f + 1) * P)
                    for a in range(2):
                        pe.matmul(o, got[:, (i + a) % RING, fs], pr[:, a, q, :], start=a == 0, stop=False)
                    m = pe.matmul(o, vnew[:, fs], prn[:, q, :], start=False, stop=True)
                m.then_inc(weighed, 1)

    return weigh_values



def project_out(k, ctx, block):
    nc, ps = k.nc, k.ps
    w_out = k.io["w_out"][0].rearrange("(k p) n -> p k n", p=P)
    w = k.sb(ctx, "w_out_tile", [P, 2, KD, P])
    landed = k.sem_ring(ctx, "landed", 2)
    multiplied, banks_free = k.sems(ctx, "multiplied", "banks_free")

    @block.sync
    def _(sp):
        for s in range(2):
            sp.dma_start(w[:, s], w_out[:, :, s * P:(s + 1) * P]).then_inc(landed[s], 16)
        with sp.Fori(0, KD // 2 - 1) as t:
            for s in range(2):
                sp.wait_ge(multiplied, 2 * t + s + 1)
                sp.dma_start(w[:, s], w_out[:, :, bass.ds((2 * t + 2 + s) * P, P)]).then_inc(landed[s], 16)

    @block.tensor
    def _(pe):
        with pe.Fori(0, KD // 2) as t:
            for s in range(2):
                pe.wait_ge(landed[s], 16 * t + 16)
                pe.wait_ge(banks_free, 2 * t + s + 1)
                for d in range(KD):
                    for g in range(G):
                        m = pe.matmul(ps[:, 4 * s + g, 0:GC], w[:, s, d, :], k.hT[:, d, g * GC:(g + 1) * GC],
                                      start=d == 0, stop=d == KD - 1)
                m.then_inc(multiplied, 1)

    @block.vector
    def _(dve):
        dve.sem_inc(banks_free, 2)
        with dve.Fori(0, KD // 2) as t:
            for s in range(2):
                dve.wait_ge(multiplied, 2 * t + s + 1)
                x = grouped(k.xT[:, 2 * t + s, :])
                dve.tensor_tensor(x, x, bank_cols(ps, 4 * s), ALU.add).then_inc(banks_free, 1)


def ffn(k, ctx, block, layer):
    nc, ps = k.nc, k.ps
    h = k.sb(ctx, "h_split", [P, 2, KD, R], F32R)
    w_up = k.io["w_up"][layer].rearrange("(k p) n -> p k n", p=P)
    w_down = k.io["w_down"][layer].rearrange("(k p) n -> p k n", p=P)
    PARTS = KF // 2
    W = 2 * P * KD
    BLOCKS = 3 * PARTS
    raw = k.sb(ctx, "w_raw", [P, 2, W])
    ws = k.sb(ctx, "w_split", [P, 2, 2, W], F32R)
    hidden = k.sb(ctx, "hidden", [P, 2, 2, 2, R], F32R)
    silu = k.sb(ctx, "silu", [P, 2, R])
    exact = k.sb(ctx, "hidden_exact", [P, R])
    landed = k.sem_ring(ctx, "w_landed", 2)
    high_made, split_ready, gate_done, silu_done, up_done, hidden_ready, down_done, drained = k.sems(
        ctx, "w_high_made", "w_split_ready", "gate_done", "silu_done", "up_done", "hidden_ready",
        "down_done", "drained")
    norm = SplitNorm(k, ctx, h, k.ffn_w[layer], square=silu, total=exact[:])

    @block.sync
    def _(sp):
        def load(j, slot, src, wait=True):
            if wait:
                sp.wait_ge(split_ready, j - 1)
            sp.dma_start(raw[:, slot].rearrange("p (k n) -> p k n", k=src.shape[1]), src).then_inc(landed[slot], 16)

        def gate(p):
            return w_up[:, :, bass.ds(p * 2 * P, 2 * P)]

        def up(p):
            return w_up[:, :, bass.ds(p * 2 * P + FF, 2 * P)]

        def down(p):
            return w_down[:, bass.ds(2 * p, 2), :]

        load(0, 0, gate(0), False)
        load(1, 1, up(0), False)
        with sp.Fori(0, (PARTS - 1) // 2) as t:
            for e in range(2):
                for m, src in enumerate((gate(2 * t + e + 1), up(2 * t + e + 1), down(2 * t + e))):
                    load(6 * t + 2 + 3 * e + m, (3 * e + m) % 2, src)
        load(BLOCKS - 1, (BLOCKS - 1) % 2, down(PARTS - 1))

    @block.tensor
    def _(pe):
        norm.tensor(pe)

        def three(out, w_at, rhs, first, last, g):
            for i, (a, b) in enumerate(((0, 0), (0, 1), (1, 0))):
                m = pe.matmul(out, w_at[a], rhs[b][:, g * GC:(g + 1) * GC], start=first and i == 0, stop=last and i == 2)
            return m

        def up_products(j, slot, p, q, normed=False):
            gates = q is None or q[0] == "g"
            pe.wait_ge(split_ready, j + 1)
            for i in range(2):
                if gates:
                    if q is not None:
                        pe.wait_ge(drained, q[1] - 1 + i)
                else:
                    pe.wait_ge(silu_done, 2 * p + 1 + i)
                for d in range(KD):
                    if normed and i == 0:
                        pe.wait_ge(norm.normed, d + 1)
                    at = d * 2 * P + i * P
                    w_at = [ws[:, slot, a, at:at + P] for a in range(2)]
                    for g in range(G):
                        m = three(ps[:, 3 * i + g, 0:GC], w_at, [h[:, a, d, :] for a in range(2)], d == 0, d == KD - 1, g)
                m.then_inc(gate_done if gates else up_done, 1)

        def down_products(j, slot, p, parity, before):
            pe.wait_ge(split_ready, j + 1)
            pe.wait_ge(hidden_ready, 2 * p + 2)
            for d in range(KD):
                pe.wait_ge(drained, before + 1 + d)
                for i in range(2):
                    at = i * D + d * P
                    w_at = [ws[:, slot, a, at:at + P] for a in range(2)]
                    for g in range(G):
                        m = three(ps[:, 3 * (d % 2) + g, 0:GC], w_at, [hidden[:, parity, i, a, :] for a in range(2)],
                                  i == 0, i == 1, g)
                m.then_inc(down_done, 1)

        up_products(0, 0, 0, None, normed=True)
        up_products(1, 1, 0, ("u", 0))
        with pe.Fori(0, (PARTS - 1) // 2) as t:
            for e in range(2):
                p, j, before = 2 * t + e, 6 * t + 2 + 3 * e, 2 + 10 * (2 * t + e)
                up_products(j, (3 * e) % 2, p + 1, ("g", before))
                up_products(j + 1, (3 * e + 1) % 2, p + 1, ("u", before))
                down_products(j + 2, (3 * e + 2) % 2, p, e, before)
        down_products(BLOCKS - 1, (BLOCKS - 1) % 2, PARTS - 1, 0, 10 * (PARTS - 1))

    @block.scalar
    def _(act):
        def high(slot, count, done=None, products=0):
            act.wait_ge(landed[slot], 16 * count)
            if done is not None:
                act.wait_ge(done, products)
            act.copy(ws[:, slot, 0], raw[:, slot]).then_inc(high_made, 1)

        def silus(p, wait=True):
            for i in range(2):
                act.wait_ge(gate_done, 2 * p + 1 + i)
                if wait:
                    act.wait_ge(hidden_ready, 2 * p - 1 + i)
                act.activation(grouped(silu[:, i]), bank_cols(ps, 3 * i), ACT.Silu).then_inc(silu_done, 1)

        def steps(t, first=False):
            for e in range(2):
                q = 2 * t + e
                n = 3 * e + 3
                if first and e == 0:
                    high(n % 2, 3 * t + n // 2 + 1, up_done, 2)
                else:
                    high(n % 2, 3 * t + n // 2 + 1, down_done, KD * q)
                silus(q + 1)
                high((n + 1) % 2, 3 * t + (n + 1) // 2 + 1, gate_done, 2 * q + 4)
                high((n + 2) % 2, 3 * t + (n + 2) // 2 + 1, up_done, 2 * q + 4)

        norm.scalar(act)
        for s in range(2):
            high(s, 1)
        norm.round(act)
        silus(0, False)
        high(0, 2, gate_done, 2)
        steps(0, first=True)
        with act.Fori(1, (PARTS - 1) // 2) as t:
            steps(t)

    @block.gpsimd
    def _(pool):
        def low(j, slot):
            pool.wait_ge(high_made, j + 1)
            pool.tensor_tensor(ws[:, slot, 1], raw[:, slot], ws[:, slot, 0].bitcast(F32), ALU.subtract).then_inc(split_ready, 1)

        for j in range(2):
            low(j, j)
        norm.pool(pool)
        with pool.Fori(1, BLOCKS // 2) as t:
            for s in range(2):
                low(2 * t + s, s)
        low(BLOCKS - 1, (BLOCKS - 1) % 2)

    @block.vector
    def _(dve):
        norm.vector(dve)
        dve.drain()

        def hiddens(p, parity):
            for i in range(2):
                dve.wait_ge(silu_done, 2 * p + 1 + i)
                dve.wait_ge(up_done, 2 * p + 1 + i)
                dve.tensor_tensor(grouped(exact[:]), grouped(silu[:, i]), bank_cols(ps, 3 * i), ALU.mult).then_inc(drained, 1)
                dve.drain()
                dve.tensor_copy(hidden[:, parity, i, 0, :], exact[:])
                dve.drain()
                dve.tensor_tensor(hidden[:, parity, i, 1, :], exact[:], hidden[:, parity, i, 0, :].bitcast(F32),
                                  ALU.subtract).then_inc(hidden_ready, 1)
                dve.drain()

        def adds(p):
            for d in range(KD):
                dve.wait_ge(down_done, KD * p + d + 1)
                x = grouped(k.xT[:, d, :])
                dve.tensor_tensor(x, x, bank_cols(ps, 3 * (d % 2)), ALU.add).then_inc(drained, 1)

        hiddens(0, 0)
        with dve.Fori(0, (PARTS - 1) // 2) as t:
            for e in range(2):
                hiddens(2 * t + e + 1, 1 - e)
                adds(2 * t + e)
        adds(PARTS - 1)


def layer_embedding(k, ctx, block, layer):
    nc, io, ps = k.nc, k.io, k.ps
    hT = k.sb(ctx, "h_ple", [P, KD, R])
    wg = io["w_ple_gate"][layer].rearrange("(k p) n -> p k n", p=P)
    wp = io["w_ple"][layer].rearrange("(k p) n -> p k n", p=P)
    KP = PLE // P
    rows = k.sb(ctx, "p_rows", [P, NT + 1, PLE])
    pT = k.sb(ctx, "pT", [P, KP, R])
    w = k.sb(ctx, "w_ple_tile", [P, 2, KD + KP, P])
    gate = k.sb(ctx, "gate", [P, R])
    term = k.sb(ctx, "term", [P, R])
    landed = k.sem_ring(ctx, "w_landed", 2)
    (p_landed,) = k.sems(ctx, "p_landed")
    turned, copied, gate_done, ple_done, gated, added = k.sems(
        ctx, "turned", "copied", "gate_done", "ple_done", "gated", "added")
    norm = Norm(k, ctx, hT, k.ple_w[layer])

    @block.sync
    def _(sp):
        sp.dma_start(rows[:, 0:NT, :], io["p_prompt"][layer, 0].rearrange("(r p) n -> p r n", p=P)).then_inc(p_landed, 16)
        sp.dma_start(rows[0:NS, NT, :], io["p_sample"][layer].rearrange("b t n -> (b t) n")).then_inc(p_landed, 16)

        def load(s, n):
            sp.dma_start(w[:, s, 0:KD, :], wg[:, :, bass.ds(n * P, P)]).then_inc(landed[s], 16)
            sp.dma_start(w[:, s, KD:KD + KP, :], wp[:, :, bass.ds(n * P, P)]).then_inc(landed[s], 16)

        for s in range(2):
            load(s, s)
        with sp.Fori(0, KD // 2 - 1) as t:
            for s in range(2):
                sp.wait_ge(ple_done, 2 * t + s + 1)
                load(s, 2 * t + 2 + s)

    @block.tensor
    def _(pe):
        pe.wait_ge(p_landed, 32)
        for r in range(NT + 1):
            n = rows_of(r)
            if r >= 2:
                pe.wait_ge(copied, r - 1)
            for i in range(KP):
                m = pe.transpose(ps[:, 6 + r % 2, i * P:i * P + n], rows[0:n, r, i * P:(i + 1) * P], k.ident[0:n, 0:n])
            m.then_inc(turned, 1)
        norm.tensor(pe)
        pe.wait_ge(copied, NT + 1)
        pe.wait_ge(norm.normed, KD)
        with pe.Fori(0, KD // 2) as t:
            for s in range(2):
                pe.wait_ge(landed[s], 32 * t + 32)
                pe.wait_ge(gated, 2 * t + s)
                for d in range(KD):
                    for g in range(G):
                        m = pe.matmul(ps[:, g, 0:GC], w[:, s, d, :], hT[:, d, g * GC:(g + 1) * GC],
                                      start=d == 0, stop=d == KD - 1)
                m.then_inc(gate_done, 1)
                pe.wait_ge(added, 2 * t + s)
                for i in range(KP):
                    for g in range(G):
                        m = pe.matmul(ps[:, 4 + g, 0:GC], w[:, s, KD + i, :], pT[:, i, g * GC:(g + 1) * GC],
                                      start=i == 0, stop=i == KP - 1)
                m.then_inc(ple_done, 1)

    @block.scalar
    def _(act):
        for r in range(NT + 1):
            n = rows_of(r)
            act.wait_ge(turned, r + 1)
            act.copy(pT[:, :, r * P:r * P + n], ps[:, 6 + r % 2, 0:PLE].rearrange("p (i n) -> p i n", n=P)[:, :, 0:n]).then_inc(copied, 1)
        norm.scalar(act)
        with act.Fori(0, KD) as n:
            act.wait_ge(gate_done, n + 1)
            act.wait_ge(added, n)
            act.activation(grouped(gate[:]), bank_cols(ps, 0), ACT.Sigmoid).then_inc(gated, 1)

    @block.vector
    def _(dve):
        norm.vector(dve)
        dve.drain()
        with dve.Fori(0, KD) as n:
            dve.wait_ge(gated, n + 1)
            dve.wait_ge(ple_done, n + 1)
            dve.tensor_tensor(grouped(term[:]), grouped(gate[:]), bank_cols(ps, 4), ALU.mult)
            dve.drain()
            x = k.xT[:, n, :]
            dve.tensor_tensor(x, x, term[:], ALU.add).then_inc(added, 1)
            dve.drain()



def pool_mix(k, ctx, block):
    nc, io, ps = k.nc, k.io, k.ps
    hT = k.sb(ctx, "h_pool", [P, KD, R])
    SEG = POOL_BUF + TD
    HEAD = POOL_BUF + SEQ
    LEN = HEAD + BD * SEG
    BUF = BD * POOL_BUF
    OUT = POOL_BUF + NS
    z = k.sb(ctx, "z", [P, KD, R])
    ext = k.sb(ctx, "ext", [P, 2, LEN])
    sums = k.sb(ctx, "sums", [P, 2, LEN])
    inv = k.sb(ctx, "inv_count", [P, len(WINDOWS), 16])
    w = k.sb(ctx, "pool_w", [P, len(WINDOWS), 2, 2 * P])
    buf = k.sb(ctx, "buf_rows", [BUF, D])
    bufT = k.sb(ctx, "bufT", [P, KD, BUF])
    last = k.sb(ctx, "last_rows", [OUT, D])
    fix = k.sb(ctx, "first_means", [P, 16])
    w_landed, buf_landed, out_stored = k.sems(ctx, "w_landed", "buf_landed", "out_stored")
    turned, copied, last_turned, last_copied, z_made, multiplied, added = k.sems(
        ctx, "turned", "copied", "last_turned", "last_copied", "z_made", "multiplied", "added")
    norm = Norm(k, ctx, hT, k.mix_w[1], square=z[:, 0:2, :], total=z[:, 2, :])

    @block.sync
    def _(sp):
        sp.dma_start(buf[:], io["state_pool"][0].rearrange("b r n -> (b r) n")).then_inc(buf_landed, 16)
        sp.dma_start(w[:], io["pool_w"][0].rearrange("g (k p) n -> p g k n", p=P)).then_inc(w_landed, 16)
        sp.dma_start(inv[:].rearrange("p w n -> p (w n)"), io["c_invcnt"].broadcast_to([P, 16 * len(WINDOWS)])).then_inc(w_landed, 16)
        sp.dma_start(io["pool_sample"][0][:, 0:POOL_BUF - TD, :], io["state_pool"][0][:, TD:POOL_BUF, :]).then_inc(out_stored, 16)
        sp.wait_ge(last_copied, 1)
        sp.dma_start(io["pool_prompt"][0, 0], last[0:POOL_BUF, :]).then_inc(out_stored, 16)
        for b in range(BD):
            at = POOL_BUF + b * TD
            sp.dma_start(io["pool_sample"][0, b, POOL_BUF - TD:POOL_BUF, :], last[at:at + TD, :]).then_inc(out_stored, 16)
        sp.wait_ge(out_stored, 16 * (BD + 2))

    @block.tensor
    def _(pe):
        pe.wait_ge(buf_landed, 16)
        for d in range(KD):
            m = pe.transpose(ps[:, 4 + d // 4, (d % 4) * P:(d % 4) * P + BUF], buf[:, d * P:(d + 1) * P], k.ident[0:BUF, 0:BUF])
        m.then_inc(turned, 1)
        norm.tensor(pe)
        pe.wait_ge(norm.normed, KD)
        for d in range(KD):
            m = pe.transpose(ps[0:OUT, 6 + d // 4, (d % 4) * P:(d % 4 + 1) * P], hT[:, d, R - OUT:R], k.ident[:])
        m.then_inc(last_turned, 1)
        pe.wait_ge(w_landed, 32)
        pe.wait_ge(copied, 1)
        for d in range(KD):
            b = 3 * (d % 2)
            pe.wait_ge(z_made, 2 * (d // 2 + 1))
            if d >= 2:
                pe.wait_ge(added, d - 1)
            for i in range(2):
                for g in range(G):
                    m = pe.matmul(ps[:, b + g, 0:GC], w[:, d // 2, i, (d % 2) * P:(d % 2 + 1) * P],
                                  z[:, 2 * (d // 2) + i, g * GC:(g + 1) * GC], start=i == 0, stop=i == 1)
            m.then_inc(multiplied, 1)

    @block.scalar
    def _(act):
        act.wait_ge(turned, 1)
        act.copy(bufT[:], ps[:, 4:6, :].rearrange("p b (d n) -> p (b d) n", n=P)[:, :, 0:BUF]).then_inc(copied, 1)
        norm.scalar(act)
        act.wait_ge(last_turned, 1)
        act.copy(last[:].rearrange("p (b n) -> p b n", b=2), ps[0:OUT, 6:8, :]).then_inc(last_copied, 1)

    @block.vector
    def _(dve):
        norm.vector(dve)
        dve.memset(ext[:, :, 0:POOL_BUF], 0.0)
        dve.memset(sums[:], 0.0)
        dve.wait_ge(copied, 1)
        dve.wait_ge(w_landed, 32)
        dve.drain()
        for d in range(KD):
            e = ext[:, d % 2, :]
            wi = d // 2
            seg = e[:, HEAD:LEN].rearrange("p (b r) -> p b r", r=SEG)
            dve.tensor_copy(e[:, POOL_BUF:HEAD], hT[:, d, 0:SEQ])
            dve.tensor_copy(seg[:, :, 0:POOL_BUF], bufT[:, d, :].rearrange("p (b r) -> p b r", r=POOL_BUF))
            dve.tensor_copy(seg[:, :, POOL_BUF:SEG], hT[:, d, SEQ:R].rearrange("p (b t) -> p b t", t=TD))
            dve.drain()
            src, reach = e, 1
            for n in range(wi + 1):
                dst = sums[:, n % 2, :]
                dve.tensor_tensor(dst[:, reach:LEN], src[:, reach:LEN], src[:, 0:LEN - reach], ALU.add)
                dve.drain()
                src, reach = dst, 2 * reach
            zp, zs = z[:, d, 0:SEQ], z[:, d, SEQ:R].rearrange("p (b t) -> p b t", t=TD)
            dve.scalar_tensor_tensor(zp, src[:, POOL_BUF:HEAD], 1.0 / reach, e[:, POOL_BUF:HEAD], ALU.mult, ALU.subtract)
            sseg = src[:, HEAD:LEN].rearrange("p (b r) -> p b r", r=SEG)
            dve.scalar_tensor_tensor(zs, sseg[:, :, POOL_BUF:SEG], 1.0 / reach, seg[:, :, POOL_BUF:SEG], ALU.mult, ALU.subtract)
            dve.tensor_tensor(fix[:], src[:, POOL_BUF:POOL_BUF + 16], inv[:, wi, :], ALU.mult)
            dve.drain()
            dve.tensor_tensor(zp[:, 0:16], fix[:], e[:, POOL_BUF:POOL_BUF + 16], ALU.subtract).then_inc(z_made, 1)
            dve.drain()
        for d in range(KD):
            dve.wait_ge(multiplied, d + 1)
            x = grouped(k.xT[:, d, :])
            dve.scalar_tensor_tensor(x, bank_cols(ps, 3 * (d % 2)), k.pool_s[:, d:d + 1], x, ALU.mult, ALU.add).then_inc(added, 1)



def finish(k, ctx, block):
    nc, io, ps = k.nc, k.io, k.ps
    hT = k.sb(ctx, "h_out", [P, KD, R])
    rows = k.sb(ctx, "y_rows", [P, 3, D])
    stored = k.sem_ring(ctx, "y_stored", 3)
    turned, copied = k.sems(ctx, "turned", "copied")
    norm = Norm(k, ctx, hT, k.final_w)

    @block.tensor
    def _(pe):
        norm.tensor(pe)
        pe.wait_ge(norm.normed, KD)
        for r in range(NT + 1):
            n, b = rows_of(r), 2 * (r % 2)
            if r >= 2:
                pe.wait_ge(copied, r - 1)
            for d in range(KD):
                m = pe.transpose(ps[0:n, b + d // 4, (d % 4) * P:(d % 4 + 1) * P], hT[:, d, r * P:r * P + n], k.ident[:])
            m.then_inc(turned, 1)

    @block.scalar
    def _(act):
        norm.scalar(act)
        for r in range(NT + 1):
            n, b = rows_of(r), 2 * (r % 2)
            act.wait_ge(turned, r + 1)
            if r >= 3:
                act.wait_ge(stored[r % 3], 16 * (r // 3))
            act.copy(rows[0:n, r % 3, :].rearrange("p (b n) -> p b n", b=2), ps[0:n, b:b + 2, :]).then_inc(copied, 1)

    block.vector(norm.vector)

    @block.sync
    def _(sp):
        for r in range(NT + 1):
            n = rows_of(r)
            sp.wait_ge(copied, r + 1)
            dst = io["y_prompt"][0, r * P:(r + 1) * P, :] if r < NT else io["y_sample"].rearrange("b t d -> (b t) d")
            sp.dma_start(dst, rows[0:n, r % 3, :]).then_inc(stored[r % 3], 16)
        for s in range(3):
            sp.wait_ge(stored[s], 16 * ((NT + 1 - s + 2) // 3))



def build(nc, io):
    scratch = {}
    for name, shape in dict(q_s=(NS, 512), iq_s=(NS, 512), iw_s=(NS, H), bi=(R, 512), bg=(R, 512),
                            gq=(BH, P, R), gk=(BH, P, R), gb=(BH, P, R)).items():
        scratch[name] = nc.dram_tensor(f"scratch_{name}", shape, F32, kind="Internal").ap()
    k = Program(nc, io, scratch)
    k.n_pool = io["cache_kidx"].shape[1]
    io["k_prompt"] = io["k_prompt"].rearrange("l b t h d -> (l b t) (h d)")
    io["v_prompt"] = io["v_prompt"].rearrange("l b t h d -> (l b t) (h d)")
    io["kidx_prompt"] = io["kidx_prompt"].rearrange("l b t d -> (l b t) d")
    io["k_sample"] = io["k_sample"].rearrange("l b t h d -> (l b t) (h d)")
    io["v_sample"] = io["v_sample"].rearrange("l b t h d -> (l b t) (h d)")
    io["kidx_sample"] = io["kidx_sample"].rearrange("l b t d -> (l b t) d")
    with k.keep:
        k.ps = k.keep.enter_context(nc.psum_tensor("ps", [P, 8, 512], F32))
        k.xT = k.sb(k.keep, "xT", [P, KD, R])
        k.ident = k.sb(k.keep, "ident", [P, P])
        k.ones = k.sb(k.keep, "ones", [P, P])
        k.eps = k.sb(k.keep, "eps", [P, 1])
        k.vec = k.sb(k.keep, "vec", [P, 9 * KD])
        k.stage((load_constants,))
        k.stage((load_x,))
        with ExitStack() as mixer:
            k.hT = k.sb(mixer, "hT", [P, KD, R])
            with ExitStack() as mix:
                k.qT, k.kT = (k.sb(mix, n, [P, 4, R]) for n in ("qT", "kT"))
                k.slot_row = k.sb(mix, "slot_row", [P, 2, NS], U32)
                k.slot_bias = k.sb(mix, "slot_bias", [P, 2, NS])
                k.new_bias = k.sb(mix, "new_bias_t", [NS, NS])
                with ExitStack() as index:
                    k.iqT = k.sb(index, "iqT", [P, 4, R])
                    k.ikT = k.sb(index, "ikT", [P, R])
                    k.iw = k.sb(index, "iw", [P, NT + 1, H])
                    k.lb = k.sb(index, "lb", [P, 2, BH])
                    with ExitStack() as proj:
                        k.rope = k.sb(proj, "rope", [P, NT + 1, 2 * DH])
                        k.part = k.sb(proj, "part_const", [P, 2])
                        k.stage((norm_into_features,), (lower_bound,))
                        k.stage((project_rows, ["iq", "ik"]))
                        k.found = k.sb(proj, "found", [P, QUARTER + TD])
                        k.stage((score_sample,))
                        k.stage((select_sample, ["aq", "ak", "av", "bi", "bg"]))
                    k.stage((attend_sample,), (project_gates,))
                    k.stage((attend_prompt,))
            k.stage((recurrence,))
            k.stage((project_out,))
        k.stage((ffn, 0))
        k.stage((layer_embedding, 0))
        k.stage((pool_mix,))
        k.stage((ffn, 1))
        k.stage((layer_embedding, 1))
        k.stage((finish,))


def norm_into_features(k, ctx, block):
    (landed,) = k.sems(ctx, "landed")
    norm = Norm(k, ctx, k.hT, k.mix_w[0])

    @block.sync
    def _(sp):
        table = k.io["c_rope"].rearrange("t a d -> t (a d)")
        sp.dma_start(k.rope[:, 0:NT, :], table[0:SEQ].rearrange("(r p) n -> p r n", p=P)).then_inc(landed, 16)
        sp.dma_start(k.rope[0:NS, NT, :], table[SEQ:R]).then_inc(landed, 16)
        sp.dma_start(k.part[:], k.io["c_part"]).then_inc(landed, 16)
        sp.wait_ge(landed, 48)

    block.scalar(norm.scalar)
    block.tensor(norm.tensor)
    block.vector(norm.vector)



_OUTS = dict(
    y_prompt=(1, SEQ, D), y_sample=(BD, TD, D),
    k_prompt=(1, 1, SEQ, H, DH), v_prompt=(1, 1, SEQ, H, DH), kidx_prompt=(1, 1, SEQ, DH),
    glr_prompt=(1, 1, BH, BK, BK), pool_prompt=(1, 1, POOL_BUF, D),
    k_sample=(1, BD, TD, H, DH), v_sample=(1, BD, TD, H, DH), kidx_sample=(1, BD, TD, DH),
    glr_sample=(1, BD, BH, BK, BK), pool_sample=(1, BD, POOL_BUF, D),
)


def kernel(**inputs):
    import concourse.bacc as _bacc
    from concourse.bass_utils import run_bass_kernel_spmd as _run

    nc = _bacc.Bacc("TRN2", target_bir_lowering=False, num_devices=1)
    arrays, io = {}, {}
    for name, a in {**inputs, **constants()}.items():
        a = np.ascontiguousarray(a)
        arrays[f"in_{name}"] = a
        io[name] = nc.dram_tensor(f"in_{name}", a.shape, mybir.dt.from_np(a.dtype), kind="ExternalInput").ap()
    for name, shape in _OUTS.items():
        io[name] = nc.dram_tensor(f"out_{name}", shape, F32, kind="ExternalOutput").ap()
    build(nc, io)
    r = _run(nc, [arrays], core_ids=[0])
    return tuple(r.results[0][f"out_{name}"] for name in _OUTS)
```

```python
from contextlib import ExitStack
import math

import numpy as np

import concourse.bass as bass
from concourse import mybir

F32, F32R, I32, U32 = mybir.dt.float32, mybir.dt.float32r, mybir.dt.int32, mybir.dt.uint32
ALU, ACT, AX = mybir.AluOpType, mybir.ActivationFunctionType, mybir.AxisListType

P = 128
D = 1024
SEQ = 1024
BD, TD = 8, 4
NS = BD * TD
R = SEQ + NS
PAGE, NPAGES = 128, 64
PAST = PAGE * NPAGES
H, DH = 8, 64
TOPK = 256
BH, BK = 4, 128
FF = 2816
PLE = 256
POOL_BUF = 15
WINDOWS = (2, 4, 8, 16)
EPS = 1e-6

KD = D // P
KF = FF // P
NT = SEQ // P
G, GC = 3, R // 3
COL = dict(aq=0, ak=512, av=1024, iq=1536, ik=2048, bq=2120, bf=2632, bi=3144, bg=3656)
IK_COLS = DH + H
QUARTER = PAST // 4
ROUNDS = TOPK // 8
MASKED = -1e30
UNSEEN = -3.0e38
TAKEN = -3.39e38
LEVELS = int(math.log2(P))


def rows_of(r):
    return P if r < NT else NS


def constants():
    half = DH // 2
    inv = (10000.0 ** (-np.arange(half) / half)).astype(np.float32)
    pos = np.concatenate([np.arange(SEQ), np.tile(PAST + np.arange(TD), BD)]).astype(np.float32)
    ang = pos[:, None] * inv[None, :]
    c, s = np.cos(ang), np.sin(ang)
    rope = np.stack([np.concatenate([c, c], 1), np.concatenate([-s, s], 1)], 1).astype(np.float32)
    a, b = np.arange(P)[:, None], np.arange(P)[None, :]
    level = [((a // (2 * w)) == (b // (2 * w))) & (a % (2 * w) < w) & (b % (2 * w) >= w)
             for w in (1 << n for n in range(LEVELS))] + [a == b]
    t = np.arange(R)
    reset = np.where(t < SEQ, t % P != 0, (t - SEQ) % TD != 0)
    q, n = np.arange(NS)[:, None], np.arange(NS)[None, :]
    same = q // TD == n // TD
    w = np.array(WINDOWS)[:, None]
    return dict(
        c_ident=np.eye(P, dtype=np.float32),
        c_rope=rope,
        c_level=np.stack(level, 1).astype(np.int32),
        c_causal=np.where(b <= a, 0.0, MASKED).astype(np.float32),
        c_reset=reset[None].astype(np.float32),
        c_batchcol=(n[0][None, :] // TD == np.arange(BD)[:, None]).reshape(1, BD * NS).astype(np.float32),
        c_batchrow=(np.arange(NS)[:, None] // TD == np.arange(BD)[None, :]).astype(np.float32),
        c_fold=(a % NS == n).astype(np.float32),
        c_newbias=np.where(same & (n % TD <= q % TD), 0.0, UNSEEN).astype(np.float32),
        c_same=same.astype(np.float32),
        c_ownhead=(a % H == np.arange(H)[None]).astype(np.float32),
        c_iota=np.arange(TOPK)[None].astype(np.float32),
        c_part=np.concatenate([a % 8, (a // NS) * QUARTER], 1).astype(np.float32),
        c_invcnt=(1.0 / np.minimum(np.arange(16)[None] + 1, w)).reshape(1, -1).astype(np.float32),
    )


class Program:

    def __init__(self, nc, io, scratch):
        self.nc, self.io, self.scratch = nc, io, scratch
        self.keep = ExitStack()
        self.used = {}
        self.in_use = []

    def numbered(self, name):
        self.used[name] = self.used.get(name, 0) + 1
        return name if self.used[name] == 1 else f"{name}_{self.used[name]}"

    def sb(self, ctx, name, shape, dt=F32):
        return ctx.enter_context(self.nc.sbuf_tensor(self.numbered(name), shape, dt))

    def sems(self, ctx, *names):
        sems = [self.nc.alloc_semaphore(self.numbered("s_" + n)) for n in names]
        self.in_use += sems
        ctx.callback(self.clear_sems)
        return sems

    def sem_ring(self, ctx, name, n):
        return self.sems(ctx, *(f"{name}{i}" for i in range(n)))

    def stage(self, *parts):
        with ExitStack() as ctx:
            with self.nc.Block() as block:
                later = [part(self, ctx, block, *args) for part, *args in parts]
                for part in later:
                    if part is not None:
                        part(self, ctx, block)

    def clear_sems(self):
        if self.in_use:
            self.nc.clear_and_free_semaphores(self.in_use)
            self.in_use = []
            self.nc.all_engine_barrier()


def bank_cols(ps, b, n=G):
    return ps[:, b:b + n, 0:GC]


def grouped(ap):
    return ap.rearrange("p (g n) -> p g n", g=G)



def load_constants(k, ctx, block):
    io = k.io
    rows = k.sb(ctx, "vec_rows", [9 * KD, P])
    landed, turned = k.sems(ctx, "landed", "turned")

    @block.sync
    def _(sp):
        sp.dma_start(k.ident[:], io["c_ident"]).then_inc(landed, 16)
        at = 0
        for name in ("mix_norm", "ffn_norm", "ple_norm", "final_norm", "pool_scale", "lb_logits"):
            a = io[name]
            n = a.size() // P if callable(a.size) else a.size // P
            flat = a.rearrange("(n p) -> n p", p=P) if len(a.shape) == 1 else a.rearrange("l (n p) -> (l n) p", p=P)
            sp.dma_start(rows[at:at + n, :], flat).then_inc(landed, 16)
            at += n
        sp.wait_ge(landed, 16 * 7)

    @block.vector
    def _(dve):
        dve.memset(k.ones[:], 1.0)
        dve.memset(k.eps[:], EPS)
        dve.wait_ge(turned, 1)
        dve.tensor_copy(k.vec[:], k.ps[:, 0, 0:9 * KD])

    @block.tensor
    def _(pe):
        pe.wait_ge(landed, 16 * 7)
        pe.transpose(k.ps[:, 0, 0:9 * KD], rows[:], k.ident[0:9 * KD, 0:9 * KD]).then_inc(turned, 1)

    k.mix_w = [k.vec[:, i * KD:(i + 1) * KD] for i in range(2)]
    k.ffn_w = [k.vec[:, (2 + i) * KD:(3 + i) * KD] for i in range(2)]
    k.ple_w = [k.vec[:, (4 + i) * KD:(5 + i) * KD] for i in range(2)]
    k.pool_s = k.vec[:, 7 * KD:8 * KD]
    k.lb_logit = [k.vec[:, 8 * KD + i * BH:8 * KD + (i + 1) * BH] for i in range(2)]



def load_normalised(k, ctx, block):
    io, ps = k.io, k.ps
    rows = k.sb(ctx, "x_rows", [P, 3, D])
    square = k.sb(ctx, "x_square", [P, D])
    stat = k.sb(ctx, "x_stat", [P, 3, 3])
    landed = k.sem_ring(ctx, "x_landed", 3)
    tables, rooted, scaled, turned, copied = k.sems(ctx, "tables", "rooted", "scaled", "turned", "copied")

    @block.sync
    def _(sp):
        for r in range(NT + 1):
            n = rows_of(r)
            if r >= 3:
                sp.wait_ge(turned, r - 2)
            src = io["x_prompt"][0, r * P:(r + 1) * P, :] if r < NT else io["x_sample"].rearrange("b t d -> (b t) d")
            sp.dma_start(rows[0:n, r % 3, :], src).then_inc(landed[r % 3], 16)
        table = io["c_rope"].rearrange("t a d -> t (a d)")
        sp.dma_start(k.rope[:, 0:NT, :], table[0:SEQ].rearrange("(r p) n -> p r n", p=P)).then_inc(tables, 16)
        sp.dma_start(k.rope[0:NS, NT, :], table[SEQ:R]).then_inc(tables, 16)
        sp.dma_start(k.part[:], io["c_part"]).then_inc(tables, 16)
        sp.wait_ge(tables, 48)

    @block.scalar
    def _(act):
        for r in range(NT + 1):
            n, s = rows_of(r), r % 3
            act.wait_ge(landed[s], 16 * (r // 3 + 1))
            if r >= 3:
                act.wait_ge(scaled, r - 2)
            act.activation(square[0:n], rows[0:n, s, :], ACT.Square, accum_out=stat[0:n, s, 0:1])
            act.drain()
            act.activation(stat[0:n, s, 1:2], stat[0:n, s, 0:1], ACT.Sqrt, bias=k.eps[0:n, 0:1], scale=1.0 / D).then_inc(rooted, 1)

    @block.vector
    def _(dve):
        def copy(r):
            n, b = rows_of(r), 2 * (r % 2)
            dve.wait_ge(turned, r + 1)
            src = ps[:, b:b + 2, :].rearrange("p b (d n) -> p (b d) n", n=P)
            dve.tensor_tensor(k.hT[:, :, r * P:r * P + n], src[:, :, 0:n], k.mix_w[0][:, :, None].broadcast_to([P, KD, n]),
                              ALU.mult).then_inc(copied, 1)

        for r in range(NT + 1):
            n, s = rows_of(r), r % 3
            dve.wait_ge(rooted, r + 1)
            dve.reciprocal(stat[0:n, s, 2:3], stat[0:n, s, 1:2])
            dve.drain()
            dve.tensor_scalar(rows[0:n, s, :], rows[0:n, s, :], stat[0:n, s, 2:3], None, ALU.mult).then_inc(scaled, 1)
            if r:
                copy(r - 1)
        copy(NT)

    @block.tensor
    def _(pe):
        for r in range(NT + 1):
            n = rows_of(r)
            pe.wait_ge(scaled, r + 1)
            if r >= 2:
                pe.wait_ge(copied, r - 1)
            for d in range(KD):
                at = (d % 4) * P
                m = pe.transpose(ps[:, 2 * (r % 2) + d // 4, at:at + n], rows[0:n, r % 3, d * P:(d + 1) * P],
                                 k.ident[0:n, 0:n])
            m.then_inc(turned, 1)


class Norm:

    def __init__(self, k, ctx, hT, weight, square=None, total=None):
        self.k, self.hT, self.weight = k, hT, weight
        self.square = k.sb(ctx, "norm_square", [P, 2, R]) if square is None else square
        self.total = k.sb(ctx, "norm_total", [P, R])[:] if total is None else total
        self.squared, self.summed, self.ssq, self.rooted, self.normed = k.sems(
            ctx, "norm_squared", "norm_summed", "norm_ssq", "norm_rooted", "normed")

    def scalar(self, act):
        k = self.k
        for d in range(KD):
            if d >= 2:
                act.wait_ge(self.summed, max(1, d - 2))
            act.activation(self.square[:, d % 2, :], k.xT[:, d, :], ACT.Square).then_inc(self.squared, 1)
        for g in range(G):
            act.wait_ge(self.ssq, g + 1)
            act.activation(self.square[:, 0, g * GC:(g + 1) * GC], k.ps[:, g, 0:GC], ACT.Sqrt,
                           bias=k.eps[:, 0:1], scale=1.0 / D).then_inc(self.rooted, 1)

    def tensor(self, pe):
        k = self.k
        pe.wait_ge(self.summed, KD - 1)
        for g in range(G):
            pe.matmul(k.ps[:, g, 0:GC], k.ones[:], self.total[:, g * GC:(g + 1) * GC],
                      start=True, stop=True).then_inc(self.ssq, 1)

    def sum_up(self, dve):
        k, total = self.k, self.total
        for d in range(1, KD):
            dve.wait_ge(self.squared, d + 1)
            first = self.square[:, 0, :] if d == 1 else total
            dve.tensor_tensor(total, first, self.square[:, d % 2, :], ALU.add).then_inc(self.summed, 1)
            dve.drain()
        for g in range(G):
            dve.wait_ge(self.rooted, g + 1)
            dve.reciprocal(total[:, g * GC:(g + 1) * GC], self.square[:, 0, g * GC:(g + 1) * GC])
        dve.drain()

    def vector(self, dve):
        k, total = self.k, self.total
        self.sum_up(dve)
        for d in range(KD):
            dve.scalar_tensor_tensor(self.hT[:, d, :], k.xT[:, d, :], self.weight[:, d:d + 1], total,
                                     ALU.mult, ALU.mult).then_inc(self.normed, 1)


class SplitNorm(Norm):

    def __init__(self, k, ctx, h, weight, square=None, total=None):
        super().__init__(k, ctx, h, weight, square, total)
        self.exact = self.square
        self.scaled, self.high, self.even_low = k.sems(ctx, "norm_scaled", "norm_high", "norm_even_low")

    def round(self, act):
        for d in range(KD):
            act.wait_ge(self.scaled, d + 1)
            act.copy(self.hT[:, 0, d, :], self.exact[:, d % 2, :]).then_inc(self.high, 1)

    def low(self, eng, d):
        eng.wait_ge(self.high, d + 1)
        return eng.tensor_tensor(self.hT[:, 1, d, :], self.exact[:, d % 2, :], self.hT[:, 0, d, :].bitcast(F32), ALU.subtract)

    def pool(self, pool):
        for d in range(1, KD, 2):
            pool.wait_ge(self.even_low, d // 2 + 1)
            self.low(pool, d).then_inc(self.normed, 2)

    def vector(self, dve):
        self.sum_up(dve)
        for d in range(KD):
            if d >= 2:
                dve.wait_ge(self.even_low if d % 2 == 0 else self.normed, d // 2 if d % 2 == 0 else d - 1)
            dve.scalar_tensor_tensor(self.exact[:, d % 2, :], self.k.xT[:, d, :], self.weight[:, d:d + 1], self.total,
                                     ALU.mult, ALU.mult).then_inc(self.scaled, 1)
            if d % 2:
                self.low(dve, d - 1).then_inc(self.even_low, 1)
        dve.wait_ge(self.normed, KD)



def project_rows(k, ctx, block, chunks, scores=False, moves=None):
    io, ps, hT = k.io, k.ps, k.hT
    w_in = io["w_in"][0].rearrange("(k p) n -> p k n", p=P)
    jobs = [(c, r) for c in chunks for r in range(NT + 1)]
    rotated = {"aq", "ak", "iq", "ik"}
    width = {c: IK_COLS if c == "ik" else 512 for c in COL}
    turns = {"aq": k.qT, "ak": k.kT, "iq": k.iqT, "ik": k.ikT}
    RAW = 3
    LAG = 3
    if scores:
        index = PromptScores(k, ctx)
        first = sum(c in rotated for c in chunks) * (NT + 1) + LAG - 1
        assert all(c not in rotated for c, _ in jobs[first:]) and 2 * (len(jobs) - first) >= len(index.steps)

    def score_steps(j):
        at = 2 * (j - first) if scores else 0
        return range(at, min(at + 2, len(index.steps))) if scores and j >= first else range(0)

    nth_rot, nth_store = {}, {}
    for j, (c, r) in enumerate(jobs):
        if c in rotated:
            nth_rot[j] = len(nth_rot)
        if c in ("ak", "av", "ik", "bi", "bg") or r == NT:
            nth_store[j] = len(nth_store)

    def dest(c, r):
        if r == NT:
            return {"ak": io["k_sample"], "av": io["v_sample"], "ik": io["kidx_sample"], "aq": k.scratch["q_s"],
                    "iq": k.scratch["iq_s"], "bi": k.scratch["bi"][SEQ:R], "bg": k.scratch["bg"][SEQ:R]}[c]
        rows = slice(r * P, (r + 1) * P)
        return {"ak": io["k_prompt"], "av": io["v_prompt"], "ik": io["kidx_prompt"],
                "bi": k.scratch["bi"], "bg": k.scratch["bg"]}[c][rows]

    w = k.sb(ctx, "w_chunk", [P, 2, KD, 512])
    raw = k.sb(ctx, "raw", [P, RAW, 512])
    rot = k.sb(ctx, "rot", [P, RAW, 512])
    part = k.sb(ctx, "rope_part", [P, 2, 512])
    w_landed = k.sem_ring(ctx, "w_landed", 2)
    stored = k.sem_ring(ctx, "rows_stored", RAW)
    projected, taken, roped, turned, copied, iw_stored = k.sems(
        ctx, "projected", "taken", "roped", "turned", "copied", "iw_stored")

    def stores_before(j):
        return sum(1 for i in nth_store if i < j and i % RAW == j % RAW)

    @block.sync
    def _(sp):
        def load(i):
            c = chunks[i]
            if i >= 2:
                sp.wait_ge(projected, (NT + 1) * (i - 1))
            sp.dma_start(w[:, i % 2, :, 0:width[c]], w_in[:, :, COL[c]:COL[c] + width[c]]).then_inc(w_landed[i % 2], 16)

        load(0)
        for j, (c, r) in enumerate(jobs):
            i = j // (NT + 1)
            if r == 1 and i + 1 < len(chunks):
                load(i + 1)
            if j in nth_store:
                n = rows_of(r)
                if c in rotated:
                    sp.wait_ge(roped, nth_rot[j] + 1)
                    cols = DH if c == "ik" else 512
                    sp.dma_start(dest(c, r), rot[0:n, j % RAW, 0:cols]).then_inc(stored[j % RAW], 16)
                else:
                    sp.wait_ge(taken, j + 1)
                    sp.dma_start(dest(c, r), raw[0:n, j % RAW, :]).then_inc(stored[j % RAW], 16)
        if "ik" in chunks:
            sp.wait_ge(taken, len(jobs))
            sp.dma_start(k.scratch["iw_s"], k.iw[0:NS, NT, :]).then_inc(iw_stored, 16)
            sp.wait_ge(iw_stored, 16)
        for s in range(RAW):
            sp.wait_ge(stored[s], 16 * sum(1 for i in nth_store if i % RAW == s))

    @block.tensor
    def _(pe):
        def turn(j):
            c, r = jobs[j]
            n, t = rows_of(r), nth_rot[j]
            pe.wait_ge(roped, t + 1)
            if t >= 4:
                pe.wait_ge(copied, t - 3)
            for i in range(1 if c == "ik" else 4):
                m = pe.transpose(ps[:, 4 + t % 4, i * P:i * P + n], rot[0:n, j % RAW, i * P:(i + 1) * P],
                                 k.ident[0:n, 0:n])
            m.then_inc(turned, 1)

        for j, (c, r) in enumerate(jobs):
            i, n = j // (NT + 1), rows_of(r)
            if r == 0:
                pe.wait_ge(w_landed[i % 2], 16 * (i // 2 + 1))
            if j >= 4:
                pe.wait_ge(taken, j - 3)
            for d in range(KD):
                m = pe.matmul(ps[0:n, j % 4, 0:width[c]], hT[:, d, r * P:r * P + n], w[:, i % 2, d, 0:width[c]],
                              start=d == 0, stop=d == KD - 1)
            m.then_inc(projected, 1)
            if j - LAG + 1 in nth_rot:
                turn(j - LAG + 1)
            for u in score_steps(j):
                if u == 0:
                    pe.wait_ge(copied, len(nth_rot))
                index.tensor(pe, u)
        for j in range(len(jobs) - LAG + 1, len(jobs)):
            if j in nth_rot:
                turn(j)

    @block.scalar
    def _(act):
        def take(j):
            c, r = jobs[j]
            n = rows_of(r)
            act.wait_ge(projected, j + 1)
            if j >= RAW:
                if j - RAW in nth_rot:
                    act.wait_ge(roped, nth_rot[j - RAW] + 1)
                if stores_before(j):
                    act.wait_ge(stored[j % RAW], 16 * stores_before(j))
            src, dst = ps[0:n, j % 4, 0:width[c]], raw[0:n, j % RAW, 0:width[c]]
            if c == "ik":
                act.activation(k.iw[0:n, r, :], src[:, DH:IK_COLS], ACT.Copy, scale=float(np.float32(H ** -0.5) * DH ** -0.5))
            act.activation(dst, src, ACT.Silu if c == "bg" else ACT.Copy).then_inc(taken, 1)

        def copy_turned(j):
            c, r = jobs[j]
            n, t = rows_of(r), nth_rot[j]
            act.wait_ge(turned, t + 1)
            src = ps[:, 4 + t % 4, :].rearrange("p (i n) -> p i n", n=P)
            if c == "ik":
                act.copy(k.ikT[:, r * P:r * P + n], src[:, 0, 0:n]).then_inc(copied, 1)
            else:
                act.copy(turns[c][:, :, r * P:r * P + n], src[:, :, 0:n]).then_inc(copied, 1)

        k.banks_taken = (taken, len(jobs))
        for j in range(len(jobs)):
            take(j)
            if j - LAG in nth_rot:
                copy_turned(j - LAG)
            for u in score_steps(j):
                index.scalar(act, u)
        for j in range(len(jobs) - LAG, len(jobs)):
            if j in nth_rot:
                copy_turned(j)

    @block.gpsimd
    def _(pool):
        for j, (c, r) in enumerate(jobs):
            if c not in rotated:
                continue
            n, t = rows_of(r), nth_rot[j]
            heads = 1 if c == "ik" else H
            cols = heads * DH
            pool.wait_ge(taken, j + 1)
            if t >= RAW:
                pool.wait_ge(turned, t - RAW + 1)
            if stores_before(j):
                pool.wait_ge(stored[j % RAW], 16 * stores_before(j))
            x = raw[0:n, j % RAW, 0:cols].rearrange("p (h t d) -> p h t d", h=heads, t=2)
            table = k.rope[0:n, r, :].rearrange("p (a t d) -> p a t d", a=2, t=2)
            for a, v in ((0, x), (1, x[:, :, ::-1, :])):
                pool.tensor_tensor(part[0:n, a, 0:cols].rearrange("p (h t d) -> p h t d", h=heads, t=2), v,
                                   table[:, a, :, :][:, None, :, :].broadcast_to([n, heads, 2, DH // 2]), ALU.mult)
            pool.drain()
            if c == "ik":
                pool.tensor_tensor(rot[0:n, j % RAW, cols:2 * cols], part[0:n, 0, 0:cols], part[0:n, 1, 0:cols], ALU.add)
            pool.tensor_tensor(rot[0:n, j % RAW, 0:cols], part[0:n, 0, 0:cols], part[0:n, 1, 0:cols],
                               ALU.add).then_inc(roped, 1)
            pool.drain()
        if scores:
            for u in range(len(index.steps)):
                if u in moves:
                    moves[u](pool)
                index.pool(pool, u)



def lower_bound(k, ctx, block):
    t = k.sb(ctx, "lb_terms", [P, 5, BH])
    lb_ready, exped = k.sems(ctx, "lb_ready", "exped")

    @block.scalar
    def _(act):
        act.wait_ge(lb_ready, 1)
        for i in range(2):
            act.activation(t[:, i, :], t[:, i, :], ACT.Exp).then_inc(exped, 1)

    @block.vector
    def _(dve):
        dve.tensor_tensor(t[:, 2, :], k.lb_logit[0], k.lb_logit[1], ALU.max)
        dve.drain()
        for i in range(2):
            dve.tensor_tensor(t[:, i, :], k.lb_logit[i], t[:, 2, :], ALU.subtract)
        dve.drain()
        dve.tensor_copy(t[:, 3, :], t[:, 2, :]).then_inc(lb_ready, 1)
        dve.wait_ge(exped, 2)
        dve.tensor_tensor(t[:, 3, :], t[:, 0, :], t[:, 1, :], ALU.add)
        dve.drain()
        dve.reciprocal(t[:, 4, :], t[:, 3, :])
        dve.drain()
        dve.tensor_tensor(k.lb[:, 0, :], t[:, 0, :], t[:, 4, :], ALU.mult)
        dve.drain()
        dve.tensor_scalar(k.lb[:, 1, :], k.lb[:, 0, :], -1.0, 1.0, ALU.mult, ALU.add)


def project_gates(k, ctx, block):
    io, ps, hT = k.io, k.ps, k.hT
    w_in = io["w_in"][0].rearrange("(k p) n -> p k n", p=P)
    w = k.sb(ctx, "w_gate_tile", [P, 2, KD, P])
    out = k.sb(ctx, "gate_out", [P, 2, R])
    keyf = k.sb(ctx, "gate_key", [P, 2, R])
    f = k.xT[:, KD - BH:KD, :]
    reset = k.sb(ctx, "reset", [P, R])
    w_landed, stored_q, stored_k, stored_b = (k.sem_ring(ctx, n, 2) for n in ("w_landed", "stored_q", "stored_k", "stored_b"))
    (const_landed,) = k.sems(ctx, "const_landed")
    multiplied, taken, sig_taken, f_made, key_made, log_taken, scanned = k.sems(
        ctx, "multiplied", "taken", "sig_taken", "f_made", "key_made", "log_taken", "scanned")
    lb_value, lb_rest = k.lb[:, 0, :], k.lb[:, 1, :]
    banks_taken = k.banks_taken
    k.banks_taken = (taken, 2 * BH)
    key_step, copy_step = k.between

    @block.sync
    def _(sp):
        def load(i):
            at = COL["bq" if i < BH else "bf"] + (i % BH) * P
            sp.dma_start(w[:, i % 2], w_in[:, :, at:at + P]).then_inc(w_landed[i % 2], 16)

        sp.dma_start(reset[:], io["c_reset"].broadcast_to([P, R])).then_inc(const_landed, 16)
        load(0)
        load(1)
        for i in range(2 * BH):
            if i + 2 < 2 * BH:
                sp.wait_ge(multiplied, i + 1)
                load(i + 2)
            if i < BH:
                sp.wait_ge(taken, i + 1)
                sp.dma_start(k.scratch["gq"][i], out[:, i % 2, :]).then_inc(stored_q[i % 2], 16)
            else:
                sp.wait_ge(key_made, i - BH + 1)
                sp.dma_start(k.scratch["gk"][i - BH], keyf[:, i % 2, :]).then_inc(stored_k[i % 2], 16)
        for i in range(BH):
            sp.wait_ge(scanned, i + 1)
            sp.dma_start(k.scratch["gb"][i], out[:, i % 2, :]).then_inc(stored_b[i % 2], 16)
        for s in range(2):
            sp.wait_ge(stored_k[s], 16 * BH // 2)
            sp.wait_ge(stored_b[s], 16 * BH // 2)

    @block.tensor
    def _(pe):
        pe.wait_ge(*banks_taken)
        for i in range(2 * BH):
            b = 4 * (i % 2)
            pe.wait_ge(w_landed[i % 2], 16 * (i // 2 + 1))
            if i >= 2:
                pe.wait_ge(taken, i - 1)
            for d in range(KD):
                for g in range(G):
                    m = pe.matmul(ps[:, b + g, 0:GC], w[:, i % 2, d, :], hT[:, d, g * GC:(g + 1) * GC],
                                  start=d == 0, stop=d == KD - 1)
                if d < KD - 1:
                    key_step(pe, i * KD + d)
            m.then_inc(multiplied, 1)
            key_step(pe, i * KD + KD - 1)

    @block.scalar
    def _(act):
        for i in range(BH):
            for j in range(i * KD, (i + 1) * KD):
                copy_step(act, j)
            act.wait_ge(multiplied, i + 1)
            if i >= 2:
                act.wait_ge(stored_q[i % 2], 16 * (i // 2))
            act.activation(grouped(out[:, i % 2, :]), bank_cols(ps, 4 * (i % 2)), ACT.Silu).then_inc(taken, 1)
        for i in range(BH):
            for j in range((BH + i) * KD, (BH + i + 1) * KD):
                copy_step(act, j)
            act.wait_ge(multiplied, BH + i + 1)
            act.activation(grouped(f[:, i, :]), bank_cols(ps, 4 * (i % 2)), ACT.Sigmoid).then_inc(sig_taken, 1)
            if i >= 2:
                act.wait_ge(stored_k[i % 2], 16 * (i // 2))
            act.activation(grouped(keyf[:, i % 2, :]), bank_cols(ps, 4 * (i % 2)), ACT.Sigmoid, scale=-1.0).then_inc(taken, 1)
        for i in range(BH):
            act.wait_ge(f_made, i + 1)
            act.activation(f[:, i, :], f[:, i, :], ACT.Ln).then_inc(log_taken, 1)

    @block.gpsimd
    def _(pool):
        for i in range(BH):
            pool.wait_ge(sig_taken, i + 1)
            pool.tensor_scalar(f[:, i, :], f[:, i, :], lb_rest[:, i:i + 1], lb_value[:, i:i + 1],
                               ALU.mult, ALU.add).then_inc(f_made, 1)
            pool.wait_ge(taken, BH + i + 1)
            pool.tensor_scalar(keyf[:, i % 2, :], keyf[:, i % 2, :], lb_rest[:, i:i + 1], None, ALU.mult).then_inc(key_made, 1)

    @block.vector
    def _(dve):
        dve.wait_ge(const_landed, 16)
        for i in range(BH):
            dve.wait_ge(log_taken, i + 1)
            dve.wait_ge(*((stored_q[i % 2], 16 * BH // 2) if i < 2 else (stored_b[i % 2], 16 * (i // 2))))
            dve.tensor_tensor_scan(out[:, i % 2, :], reset[:], f[:, i, :], 0.0, ALU.mult, ALU.add).then_inc(scanned, 1)



def recurrence(k, ctx, block):
    io, ps, mixT = k.io, k.ps, k.hT
    tiles = NT + 1
    NORM_AT = 2
    q = k.sb(ctx, "g_q", [P, 2, BH, P])
    key = k.sb(ctx, "g_key", [P, 2, BH, P])
    b = k.sb(ctx, "g_b", [P, 2, BH, P])
    val = k.sb(ctx, "g_val", [P, 2, BH, P])
    gate = k.sb(ctx, "g_gate", [P, 2, BH, P])
    dif = k.sb(ctx, "g_dif", [P, 2, BH * P])
    uq = k.sb(ctx, "g_uq", [P, 2, BH, P])
    uk = k.sb(ctx, "g_uk", [P, 2, BH, P])
    att = k.sb(ctx, "g_att", [P, BH, P])
    eb = k.sb(ctx, "g_eb", [P, BH, P])
    el = k.sb(ctx, "g_el", [P, BH, P])
    qe = k.sb(ctx, "g_qe", [P, BH, P])
    ke = k.sb(ctx, "g_ke", [P, BH, P])
    ker = k.sb(ctx, "g_ker", [P, BH, P])
    state = k.sb(ctx, "g_state", [P, BH, P])
    osq = k.sb(ctx, "g_osq", [P, BH, P])
    on = k.sb(ctx, "g_on", [P, BH, P])
    small = k.sb(ctx, "g_small", [P, 4, BH])
    normw = k.sb(ctx, "g_normw", [P, P])
    level = k.sb(ctx, "g_level", [P, LEVELS + 1, P], I32)
    s0 = k.sb(ctx, "g_s0", [P, BD * BH, P])
    snew = k.sb(ctx, "g_snew", [P, 2, BD, P])
    qm = k.sb(ctx, "g_qm", [P, BH, BD, NS])
    vm = k.sb(ctx, "g_vm", [NS, BH, BD, P])
    bcol = k.sb(ctx, "g_bcol", [P, BD * NS])
    brow = k.sb(ctx, "g_brow", [NS, BD])
    x_rows = k.sb(ctx, "x_rows", [P, 2, D])
    x_landed = k.sem_ring(ctx, "x_landed", 2)
    x_turned, x_copied = k.sems(ctx, "x_turned", "x_copied")
    landed = k.sem_ring(ctx, "g_landed", 2)
    const, s0_landed, state_stored = k.sems(ctx, "g_const", "g_s0_landed", "g_state_stored")
    (dif_made, exped, scaled, multiplied, placed, edge_dif, edge_exp, qe_made, ke_turned, ke_copied, out_done,
     update_done, updated, squared, means, rstd_made, gated, out_turned, out_copied, s_update, snew_made,
     qm_made, tile_read, zeroed) = k.sems(
        ctx, "g_dif_made", "g_exped", "g_scaled", "g_multiplied", "g_placed", "g_edge_dif", "g_edge_exp",
        "g_qe_made", "g_ke_turned", "g_ke_copied", "g_out_done", "g_update_done", "g_updated", "g_squared",
        "g_means", "g_rstd_made", "g_gated", "g_out_turned", "g_out_copied", "g_s_update", "g_snew_made",
        "g_qm_made", "g_tile_read", "g_zeroed")

    def levels_of(c):
        return list(range(LEVELS)) if c < NT else list(range(int(math.log2(TD))))

    def level_count(c):
        return sum(len(levels_of(i)) for i in range(c))

    def product_count(c):
        return level_count(c) + c

    def turn_x(pe, c, half):
        n = rows_of(c)
        pe.wait_ge(x_landed[c % 2], 16 * (c // 2 + 1))
        if c or half:
            pe.wait_ge(x_copied, 2 * c + half)
        for d in range(4):
            at = (4 * half + d) * P
            m = pe.transpose(ps[:, 7, d * P:d * P + n], x_rows[0:n, c % 2, at:at + P], k.ident[0:n, 0:n])
        m.then_inc(x_turned, 1)

    def copy_x(act, c, half):
        n = rows_of(c)
        act.wait_ge(x_turned, 2 * c + half + 1)
        act.copy(k.xT[:, 4 * half:4 * half + 4, c * P:c * P + n], ps[:, 7, :].rearrange("p (d n) -> p d n", n=P)[:, :, 0:n]
                 ).then_inc(x_copied, 1)

    scr = k.scratch

    def halves(ap, w):
        return ap.rearrange("p h (m a w) -> p h m a w", a=2, w=w)

    @block.sync
    def _(sp):
        sp.dma_start(normw[:], io["glr_norm"].broadcast_to([P, P])).then_inc(const, 16)
        sp.dma_start(level[:], io["c_level"]).then_inc(const, 16)
        sp.dma_start(bcol[:], io["c_batchcol"].broadcast_to([P, BD * NS])).then_inc(const, 16)
        sp.dma_start(brow[:], io["c_batchrow"]).then_inc(const, 16)
        for c in range(tiles):
            n = rows_of(c)
            if c == 2:
                sp.dma_start(s0[:], io["state_glr"][0].rearrange("b h d v -> d (b h) v")).then_inc(s0_landed, 16)
            if c >= 2:
                sp.wait_ge(tile_read, c - 1)
            for buf, name in ((q, "gq"), (key, "gk"), (b, "gb")):
                sp.dma_start(buf[:, c % 2, :, 0:n], scr[name].rearrange("h d t -> d h t")[:, :, c * P:c * P + n]
                             ).then_inc(landed[c % 2], 16)
            src = io["x_prompt"][0, c * P:(c + 1) * P, :] if c < NT else io["x_sample"].rearrange("b t d -> (b t) d")
            if c >= 2:
                sp.wait_ge(x_turned, 2 * (c - 1))
            sp.dma_start(x_rows[0:n, c % 2, :], src).then_inc(x_landed[c % 2], 16)
            for buf, name in ((val, "bi"), (gate, "bg")):
                sp.dma_start(buf[0:n, c % 2], scr[name][c * P:c * P + n].rearrange("t (h v) -> t h v", h=BH)
                             ).then_inc(landed[c % 2], 16)
        sp.wait_ge(updated, NT)
        sp.dma_start(io["glr_prompt"][0, 0].rearrange("h d v -> d h v"), state[:]).then_inc(state_stored, 16)
        for h in range(BH):
            sp.wait_ge(snew_made, h + 1)
            sp.dma_start(io["glr_sample"][0].rearrange("b h d v -> h d b v")[h], snew[:, h % 2]).then_inc(state_stored, 16)
            sp.wait_ge(state_stored, 16 * (h + 2))

    @block.vector
    def _(dve):
        dve.memset(att[:], 0.0)
        dve.memset(state[:], 0.0)
        dve.memset(uq[:], 0.0)
        dve.memset(uk[:], 0.0)
        dve.memset(dif[:], 0.0).then_inc(zeroed, 1)
        dve.wait_ge(const, 64)
        dve.drain()

        def mean(c):
            n = rows_of(c)
            dve.wait_ge(squared, c + 1)
            dve.tensor_reduce(small[0:n, 0, :], osq[0:n], AX.X, ALU.add)
            dve.drain()
            dve.tensor_scalar(small[0:n, 1, :], small[0:n, 0, :], 1.0 / P, EPS, ALU.mult, ALU.add).then_inc(means, 1)

        def normalise(c):
            n = rows_of(c)
            dve.wait_ge(rstd_made, c + 1)
            if c:
                dve.wait_ge(out_turned, c)
            dve.tensor_tensor(on[0:n], ps[0:n, 3, :].rearrange("p (h v) -> p h v", h=BH),
                              small[0:n, 2, :][:, :, None].broadcast_to([n, BH, P]), ALU.mult)
            dve.drain()
            dve.tensor_tensor(on[0:n], on[0:n], normw[0:n][:, None, :].broadcast_to([n, BH, P]), ALU.mult)
            dve.drain()
            dve.tensor_tensor(on[0:n], on[0:n], gate[0:n, c % 2], ALU.mult).then_inc(gated, 1)
            dve.drain()

        for c in range(tiles):
            n, s = rows_of(c), c % 2
            lv = levels_of(c)
            dve.wait_ge(landed[s], 80 * (c // 2 + 1))
            qt, kt = q[:, s, :, 0:n], key[:, s, :, 0:n]

            def scale(i):
                w = 1 << lv[i]
                e = level_count(c) + i
                dve.wait_ge(exped, e + 1)
                u = product_count(c) + i
                if e >= 2:
                    before = u - 2 if i >= 2 else (product_count(c - 1) + len(levels_of(c - 1)) - 2 + i if c else 0)
                    dve.wait_ge(multiplied, before + 1)
                d4 = dif[:, e % 2, 0:BH * n].rearrange("p (h m a w) -> p h m a w", h=BH, a=2, w=w)
                dve.tensor_tensor(halves(uk[:, e % 2, :, 0:n], w)[:, :, :, 0, :], halves(kt, w)[:, :, :, 0, :],
                                  d4[:, :, :, 0, :], ALU.mult)
                dve.tensor_tensor(halves(uq[:, e % 2, :, 0:n], w)[:, :, :, 1, :], halves(qt, w)[:, :, :, 1, :],
                                  d4[:, :, :, 1, :], ALU.mult).then_inc(scaled, 1)

            def place(i):
                u = product_count(c) + i
                lvl = lv[i] if i < len(lv) else LEVELS
                dve.wait_ge(multiplied, u + 1)
                if i == 0 and c:
                    dve.wait_ge(out_done, c)
                    if c == NT:
                        dve.memset(att[0:n, :, 0:n], 0.0)
                        dve.drain()
                src = ps[0:n, u % 2, :].rearrange("p (h t) -> p h t", h=BH)[:, :, 0:n]
                dve.copy_predicated(att[0:n, :, 0:n], level[0:n, lvl, 0:n][:, None, :].broadcast_to([n, BH, n]), src
                                    ).then_inc(placed, 1)
                dve.drain()

            for i in range(len(lv)):
                scale(i)
                if i == 0:
                    dve.wait_ge(edge_exp, c + 1)
                    if c:
                        dve.wait_ge(out_done, c)
                    dve.tensor_tensor(ke[:, :, 0:n], kt, el[:, :, 0:n], ALU.mult)
                    dve.tensor_tensor(qe[:, :, 0:n], qt, eb[:, :, 0:n], ALU.mult).then_inc(qe_made, 1)
                    dve.drain()
                if i:
                    place(i - 1)
                if c and len(lv) == LEVELS and i == NORM_AT:
                    mean(c - 1)
                if c and len(lv) == LEVELS and i == NORM_AT + 1:
                    normalise(c - 1)
            place(len(lv) - 1)
            place(len(lv))
            if len(lv) < LEVELS:
                mean(c - 1)
                normalise(c - 1)
            if c == NT:
                for h in range(BH):
                    dve.tensor_tensor(qm[:, h], qe[:, h, 0:n][:, None, :].broadcast_to([P, BD, NS]),
                                      bcol[:].rearrange("p (b t) -> p b t", b=BD), ALU.mult)
                    y = dve.tensor_tensor(vm[:, h], val[0:NS, s, h, :][:, None, :].broadcast_to([NS, BD, P]),
                                          brow[:, :, None].broadcast_to([NS, BD, P]), ALU.mult)
                y.then_inc(qm_made, 1)
            if c < NT:
                dve.wait_ge(update_done, c + 1)
                dve.wait_ge(out_done, c + 1)
                for h in range(BH):
                    x = dve.scalar_tensor_tensor(state[:, h, :], state[:, h, :], eb[:, h, P - 1:P],
                                                 ps[:, 4, h * P:(h + 1) * P], ALU.mult, ALU.add)
                x.then_inc(updated, 1)
            else:
                dve.wait_ge(s0_landed, 16)
                s0v = s0[:].rearrange("p (b h) v -> p b h v", h=BH)
                for h in range(BH):
                    if h >= 2:
                        dve.wait_ge(state_stored, 16 * h)
                    last = eb[:, h, TD - 1:NS:TD]
                    dve.tensor_tensor(snew[:, h % 2], s0v[:, :, h, :], last[:, :, None].broadcast_to([P, BD, P]), ALU.mult)
                    dve.drain()
                    dve.wait_ge(s_update, h + 1)
                    dve.tensor_tensor(snew[:, h % 2], snew[:, h % 2],
                                      ps[:, 0:2, :].rearrange("p a (b v) -> p (a b) v", v=P), ALU.add).then_inc(snew_made, 1)
                    dve.drain()
        mean(NT)
        normalise(NT)

    @block.scalar
    def _(act):
        def square(c):
            n = rows_of(c)
            act.wait_ge(out_done, c + 1)
            if c:
                act.wait_ge(means, c)
            act.activation(osq[0:n], ps[0:n, 3, :].rearrange("p (h v) -> p h v", h=BH), ACT.Square).then_inc(squared, 1)

        def copy_out(c):
            n = rows_of(c)
            act.wait_ge(out_turned, c + 1)
            src = ps[:, 5, :].rearrange("p (h t) -> p h t", h=BH)
            act.copy(mixT[:, BH:2 * BH, c * P:c * P + n], src[:, :, 0:n]).then_inc(out_copied, 1)

        for c in range(tiles):
            n, s = rows_of(c), c % 2
            lv = levels_of(c)
            act.wait_ge(edge_dif, c + 1)
            if c:
                act.wait_ge(updated, c)
            act.activation(eb[:, :, 0:n], b[:, s, :, 0:n], ACT.Exp)
            act.activation(el[:, :, 0:n], el[:, :, 0:n], ACT.Exp).then_inc(edge_exp, 1)
            for i in range(len(lv)):
                e = level_count(c) + i
                act.wait_ge(dif_made, e + 1)
                act.activation(dif[:, e % 2, 0:BH * n], dif[:, e % 2, 0:BH * n], ACT.Exp).then_inc(exped, 1)
                if c and i == 1:
                    square(c - 1)
                if c and i == NORM_AT + 3:
                    copy_out(c - 1)
            if len(lv) < LEVELS:
                copy_out(c - 1)
            act.wait_ge(ke_turned, c + 1)
            act.copy(ker[0:n], ps[0:n, 2, :].rearrange("p (h d) -> p h d", h=BH)).then_inc(ke_copied, 1)
            for half in range(2):
                copy_x(act, c, half)
        square(NT)
        copy_out(NT)

    @block.gpsimd
    def _(pool):
        pool.memset(small[:, 3, :], -0.5)
        pool.wait_ge(zeroed, 1)
        pool.drain()

        def edge(c):
            n, span = rows_of(c), P if c < NT else TD
            pool.wait_ge(landed[c % 2], 80 * (c // 2 + 1))
            if c:
                pool.wait_ge(qe_made, c)
            bs = b[:, c % 2, :, 0:n].rearrange("p h (m w) -> p h m w", w=span)
            pool.tensor_tensor(el[:, :, 0:n].rearrange("p h (m w) -> p h m w", w=span),
                               bs[:, :, :, span - 1:span].broadcast_to([P, BH, n // span, span]), bs, ALU.subtract
                               ).then_inc(edge_dif, 1)

        def make_dif(c, i):
            n, w = rows_of(c), 1 << levels_of(c)[i]
            e = level_count(c) + i
            if e >= 2:
                pool.wait_ge(scaled, e - 1)
            d4 = dif[:, e % 2, 0:BH * n].rearrange("p (h m a w) -> p h m a w", h=BH, a=2, w=w)
            b4 = halves(b[:, c % 2, :, 0:n], w)
            ref = b4[:, :, :, 0, w - 1:w].broadcast_to([P, BH, n // (2 * w), w])
            pool.tensor_tensor(d4[:, :, :, 0, :], ref, b4[:, :, :, 0, :], ALU.subtract)
            pool.tensor_tensor(d4[:, :, :, 1, :], b4[:, :, :, 1, :], ref, ALU.subtract).then_inc(dif_made, 1)

        def rstd(c):
            n = rows_of(c)
            pool.wait_ge(means, c + 1)
            if c:
                pool.wait_ge(gated, c)
            pool.tensor_tensor(small[0:n, 2, :], small[0:n, 1, :], small[0:n, 3, :], ALU.pow).then_inc(rstd_made, 1)

        AHEAD = 2
        for c in range(tiles):
            if c == 0:
                edge(0)
                for i in range(AHEAD):
                    make_dif(0, i)
            for i in range(AHEAD, len(levels_of(c))):
                make_dif(c, i)
                if c and i == NORM_AT + 1:
                    rstd(c - 1)
            if len(levels_of(c)) < LEVELS:
                rstd(c - 1)
            if c + 1 < tiles:
                edge(c + 1)
                for i in range(AHEAD):
                    make_dif(c + 1, i)
        rstd(NT)

    @block.tensor
    def _(pe):
        def turn_out(c):
            n = rows_of(c)
            pe.wait_ge(gated, c + 1)
            if c:
                pe.wait_ge(out_copied, c)
            for h in range(BH):
                m = pe.transpose(ps[:, 5, h * P:h * P + n], on[0:n, h, :], k.ident[0:n, 0:n])
            m.then_inc(out_turned, 1)
            pe.matmul(ps[0:1, 6, 0:1], k.ones[:, 0:1], k.ones[:, 0:1], start=True, stop=True).then_inc(tile_read, 1)

        for c in range(tiles):
            n, s = rows_of(c), c % 2
            lv = levels_of(c)
            pe.wait_ge(landed[s], 80 * (c // 2 + 1))

            def product(i):
                u = product_count(c) + i
                if u >= 2:
                    pe.wait_ge(placed, u - 1)
                e = level_count(c) + i
                if i < len(lv):
                    pe.wait_ge(scaled, e + 1)
                for h in range(BH):
                    lhs = uk[:, e % 2, h, 0:n] if i < len(lv) else key[:, s, h, 0:n]
                    rhs = uq[:, e % 2, h, 0:n] if i < len(lv) else q[:, s, h, 0:n]
                    m = pe.matmul(ps[0:n, u % 2, h * P:h * P + n], lhs, rhs, start=True, stop=True)
                m.then_inc(multiplied, 1)

            for i in range(len(lv) + 1):
                product(i)
                if i == 0:
                    pe.wait_ge(qe_made, c + 1)
                    if c:
                        pe.wait_ge(ke_copied, c)
                    for h in range(BH):
                        m = pe.transpose(ps[0:n, 2, h * P:(h + 1) * P], ke[:, h, 0:n], k.ident[:])
                    m.then_inc(ke_turned, 1)
                if c and i == NORM_AT + 2 and len(lv) == LEVELS:
                    turn_out(c - 1)
            if len(lv) < LEVELS:
                turn_out(c - 1)
            turn_x(pe, c, 0)
            pe.wait_ge(placed, product_count(c + 1))
            if c:
                pe.wait_ge(updated, c)
                pe.wait_ge(gated, c)
            if c == NT:
                pe.wait_ge(qm_made, 1)
                pe.wait_ge(s0_landed, 16)
            for h in range(BH):
                o = ps[0:n, 3, h * P:(h + 1) * P]
                pe.matmul(o, att[0:n, h, 0:n], val[0:n, s, h, :], start=True, stop=False)
                if c < NT:
                    m = pe.matmul(o, qe[:, h, :], state[:, h, :], start=False, stop=True)
                else:
                    for e in range(BD):
                        m = pe.matmul(o, qm[:, h, e, :], s0[:, e * BH + h, :], start=False, stop=e == BD - 1)
            m.then_inc(out_done, 1)
            pe.wait_ge(ke_copied, c + 1)
            if c < NT:
                for h in range(BH):
                    m = pe.matmul(ps[:, 4, h * P:(h + 1) * P], ker[0:n, h, :], val[0:n, s, h, :], start=True, stop=True)
                m.then_inc(update_done, 1)
            else:
                for h in range(BH):
                    if h:
                        pe.wait_ge(snew_made, h)
                    for a in range(2):
                        m = pe.matmul(ps[:, a, :], ker[0:n, h, :], vm[:, h, a * 4:(a + 1) * 4, :].rearrange("p b v -> p (b v)"),
                                      start=True, stop=True)
                    m.then_inc(s_update, 1)
            turn_x(pe, c, 1)
        turn_out(NT)



def mask_offset(i):
    return sum((j + 1) * P for j in range(2, i))


def mask_of(k, i):
    at = mask_offset(i)
    return k.xT[:, 0:4, :].rearrange("p d n -> p (d n)")[:, at:at + (i + 1) * P]


class PromptScores:

    def __init__(self, k, ctx):
        self.k = k
        self.steps = [(i, h) for i in range(2, NT) for h in range(H)]
        self.relu = k.xT[:, 4:6, :]
        self.spare = k.sb(ctx, "spare", [1, 1])
        self.scored, self.rectified, self.weighted, self.summed = k.sems(ctx, "scored", "rectified", "weighted", "summed")

    def tensor(self, pe, u):
        k, (i, h) = self.k, self.steps[u]
        w, row = (i + 1) * P, (h % 2) * DH
        if u >= 2:
            pe.wait_ge(self.rectified, u - 1)
        for a in range(0, w, 512):
            n = min(512, w - a)
            m = pe.matmul(k.ps[:, 4 + 2 * (u % 2) + a // 512, 0:n], k.iqT[row:row + DH, h // 2, i * P:(i + 1) * P],
                          k.ikT[row:row + DH, a:a + n], start=True, stop=True)
        m.then_inc(self.scored, 1)

    def scalar(self, act, u):
        k, (i, h) = self.k, self.steps[u]
        w, b = (i + 1) * P, 4 + 2 * (u % 2)
        relu = self.relu[:, u % 2, 0:w]
        act.wait_ge(self.scored, u + 1)
        if u >= 2:
            act.wait_ge(self.summed, u - 1)
        act.activation(relu, k.ps[:, b:b + 2, :].rearrange("p b n -> p (b n)")[:, 0:w], ACT.Relu).then_inc(self.rectified, 1)
        act.drain()
        act.activation(mask_of(k, i) if h == 0 else relu, relu, ACT.Copy, scale=k.iw[:, i, h:h + 1]).then_inc(self.weighted, 1)

    def pool(self, pool, u):
        k, (i, h) = self.k, self.steps[u]
        sc = mask_of(k, i)
        pool.wait_ge(self.weighted, u + 1)
        if h == 0:
            pool.tensor_copy(self.spare[:], k.ones[0:1, 0:1]).then_inc(self.summed, 1)
        else:
            pool.tensor_tensor(sc, sc, self.relu[:, u % 2, 0:(i + 1) * P], ALU.add).then_inc(self.summed, 1)
        pool.drain()
        if h == H - 1:
            diag = sc[:, i * P:(i + 1) * P]
            pool.affine_select(out=diag, in_=diag, compare_op=ALU.is_ge, fill=UNSEEN, base=0,
                               pattern=[[-1, P]], channel_multiplier=1)


def take_best(k, dve, best, tiles, first, rounds):
    UNROLL = min(rounds, 8)
    with dve.Fori(0, rounds // UNROLL):
        for _ in range(UNROLL):
            for n, i in enumerate(tiles):
                dve.max(best[:, n], mask_of(k, i))
            dve.drain()
            for n, i in enumerate(tiles):
                dve.match_replace(mask_of(k, i), best[:, n], mask_of(k, i), TAKEN)
            dve.drain()
    if first + rounds == ROUNDS:
        for i in tiles:
            dve.tensor_scalar(mask_of(k, i), mask_of(k, i), TAKEN, MASKED, ALU.is_gt, ALU.mult)
        dve.drain()



def attend_prompt(k, ctx, block):
    io, ps, mixT = k.io, k.ps, k.hT
    steps = [(i, h) for i in range(NT) for h in range(H)]
    scale = DH ** -0.5
    v = k.sb(ctx, "v_rows", [P, NT, H * DH])
    causal = k.sb(ctx, "causal", [P, 2, 2 * P])
    logit = k.sb(ctx, "logit", [P, 2, SEQ])
    prob = k.sb(ctx, "prob", [P, 2, SEQ])
    probT = k.sb(ctx, "probT", [P, 2, NT, P])
    top = k.sb(ctx, "top", [P, 2, 2])
    total = k.sb(ctx, "total", [P, 2, H])
    inv = k.sb(ctx, "inv", [P, H])
    att = k.sb(ctx, "att_rows", [P, 2, H * DH])
    best = k.sb(ctx, "best", [P, 2, 8])
    v_landed, c_landed = k.sems(ctx, "v_landed", "c_landed")
    scored, biased, exped, turned, copied, weighed, normed, att_turned, att_copied = k.sems(
        ctx, "scored", "biased", "exped", "turned", "copied", "weighed", "normed", "att_turned", "att_copied")

    def two_banks(b):
        return ps[:, b:b + 2, :].rearrange("p b n -> p (b n)")

    @block.sync
    def _(sp):
        sp.dma_start(causal[:, 0, 0:P], io["c_causal"]).then_inc(c_landed, 16)
        sp.dma_start(causal[:, 1, P:2 * P], io["c_causal"]).then_inc(c_landed, 16)
        sp.dma_start(v[:], io["v_prompt"].rearrange("(i p) n -> p i n", p=P)).then_inc(v_landed, 16)

    @block.tensor
    def _(pe):
        def score(u):
            i, h = steps[u]
            w, row = (i + 1) * P, (h % 2) * DH
            if u >= 2:
                pe.wait_ge(biased, u - 1)
            for a in range(0, w, 512):
                n = min(512, w - a)
                m = pe.matmul(ps[:, 2 * (u % 2) + a // 512, 0:n], k.qT[row:row + DH, h // 2, i * P:(i + 1) * P],
                              k.kT[row:row + DH, h // 2, a:a + n], start=True, stop=True)
            m.then_inc(scored, 1)

        def turn(u):
            i, h = steps[u]
            pe.wait_ge(exped, u + 1)
            if u:
                pe.wait_ge(copied, u)
            for j in range(i + 1):
                m = pe.transpose(ps[:, 4 + j // 4, (j % 4) * P:(j % 4 + 1) * P], prob[:, u % 2, j * P:(j + 1) * P], k.ident[:])
            m.then_inc(turned, 1)

        def weigh(u):
            i, h = steps[u]
            pe.wait_ge(copied, u + 1)
            if h == 0:
                pe.wait_ge(v_landed, 16)
                if i:
                    pe.wait_ge(normed, i)
            for j in range(i + 1):
                m = pe.matmul(ps[:, 6, h * DH:(h + 1) * DH], probT[:, u % 2, j, :], v[:, j, h * DH:(h + 1) * DH],
                              start=j == 0, stop=j == i)
            m.then_inc(weighed, 1)

        def turn_att(i):
            pe.wait_ge(normed, i + 1)
            if i:
                pe.wait_ge(att_copied, i)
            for f in range(4):
                m = pe.transpose(ps[:, 7, f * P:(f + 1) * P], att[:, i % 2, f * P:(f + 1) * P], k.ident[:])
            m.then_inc(att_turned, 1)

        score(0)
        for u in range(len(steps) + 1):
            if u + 1 < len(steps):
                score(u + 1)
            if u < len(steps):
                turn(u)
            if u:
                weigh(u - 1)
            if u >= 10 and (u - 10) % H == 0:
                turn_att((u - 10) // H)
        turn_att(NT - 1)

    @block.vector
    def _(dve):
        dve.memset(causal[:, 1, 0:P], 0.0)
        dve.wait_ge(c_landed, 32)
        dve.drain()

        def bias(u):
            i, h = steps[u]
            w = (i + 1) * P
            mask = causal[:, i, 0:w] if i < 2 else mask_of(k, i)
            dve.wait_ge(scored, u + 1)
            if u >= 2:
                dve.wait_ge(exped, u - 1)
            dve.tensor_tensor_reduce(logit[:, u % 2, 0:w], two_banks(2 * (u % 2))[:, 0:w], mask, 1.0, UNSEEN,
                                     ALU.add, ALU.max, top[:, u % 2, 0:1])
            dve.drain()
            dve.tensor_scalar(top[:, u % 2, 1:2], top[:, u % 2, 0:1], -scale, None, ALU.mult).then_inc(biased, 1)

        def normalise(i):
            dve.wait_ge(weighed, (i + 1) * H)
            if i >= 2:
                dve.wait_ge(att_turned, i - 1)
            dve.reciprocal(inv[:], total[:, i % 2, :])
            dve.drain()
            dve.tensor_tensor(att[:, i % 2].rearrange("p (h d) -> p h d", h=H), ps[:, 6, :].rearrange("p (h d) -> p h d", h=H),
                              inv[:][:, :, None].broadcast_to([P, H, DH]), ALU.mult).then_inc(normed, 1)
            dve.drain()

        for u, (i, h) in enumerate(steps):
            bias(u)
            if u >= H and h == 1:
                normalise(i - 1)
            if 1 <= i <= 4:
                take_best(k, dve, best, (NT - 1,), u - H, 1)
        normalise(NT - 1)

    @block.scalar
    def _(act):
        def exp(u):
            i, h = steps[u]
            w = (i + 1) * P
            act.wait_ge(biased, u + 1)
            if u >= 2:
                act.wait_ge(turned, u - 1)
            if h == 0 and i >= 2:
                act.wait_ge(normed, i - 1)
            act.activation(prob[:, u % 2, 0:w], logit[:, u % 2, 0:w], ACT.Exp, bias=top[:, u % 2, 1:2], scale=scale,
                           accum_out=total[:, i % 2, h:h + 1])
            act.drain()
            act.copy(top[0:1, u % 2, 0:1], top[0:1, u % 2, 1:2]).then_inc(exped, 1)

        def copy(u):
            i, h = steps[u]
            act.wait_ge(turned, u + 1)
            if u >= 2:
                act.wait_ge(weighed, u - 1)
            act.copy(probT[:, u % 2].rearrange("p j n -> p (j n)")[:, 0:(i + 1) * P], two_banks(4)[:, 0:(i + 1) * P]
                     ).then_inc(copied, 1)

        def copy_att(i):
            act.wait_ge(att_turned, i + 1)
            act.copy(mixT[:, 0:4, i * P:(i + 1) * P], ps[:, 7, :].rearrange("p (f n) -> p f n", f=4)).then_inc(att_copied, 1)

        exp(0)
        for u in range(len(steps)):
            copy(u)
            if u + 1 < len(steps):
                exp(u + 1)
            if u >= 11 and (u - 11) % H == 0:
                copy_att((u - 11) // H)
        copy_att(NT - 1)



def score_sample(k, ctx, block):
    io, ps = k.io, k.ps
    N = BD * 4
    E16 = PAGE // 8
    pages = k.sb(ctx, "pages", [P, N], I32)
    index = k.sb(ctx, "index", [P, N], I32)
    keys = k.sb(ctx, "keys", [P, 4, E16 * DH])
    keysT = k.sb(ctx, "keysT", [P, 2, 8, P])
    part = k.sb(ctx, "part", [P, 2, 8 * 2 * TD * H])
    iq2 = k.sb(ctx, "iq_twice", [NS, H, 2, DH])
    bd = k.sb(ctx, "iq_blocks", [P, BD, 2, TD, H])
    wb = k.sb(ctx, "iw_all", [P, NS, H])
    sc = k.sb(ctx, "key_scores", [P, E16, 4, NS])
    newp = k.sb(ctx, "new_part", [NS, NS * H])
    news = k.sb(ctx, "new_scores", [NS, NS])
    newt = k.sb(ctx, "new_turned", [NS, NS])
    newb = k.sb(ctx, "new_bias", [NS, NS])
    newq = k.sb(ctx, "new_query", [NS, TD])
    g_landed = k.sem_ring(ctx, "keys_landed", 4)
    pt_landed, small_landed, placed = k.sems(ctx, "pt_landed", "small_landed", "placed")
    (indexed, turned, copied, multiplied, weighted, iq_turned, blocks_made, new_scored, new_summed, new_turned,
     new_ready, sc_turned, sc_copied, zeroed, reduced) = k.sems(
        ctx, "indexed", "turned", "copied", "multiplied", "weighted", "iq_turned", "blocks_made", "new_scored",
        "new_summed", "new_turned", "new_ready", "sc_turned", "sc_copied", "zeroed", "reduced")

    @block.sync
    def _(sp):
        src = io["page_table"].rearrange("b (k i) -> i b k", i=16)
        for s in range(8):
            sp.dma_start(pages[s:P:8, :].rearrange("p (b k) -> p b k", b=BD), src,
                         allow_slow_non_contiguous=True).then_inc(pt_landed, 16)
        iq = k.scratch["iq_s"].rearrange("r (h d) -> r h d", h=H)
        for a in range(2):
            sp.dma_start(iq2[:, :, a, :], iq).then_inc(small_landed, 16)
        sp.dma_start(wb[:].rearrange("p q h -> p (q h)"),
                     k.scratch["iw_s"].rearrange("(o q) h -> o (q h)", o=1).broadcast_to([P, NS * H])).then_inc(small_landed, 16)
        sp.dma_start(newb[:], io["c_newbias"]).then_inc(small_landed, 16)
        sp.wait_ge(new_ready, 1)
        sp.wait_ge(zeroed, 1)
        sp.dma_start(k.found[3 * NS:P, QUARTER:QUARTER + TD], newq[:]).then_inc(placed, 16)
        sp.wait_ge(placed, 16)

    @block.gpsimd
    def _(pool):
        view = io["cache_kidx"][0].rearrange("g (s e) d -> (g s) (e d)", s=8)
        pool.wait_ge(indexed, 1)
        for j in range(N):
            if j >= 4:
                pool.wait_ge(turned, 2 * (j - 3))
            pool.indirect_dma_start(keys[:, j % 4], None, view,
                                    bass.IndirectOffsetOnAxis(ap=index[:, j:j + 1].bitcast(U32), axis=0)
                                    ).then_inc(g_landed[j % 4], 16)

    @block.tensor
    def _(pe):
        pe.wait_ge(small_landed, 64)
        for h in range(H):
            m = pe.transpose(ps[:, 7, h * NS:(h + 1) * NS], iq2[:, h].rearrange("p a d -> p (a d)"), k.ident[0:NS, 0:NS])
        m.then_inc(iq_turned, 1)
        pe.wait_ge(blocks_made, 1)
        pe.matmul(ps[0:NS, 6, 0:NS * H].rearrange("p (b q) -> p b q", b=BD), k.ikT[0:DH, SEQ:R],
                  bd[0:DH, :, 0].rearrange("p b t h -> p b (t h)"), start=True, stop=True).then_inc(new_scored, 1)

        def turn(j):
            pe.wait_ge(g_landed[j % 4], 16 * (j // 4 + 1))
            for a in range(2):
                if j >= 2:
                    pe.wait_ge(copied, 2 * j + a - 3)
                for e in range(4):
                    x = 2 * (4 * a + e) * DH
                    m = pe.transpose(ps[:, 4 * (j % 2) + a, e * P:(e + 1) * P], keys[:, j % 4, x:x + 2 * DH], k.ident[:])
                m.then_inc(turned, 1)

        def multiply(j):
            if j >= 2:
                pe.wait_ge(weighted, j - 1)
            pe.wait_ge(copied, 2 * j + 2)
            for e in range(8):
                m = pe.matmul(ps[:, 2 + j % 2, e * 64:(e + 1) * 64], keysT[:, j % 2, e, :],
                              bd[:, j // 4].rearrange("p a t h -> p (a t h)"), start=True, stop=True)
            m.then_inc(multiplied, 1)

        for j in range(N + 1):
            if j < N:
                turn(j)
            if j:
                multiply(j - 1)
        pe.wait_ge(new_summed, 1)
        pe.transpose(ps[0:NS, 7, 0:NS], news[:], k.ident[0:NS, 0:NS]).then_inc(new_turned, 1)
        pe.wait_ge(reduced, 1)
        for e in range(E16):
            if e % 4 == 0 and e >= 8:
                pe.wait_ge(sc_copied, e // 4 - 1)
            m = pe.transpose(ps[:, 4 + (e // 4) % 2, (e % 4) * P:(e % 4 + 1) * P], sc[:, e].rearrange("p a q -> p (a q)"), k.ident[:])
            if e % 4 == 3:
                m.then_inc(sc_turned, 1)

    @block.scalar
    def _(act):
        for j in range(N):
            for a in range(2):
                act.wait_ge(turned, 2 * j + a + 1)
                if j >= 2 and a == 0:
                    act.wait_ge(multiplied, j - 1)
                act.copy(keysT[:, j % 2, 4 * a:4 * a + 4, :], ps[:, 4 * (j % 2) + a, :].rearrange("p (e n) -> p e n", n=P)).then_inc(copied, 1)

    @block.vector
    def _(dve):
        dve.wait_ge(pt_landed, 128)
        dve.tensor_scalar(index[:], pages[:], 8.0, k.part[:, 0:1], ALU.mult, ALU.add).then_inc(indexed, 1)
        dve.memset(bd[:], 0.0)
        dve.memset(k.found[:, QUARTER:QUARTER + TD], UNSEEN)
        dve.drain()
        dve.memset(newp[0:1, 0:1], 0.0).then_inc(zeroed, 1)
        dve.wait_ge(iq_turned, 1)
        for a in range(2):
            rows = slice(a * DH, (a + 1) * DH)
            src = ps[rows, 7, 0:H * NS].rearrange("p (h b t) -> p h b t", h=H, b=BD)
            for t in range(TD):
                dve.tensor_copy(bd[rows, :, a, t, :], src[:, :, :, t].rearrange("p h b -> p b h"))
        dve.drain()
        dve.memset(newp[0:1, 0:1], 0.0).then_inc(blocks_made, 1)
        dve.wait_ge(new_scored, 1)
        dve.wait_ge(small_landed, 64)
        dve.drain()
        dve.scalar_tensor_tensor(newp[:], ps[0:NS, 6, 0:NS * H], 0.0, wb[0:NS].rearrange("p q h -> p (q h)"), ALU.max, ALU.mult)
        dve.drain()
        dve.tensor_reduce(news[:], newp[:].rearrange("p (q h) -> p q h", h=H), AX.X, ALU.add).then_inc(new_summed, 1)
        for j in range(N):
            b, a = j // 4, j % 4
            dve.wait_ge(multiplied, j + 1)
            w = wb[:, b * TD:(b + 1) * TD, :].rearrange("p t h -> p (t h)")
            dve.scalar_tensor_tensor(part[:, j % 2].rearrange("p (e n) -> p e n", n=TD * H),
                                     ps[:, 2 + j % 2, :].rearrange("p (e n) -> p e n", n=TD * H), 0.0,
                                     w[:, None, :].broadcast_to([P, E16, TD * H]), ALU.max, ALU.mult).then_inc(weighted, 1)
            dve.drain()
            dve.tensor_reduce(sc[:, :, a, b * TD:(b + 1) * TD], part[:, j % 2].rearrange("p (e t h) -> p e t h", e=E16, h=H),
                              AX.X, ALU.add)
        dve.drain()
        dve.memset(newp[0:1, 0:1], 0.0).then_inc(reduced, 1)
        dve.wait_ge(new_turned, 1)
        dve.tensor_tensor(newt[:], ps[0:NS, 7, 0:NS], newb[:], ALU.add)
        dve.drain()
        dve.tensor_reduce(newq[:], newt[:].rearrange("p (b s) -> p s b", b=BD), AX.X, ALU.max).then_inc(new_ready, 1)
        for g in range(4):
            dve.wait_ge(sc_turned, g + 1)
            dst = k.found[:, 0:QUARTER].rearrange("p (n e) -> p e n", e=E16)
            dve.tensor_copy(dst[:, 4 * g:4 * g + 4, :], ps[:, 4 + g % 2, :].rearrange("p (e n) -> p e n", n=P)).then_inc(sc_copied, 1)


def select_sample(k, ctx, block, chunks):
    io, ps = k.io, k.ps
    F = k.found
    FIRST_NEW = k.n_pool * PAGE
    best = k.sb(ctx, "best", [P, TOPK])
    where = k.sb(ctx, "where", [P, TOPK], U32)
    tabi = k.sb(ctx, "table_i", [P, 16], I32)
    tab = k.sb(ctx, "table", [P, 16])
    pagef = k.sb(ctx, "page_f", [P, TOPK])
    blk = k.sb(ctx, "block_u", [P, TOPK], U32)
    offu = k.sb(ctx, "offset_u", [P, TOPK], U32)
    hit = k.sb(ctx, "hit", [P, TOPK])
    row = k.sb(ctx, "row", [P, 2, 2 * TOPK])
    iota = k.sb(ctx, "iota", [P, TOPK])
    cand = k.sb(ctx, "cand", [NS, 4, TOPK])
    cbest = k.sb(ctx, "cand_best", [NS, 8])
    ceq = k.sb(ctx, "cand_taken", [NS, 4, TOPK])
    span = k.sb(ctx, "span", [NS, 4, 2])
    cnt = k.sb(ctx, "cnt", [NS, 4])
    sp4 = k.sb(ctx, "span_of_part", [P, 2])
    bitsu = k.sb(ctx, "bits_u", [P, 10], I32)
    bits = k.sb(ctx, "bits", [P, 10])
    fold = k.sb(ctx, "fold", [P, NS])
    newc = k.sb(ctx, "new_count", [P, TD])
    newq = k.sb(ctx, "new_by_query", [NS, TD])
    newm = k.sb(ctx, "new_matrix", [NS, BD, TD])
    same = k.sb(ctx, "same_entry", [NS, NS])
    slots = k.sb(ctx, "slots", [P, 2, NS])
    landed, cand_landed, span_landed = k.sems(ctx, "landed", "cand_landed", "span_landed")
    found, counted, placed, folded, new_made, new_turned = k.sems(
        ctx, "found", "counted", "placed", "folded", "new_made", "new_turned")

    @block.sync
    def _(sp):
        pt = io["page_table"].rearrange("b (a i) -> a b i", a=4)
        for a in range(4):
            sp.dma_start(tabi[a * NS:(a + 1) * NS, :],
                         pt[a][:, None, :].broadcast_to([BD, TD, 16])).then_inc(landed, 16)
        sp.dma_start(iota[:], io["c_iota"].broadcast_to([P, TOPK])).then_inc(landed, 16)
        sp.dma_start(fold[:], io["c_fold"]).then_inc(landed, 16)
        sp.dma_start(same[:], io["c_same"]).then_inc(landed, 16)

    def gather_candidates(pool):
        pool.wait_ge(found, 1)
        for a in range(4):
            pool.dma_start(cand[:, a, :], best[a * NS:(a + 1) * NS, :]).then_inc(cand_landed, 16)

    def spread_spans(pool):
        pool.wait_ge(counted, 1)
        for a in range(4):
            pool.dma_start(sp4[a * NS:(a + 1) * NS, :], span[:, a, :]).then_inc(span_landed, 16)

    project_rows(k, ctx, block, chunks, scores=True, moves={22: gather_candidates, 38: spread_spans})

    @block.vector
    def _(dve):
        for i in range(ROUNDS):
            b8 = best[:, 8 * i:8 * i + 8]
            dve.max(b8, F[:])
            dve.drain()
            dve.max_index(where[:, 8 * i:8 * i + 8], b8, F[:])
            dve.drain()
            dve.match_replace(F[:], b8, F[:], TAKEN)
            dve.drain()
        dve.tensor_copy(tab[0:1, 0:1], best[0:1, 0:1]).then_inc(found, 1)
        dve.wait_ge(landed, 112)
        dve.drain()
        dve.tensor_copy(tab[:], tabi[:])
        dve.tensor_scalar(blk[:], where[:], 7, None, ALU.logical_shift_right)
        dve.tensor_scalar(offu[:], where[:], PAGE - 1, None, ALU.bitwise_and)
        dve.memset(row[:], 0.0)
        dve.drain()
        dve.tensor_copy(pagef[:], blk[:])
        dve.drain()
        data = row[:, 0, TOPK:2 * TOPK]
        dve.tensor_scalar(data, pagef[:], 16.0, float(k.n_pool), ALU.is_equal, ALU.mult)
        dve.drain()
        for i in range(16):
            dve.tensor_scalar(hit[:], pagef[:], float(i), tab[:, i:i + 1], ALU.is_equal, ALU.mult)
            dve.drain()
            dve.tensor_tensor(data, data, hit[:], ALU.add)
            dve.drain()
        dve.scalar_tensor_tensor(data, data, float(PAGE), offu[:], ALU.mult, ALU.add)
        dve.wait_ge(cand_landed, 64)
        c = cand[:].rearrange("p a n -> p (a n)")
        with dve.Fori(0, ROUNDS):
            dve.max(cbest[:], c)
            dve.drain()
            dve.match_replace(c, cbest[:], c, TAKEN)
            dve.drain()
        dve.tensor_scalar(ceq[:], cand[:], TAKEN, None, ALU.is_equal)
        dve.drain()
        dve.tensor_reduce(cnt[:], ceq[:], AX.X, ALU.add)
        dve.memset(span[:, 0, 0:1], 0.0)
        dve.drain()
        for a in range(4):
            dve.tensor_tensor(span[:, a, 1:2], span[:, a, 0:1], cnt[:, a:a + 1], ALU.add)
            dve.drain()
            if a < 3:
                dve.tensor_copy(span[:, a + 1, 0:1], span[:, a, 1:2])
                dve.drain()
        dve.tensor_copy(cbest[:, 0:1], cnt[:, 0:1]).then_inc(counted, 1)
        dve.wait_ge(span_landed, 64)
        dve.tensor_copy(bitsu[:, 9:10], sp4[:, 0:1])
        dve.drain()
        for i in range(9):
            dve.tensor_scalar(bitsu[:, i:i + 1], bitsu[:, 9:10], i, 1, ALU.arith_shift_right, ALU.bitwise_and)
        dve.drain()
        dve.tensor_copy(bits[:, 0:9], bitsu[:, 0:9])
        dve.drain()
        for i in range(9):
            x, y = row[:, i % 2], row[:, (i + 1) % 2]
            dve.tensor_tensor(hit[:], x[:, TOPK - (1 << i):2 * TOPK - (1 << i)], x[:, TOPK:2 * TOPK], ALU.subtract)
            dve.drain()
            dve.scalar_tensor_tensor(y[:, TOPK:2 * TOPK], hit[:], bits[:, i:i + 1], x[:, TOPK:2 * TOPK], ALU.mult, ALU.add)
            dve.drain()
        y = row[:, 1, TOPK:2 * TOPK]
        dve.scalar_tensor_tensor(hit[:], iota[:], sp4[:, 0:1], y, ALU.is_ge, ALU.mult)
        dve.drain()
        dve.scalar_tensor_tensor(y, iota[:], sp4[:, 1:2], hit[:], ALU.is_lt, ALU.mult)
        dve.drain()
        for s in range(TD):
            dve.tensor_scalar(hit[:], y, float(FIRST_NEW + s), None, ALU.is_equal)
            dve.drain()
            dve.tensor_reduce(newc[:, s:s + 1], hit[:], AX.X, ALU.add)
            dve.drain()
        dve.tensor_copy(bits[0:1, 9:10], bits[0:1, 8:9]).then_inc(placed, 1)
        dve.wait_ge(folded, 1)
        dve.tensor_copy(slots[:], ps[:, 0, 0:2 * NS].rearrange("p (a q) -> p a q", a=2))
        dve.tensor_copy(newq[:], ps[0:NS, 1, 0:TD])
        dve.drain()
        dve.tensor_scalar(k.slot_bias[:], slots[:], float(FIRST_NEW), MASKED, ALU.is_ge, ALU.mult)
        dve.tensor_scalar(k.slot_row[:], slots[:], float(FIRST_NEW - 1), None, ALU.min)
        dve.tensor_tensor(newm[:], newq[:][:, None, :].broadcast_to([NS, BD, TD]), same[:].rearrange("p (b s) -> p b s", b=BD),
                          ALU.mult).then_inc(new_made, 1)
        dve.wait_ge(new_turned, 1)
        dve.tensor_scalar(k.new_bias[:], ps[0:NS, 1, 0:NS], -1.0, -MASKED, ALU.add, ALU.mult)

    @block.tensor
    def _(pe):
        pe.wait_ge(placed, 1)
        pe.wait_ge(landed, 112)
        pe.wait_ge(*k.banks_taken)
        for a in range(2):
            pe.matmul(ps[:, 0, a * NS:(a + 1) * NS], row[:, 1, TOPK + a * P:TOPK + (a + 1) * P], fold[:], start=True, stop=True)
        pe.matmul(ps[0:NS, 1, 0:TD], fold[:], newc[:], start=True, stop=True).then_inc(folded, 1)
        pe.wait_ge(new_made, 1)
        pe.transpose(ps[0:NS, 1, 0:NS], newm[:].rearrange("p b s -> p (b s)"), k.ident[0:NS, 0:NS]).then_inc(new_turned, 1)



def attend_sample(k, ctx, block):
    io, ps, mixT = k.io, k.ps, k.hT
    RING = 12
    scale = DH ** -0.5
    pairs = [(q, a) for q in range(NS) for a in range(2)]
    HALF = NS // 2
    SLOTS = TOPK + NS
    EDGE = P - H
    WIDE = EDGE + P
    got = k.sb(ctx, "gathered", [P, RING, H * DH])
    qz = k.sb(ctx, "q_among_zeros", [P, 2, 4 * WIDE])
    keysT = k.sb(ctx, "gathered_keysT", [P, 2, 4, P])
    bias = k.sb(ctx, "slot_bias_heads", [P, 2, NS, H])
    lgn = k.sb(ctx, "new_logits", [NS, NS, H])
    prob = k.sb(ctx, "prob_rows", [P, 2, SLOTS])
    pr = k.sb(ctx, "slot_probs", [P, 2, NS, H])
    prn = k.sb(ctx, "new_probs", [NS, NS, H])
    vnew = k.sb(ctx, "v_new", [NS, H * DH])
    best = k.sb(ctx, "best", [P, 2, 8])
    top = k.sb(ctx, "top", [P, 2, 2])
    total = k.sb(ctx, "total", [P, 2, 2])
    own = k.sb(ctx, "own_head", [P, H])
    g_landed = k.sem_ring(ctx, "g_landed", RING)
    (v_landed,) = k.sems(ctx, "v_landed")
    (scored_new, new_read, zeros_made, biased, keys_turned, keys_copied, q_placed, keys_scored, turned, topped, exped, scaled,
     returned, probs_copied, p_placed, weighed, own_kept, out_turned) = k.sems(
        ctx, "scored_new", "new_read", "zeros_made", "biased", "keys_turned", "keys_copied", "q_placed", "keys_scored",
        "turned", "topped", "exped", "scaled", "returned", "probs_copied", "p_placed", "weighed", "own_kept", "out_turned")
    k.banks_taken = (new_read, 1)

    @block.sync
    def _(sp):
        sp.dma_start(vnew[:], io["v_sample"]).then_inc(v_landed, 16)
        sp.dma_start(own[:], io["c_ownhead"]).then_inc(v_landed, 16)

    def gather(pool, i):
        n, (q, a) = i // len(pairs), pairs[i % len(pairs)]
        before = i - RING
        if before >= len(pairs):
            pool.wait_ge(weighed, before - len(pairs) + 1)
        elif before >= 0:
            pool.wait_ge(keys_turned, before + 1)
        view = io[("cache_k", "cache_v")[n]][0].rearrange("g r h d -> (g r) (h d)")
        pool.indirect_dma_start(got[:, i % RING, :], None, view,
                                bass.IndirectOffsetOnAxis(ap=k.slot_row[:, a, q:q + 1], axis=0)
                                ).then_inc(g_landed[i % RING], 16)

    @block.gpsimd
    def _(pool):
        for i in range(len(pairs)):
            gather(pool, i)

    @block.vector
    def _(dve):
        dve.memset(qz[:], 0.0).then_inc(zeros_made, 1)
        dve.tensor_copy(bias[:], k.slot_bias[:][:, :, :, None].broadcast_to([P, 2, NS, H])).then_inc(biased, 1)
        dve.wait_ge(scored_new, 1)
        for a in range(2):
            x = dve.tensor_tensor(lgn[:, :, a:H:2], ps[0:NS, 6 + a, 0:NS * H // 2].rearrange("p (f q) -> p q f", q=NS),
                                  k.new_bias[:][:, :, None].broadcast_to([NS, NS, H // 2]), ALU.add)
        x.then_inc(new_read, 1)
        take_best(k, dve, best, (2, 3), 0, ROUNDS)
        take_best(k, dve, best, (4, 5), 0, ROUNDS)

    def logit_tile(q, a):
        at = (q // HALF) * TOPK + a * P
        return ps[:, 3, at:at + P]

    @block.tensor
    def _(pe):
        for h in range(H):
            row = (h % 2) * DH
            m = pe.matmul(ps[0:NS, 6 + h % 2, (h // 2) * NS:(h // 2 + 1) * NS], k.kT[row:row + DH, h // 2, SEQ:R],
                          k.qT[row:row + DH, h // 2, SEQ:R], start=True, stop=True)
        m.then_inc(scored_new, 1)
        pe.wait_ge(zeros_made, 1)
        pe.wait_ge(biased, 1)
        pe.matmul(ps[:, 3, :], qz[:, 0, P:2 * P], bias[:].rearrange("p a q h -> p (a q h)"), start=True, stop=False)
        for g in range(2):
            for a in range(2):
                pe.matmul(logit_tile(g * HALF, a), bias[:, a, g * HALF:(g + 1) * HALF, :].rearrange("p q h -> p (q h)"),
                          k.ident[:], start=False, stop=False)

    def key_step(pe, j):
        if j:
            pe.wait_ge(keys_copied, j)
        if j < len(pairs):
            pe.wait_ge(g_landed[j % RING], 16 * (j // RING + 1))
            for f in range(4):
                m = pe.transpose(ps[:, 7, f * P:(f + 1) * P], got[:, j % RING, f * P:(f + 1) * P], k.ident[:])
            m.then_inc(keys_turned, 1)
        if j:
            q, a = pairs[j - 1]
            pe.wait_ge(q_placed, q + 1)
            for f in range(4):
                at = f * WIDE + EDGE - H * (q % HALF)
                m = pe.matmul(logit_tile(q, a), qz[:, q % 2, at:at + P], keysT[:, (j - 1) % 2, f, :], start=False,
                              stop=j == len(pairs) and f == 3)
            m.then_inc(keys_scored, 1)

    def copy_step(act, j):
        q, a = pairs[j]
        if a == 0:
            if q >= 2:
                act.wait_ge(keys_scored, 2 * (q - 1))
            else:
                act.wait_ge(zeros_made, 1)
            for b in range(2):
                rows = slice(b * DH, (b + 1) * DH)
                x = act.copy(qz[rows, q % 2, EDGE + b::WIDE + 2], k.qT[rows, 0:4, SEQ + q])
            x.then_inc(q_placed, 1)
        act.wait_ge(keys_turned, j + 1)
        if j >= 2:
            act.wait_ge(keys_scored, j - 1)
        act.copy(keysT[:, j % 2], ps[:, 7, :].rearrange("p (f n) -> p f n", f=4)).then_inc(keys_copied, 1)

    k.between = (key_step, copy_step)

    def weigh_values(k, ctx, block):
        windows = qz[:].rearrange("p s (f n) -> p (s f) n", n=WIDE)
        kept = keysT[:].rearrange("p g f n -> p g (f n)")

        @block.gpsimd
        def _(pool):
            for i in range(len(pairs), 2 * len(pairs)):
                gather(pool, i)

        @block.vector
        def _(dve):
            for g in range(2):
                dve.wait_ge(turned, g + 1)
                dve.tensor_copy(prob[:, g, 0:TOPK], ps[:, 3, g * TOPK:(g + 1) * TOPK])
                dve.tensor_copy(prob[:, g, TOPK:SLOTS], ps[:, g, 0:NS])
                dve.drain()
                dve.tensor_reduce(top[:, g, 0:1], prob[:, g, :], AX.X, ALU.max)
                dve.drain()
                dve.tensor_scalar(top[:, g, 1:2], top[:, g, 0:1], -scale, None, ALU.mult).then_inc(topped, 1)
            for g in range(2):
                dve.wait_ge(exped, g + 1)
                dve.reciprocal(total[:, g, 1:2], total[:, g, 0:1])
                dve.drain()
                dve.tensor_scalar(prob[:, g, :], prob[:, g, :], total[:, g, 1:2], None, ALU.mult).then_inc(scaled, 1)
            for g in range(2):
                dve.wait_ge(returned, g + 1)
                qs = slice(g * HALF, (g + 1) * HALF)
                dve.tensor_copy(pr[:, :, qs, :], ps[:, 6 + g, 0:TOPK].rearrange("p (a q h) -> p a q h", a=2, h=H))
                dve.tensor_copy(prn[:, qs, :], ps[0:NS, 6 + g, TOPK:TOPK + P].rearrange("p (q h) -> p q h", h=H)).then_inc(probs_copied, 1)
            take_best(k, dve, best, (6,), 0, ROUNDS)
            dve.wait_ge(v_landed, 32)
            for g in range(2):
                dve.wait_ge(weighed, (g + 1) * TOPK // H)
                dve.tensor_tensor(kept[:, g].rearrange("p (h d) -> p h d", h=H), ps[:, 4 + g, :].rearrange("p (h d) -> p h d", h=H),
                                  own[:][:, :, None].broadcast_to([P, H, DH]), ALU.mult).then_inc(own_kept, 1)
            for g in range(2):
                dve.wait_ge(out_turned, g + 1)
                at = SEQ + g * HALF
                dve.tensor_reduce(mixT[:, 0:4, at:at + HALF], ps[:, 6 + g, :].rearrange("p (f q h) -> p f q h", f=4, h=H), AX.X, ALU.add)

        @block.scalar
        def _(act):
            for g in range(2):
                act.wait_ge(topped, g + 1)
                act.activation(prob[:, g, :], prob[:, g, :], ACT.Exp, bias=top[:, g, 1:2], scale=scale,
                               accum_out=total[:, g, 0:1])
                act.drain()
                act.copy(top[0:1, g, 0:1], top[0:1, g, 1:2]).then_inc(exped, 1)
            act.wait_ge(probs_copied, 2)
            for j, (q, a) in enumerate(pairs):
                if j >= 8:
                    act.wait_ge(weighed, j - 7)
                act.copy(windows[:, j % 8, EDGE:EDGE + H], pr[:, a, q, :]).then_inc(p_placed, 1)

        @block.tensor
        def _(pe):
            pe.wait_ge(*k.banks_taken)
            key_step(pe, len(pairs))
            for g in range(2):
                qs = slice(g * HALF, (g + 1) * HALF)
                pe.transpose(ps[:, g, 0:NS], lgn[:, qs, :].rearrange("p q h -> p (q h)"), k.ident[0:NS, 0:NS]).then_inc(turned, 1)
            for g in range(2):
                pe.wait_ge(scaled, g + 1)
                for a in range(2):
                    pe.transpose(ps[:, 6 + g, a * P:(a + 1) * P], prob[:, g, a * P:(a + 1) * P], k.ident[:])
                pe.transpose(ps[0:NS, 6 + g, TOPK:TOPK + P], prob[:, g, TOPK:SLOTS], k.ident[:]).then_inc(returned, 1)
            pe.wait_ge(probs_copied, 2)
            pe.wait_ge(v_landed, 32)
            for g in range(2):
                pe.matmul(ps[:, 4 + g, :], prn[:, g * HALF:(g + 1) * HALF, :].rearrange("p q h -> p (q h)"), vnew[:],
                          start=True, stop=False)
            for j, (q, a) in enumerate(pairs):
                i = len(pairs) + j
                pe.wait_ge(g_landed[i % RING], 16 * (i // RING + 1))
                pe.wait_ge(p_placed, j + 1)
                at = EDGE - H * (q % HALF)
                pe.matmul(ps[:, 4 + q // HALF, :], windows[:, j % 8, at:at + P], got[:, i % RING, :], start=False,
                          stop=a == 1 and q % HALF == HALF - 1).then_inc(weighed, 1)
            for g in range(2):
                pe.wait_ge(own_kept, g + 1)
                for f in range(4):
                    m = pe.transpose(ps[:, 6 + g, f * P:(f + 1) * P], kept[:, g, f * P:(f + 1) * P], k.ident[:])
                m.then_inc(out_turned, 1)

    return weigh_values



def three_pass(pe, out, w, x, g, first, last):
    for i, (a, b) in enumerate(((0, 0), (0, 1), (1, 0))):
        m = pe.matmul(out, w[a], x[b][:, g * GC:(g + 1) * GC], start=first and i == 0, stop=last and i == 2)
    return m


class SplitWeights:

    def __init__(self, k, ctx, name, tiles):
        self.raw = k.sb(ctx, f"{name}_raw", [P, 2, tiles, P])
        self.ws = k.sb(ctx, f"{name}_split", [P, 2, 2, tiles, P], F32R)
        self.landed = k.sem_ring(ctx, f"{name}_landed", 2)
        self.high_made, self.ready = k.sems(ctx, f"{name}_high_made", f"{name}_split_ready")

    def load(self, sp, slot, at, src):
        sp.dma_start(self.raw[:, slot, at:at + src.shape[1], :], src).then_inc(self.landed[slot], 16)

    def high(self, act, slot, landed):
        act.wait_ge(self.landed[slot], landed)
        act.copy(self.ws[:, slot, 0], self.raw[:, slot]).then_inc(self.high_made, 1)

    def low(self, pool, j, slot):
        pool.wait_ge(self.high_made, j + 1)
        pool.tensor_tensor(self.ws[:, slot, 1], self.raw[:, slot], self.ws[:, slot, 0].bitcast(F32), ALU.subtract
                           ).then_inc(self.ready, 1)

    def parts(self, slot, d):
        return [self.ws[:, slot, a, d, :] for a in range(2)]


def project_out(k, ctx, block):
    ps, mixT = k.ps, k.hT
    w_out = k.io["w_out"][0].rearrange("(k p) n -> p k n", p=P)
    mix = k.sb(ctx, "mix_split", [P, 2, KD, R], F32R)
    weights = SplitWeights(k, ctx, "w_out", KD)
    mix_high, mix_even, mix_odd, multiplied, banks_free = k.sems(
        ctx, "mix_high", "mix_even", "mix_odd", "multiplied", "banks_free")

    @block.sync
    def _(sp):
        for s in range(2):
            weights.load(sp, s, 0, w_out[:, :, s * P:(s + 1) * P])
        with sp.Fori(0, KD // 2 - 1) as t:
            for s in range(2):
                sp.wait_ge(weights.ready, 2 * t + s + 1)
                weights.load(sp, s, 0, w_out[:, :, bass.ds((2 * t + 2 + s) * P, P)])

    @block.tensor
    def _(pe):
        def product(n, s, first=False):
            pe.wait_ge(weights.ready, n + 1)
            pe.wait_ge(banks_free, n + 1)
            for d in range(KD):
                if first:
                    pe.wait_ge(mix_odd if d % 2 else mix_even, d // 2 + 1)
                for g in range(G):
                    m = three_pass(pe, ps[:, 4 * s + g, 0:GC], weights.parts(s, d), [mix[:, a, d, :] for a in range(2)], g,
                                   d == 0, d == KD - 1)
            m.then_inc(multiplied, 1)

        product(0, 0, first=True)
        product(1, 1)
        with pe.Fori(1, KD // 2) as t:
            for s in range(2):
                product(2 * t + s, s)

    @block.scalar
    def _(act):
        for d in range(KD):
            act.copy(mix[:, 0, d, :], mixT[:, d, :]).then_inc(mix_high, 1)
            if d < 2:
                weights.high(act, d, 16)
        with act.Fori(1, KD // 2) as t:
            for s in range(2):
                act.wait_ge(multiplied, 2 * t + s - 1)
                weights.high(act, s, 16 * t + 16)

    def mix_low(eng, d):
        eng.wait_ge(mix_high, d + 1)
        return eng.tensor_tensor(mix[:, 1, d, :], mixT[:, d, :], mix[:, 0, d, :].bitcast(F32), ALU.subtract)

    @block.gpsimd
    def _(pool):
        for s in range(2):
            weights.low(pool, s, s)
            mix_low(pool, 2 * s + 1).then_inc(mix_odd, 1)
        for d in (5, 7):
            mix_low(pool, d).then_inc(mix_odd, 1)
        with pool.Fori(1, KD // 2) as t:
            for s in range(2):
                weights.low(pool, 2 * t + s, s)

    @block.vector
    def _(dve):
        dve.sem_inc(banks_free, 2)
        for d in range(0, KD, 2):
            mix_low(dve, d).then_inc(mix_even, 1)
        with dve.Fori(0, KD // 2) as t:
            for s in range(2):
                dve.wait_ge(multiplied, 2 * t + s + 1)
                x = grouped(k.xT[:, 2 * t + s, :])
                dve.tensor_tensor(x, x, bank_cols(ps, 4 * s), ALU.add).then_inc(banks_free, 1)


def ffn(k, ctx, block, layer):
    ps = k.ps
    h = k.sb(ctx, "h_split", [P, 2, KD, R], F32R)
    w_up = k.io["w_up"][layer].rearrange("(k p) n -> p k n", p=P)
    w_down = k.io["w_down"][layer].rearrange("(k p) n -> p k n", p=P)
    PARTS = KF // 2
    W = 2 * P * KD
    BLOCKS = 3 * PARTS
    raw = k.sb(ctx, "w_raw", [P, 2, W])
    ws = k.sb(ctx, "w_split", [P, 2, 2, W], F32R)
    hidden = k.sb(ctx, "hidden", [P, 2, 2, 2, R], F32R)
    silu = k.sb(ctx, "silu", [P, 2, R])
    exact = k.sb(ctx, "hidden_exact", [P, R])
    landed = k.sem_ring(ctx, "w_landed", 2)
    high_made, split_ready, gate_done, silu_done, up_done, hidden_ready, down_done, drained = k.sems(
        ctx, "w_high_made", "w_split_ready", "gate_done", "silu_done", "up_done", "hidden_ready",
        "down_done", "drained")
    norm = SplitNorm(k, ctx, h, k.ffn_w[layer], square=silu, total=exact[:])

    @block.sync
    def _(sp):
        def load(j, slot, src, wait=True):
            if wait:
                sp.wait_ge(split_ready, j - 1)
            sp.dma_start(raw[:, slot].rearrange("p (k n) -> p k n", k=src.shape[1]), src).then_inc(landed[slot], 16)

        def gate(p):
            return w_up[:, :, bass.ds(p * 2 * P, 2 * P)]

        def up(p):
            return w_up[:, :, bass.ds(p * 2 * P + FF, 2 * P)]

        def down(p):
            return w_down[:, bass.ds(2 * p, 2), :]

        load(0, 0, gate(0), False)
        load(1, 1, up(0), False)
        with sp.Fori(0, (PARTS - 1) // 2) as t:
            for e in range(2):
                for m, src in enumerate((gate(2 * t + e + 1), up(2 * t + e + 1), down(2 * t + e))):
                    load(6 * t + 2 + 3 * e + m, (3 * e + m) % 2, src)
        load(BLOCKS - 1, (BLOCKS - 1) % 2, down(PARTS - 1))

    @block.tensor
    def _(pe):
        norm.tensor(pe)

        def up_products(j, slot, p, q, normed=False):
            gates = q is None or q[0] == "g"
            pe.wait_ge(split_ready, j + 1)
            for i in range(2):
                if gates:
                    if q is not None:
                        pe.wait_ge(drained, q[1] - 1 + i)
                else:
                    pe.wait_ge(silu_done, 2 * p + 1 + i)
                for d in range(KD):
                    if normed and i == 0:
                        pe.wait_ge(norm.normed, d + 1)
                    at = d * 2 * P + i * P
                    w_at = [ws[:, slot, a, at:at + P] for a in range(2)]
                    for g in range(G):
                        m = three_pass(pe, ps[:, 3 * i + g, 0:GC], w_at, [h[:, a, d, :] for a in range(2)], g, d == 0, d == KD - 1)
                m.then_inc(gate_done if gates else up_done, 1)

        def down_products(j, slot, p, parity, before):
            pe.wait_ge(split_ready, j + 1)
            pe.wait_ge(hidden_ready, 2 * p + 2)
            for d in range(KD):
                pe.wait_ge(drained, before + 1 + d)
                for i in range(2):
                    at = i * D + d * P
                    w_at = [ws[:, slot, a, at:at + P] for a in range(2)]
                    for g in range(G):
                        m = three_pass(pe, ps[:, 3 * (d % 2) + g, 0:GC], w_at, [hidden[:, parity, i, a, :] for a in range(2)], g,
                                       i == 0, i == 1)
                m.then_inc(down_done, 1)

        up_products(0, 0, 0, None, normed=True)
        up_products(1, 1, 0, ("u", 0))
        with pe.Fori(0, (PARTS - 1) // 2) as t:
            for e in range(2):
                p, j, before = 2 * t + e, 6 * t + 2 + 3 * e, 2 + 10 * (2 * t + e)
                up_products(j, (3 * e) % 2, p + 1, ("g", before))
                up_products(j + 1, (3 * e + 1) % 2, p + 1, ("u", before))
                down_products(j + 2, (3 * e + 2) % 2, p, e, before)
        down_products(BLOCKS - 1, (BLOCKS - 1) % 2, PARTS - 1, 0, 10 * (PARTS - 1))

    @block.scalar
    def _(act):
        def high(slot, count, done=None, products=0):
            act.wait_ge(landed[slot], 16 * count)
            if done is not None:
                act.wait_ge(done, products)
            act.copy(ws[:, slot, 0], raw[:, slot]).then_inc(high_made, 1)

        def silus(p, wait=True):
            for i in range(2):
                act.wait_ge(gate_done, 2 * p + 1 + i)
                if wait:
                    act.wait_ge(hidden_ready, 2 * p - 1 + i)
                act.activation(grouped(silu[:, i]), bank_cols(ps, 3 * i), ACT.Silu).then_inc(silu_done, 1)

        def steps(t, first=False):
            for e in range(2):
                q = 2 * t + e
                n = 3 * e + 3
                if first and e == 0:
                    high(n % 2, 3 * t + n // 2 + 1, up_done, 2)
                else:
                    high(n % 2, 3 * t + n // 2 + 1, down_done, KD * q)
                silus(q + 1)
                high((n + 1) % 2, 3 * t + (n + 1) // 2 + 1, gate_done, 2 * q + 4)
                high((n + 2) % 2, 3 * t + (n + 2) // 2 + 1, up_done, 2 * q + 4)

        norm.scalar(act)
        for s in range(2):
            high(s, 1)
        norm.round(act)
        silus(0, False)
        high(0, 2, gate_done, 2)
        steps(0, first=True)
        with act.Fori(1, (PARTS - 1) // 2) as t:
            steps(t)

    @block.gpsimd
    def _(pool):
        def low(j, slot):
            pool.wait_ge(high_made, j + 1)
            pool.tensor_tensor(ws[:, slot, 1], raw[:, slot], ws[:, slot, 0].bitcast(F32), ALU.subtract).then_inc(split_ready, 1)

        for j in range(2):
            low(j, j)
        norm.pool(pool)
        with pool.Fori(1, BLOCKS // 2) as t:
            for s in range(2):
                low(2 * t + s, s)
        low(BLOCKS - 1, (BLOCKS - 1) % 2)

    @block.vector
    def _(dve):
        norm.vector(dve)
        dve.drain()

        def hiddens(p, parity):
            for i in range(2):
                dve.wait_ge(silu_done, 2 * p + 1 + i)
                dve.wait_ge(up_done, 2 * p + 1 + i)
                dve.tensor_tensor(grouped(exact[:]), grouped(silu[:, i]), bank_cols(ps, 3 * i), ALU.mult).then_inc(drained, 1)
                dve.drain()
                dve.tensor_copy(hidden[:, parity, i, 0, :], exact[:])
                dve.drain()
                dve.tensor_tensor(hidden[:, parity, i, 1, :], exact[:], hidden[:, parity, i, 0, :].bitcast(F32),
                                  ALU.subtract).then_inc(hidden_ready, 1)
                dve.drain()

        def adds(p):
            for d in range(KD):
                dve.wait_ge(down_done, KD * p + d + 1)
                x = grouped(k.xT[:, d, :])
                dve.tensor_tensor(x, x, bank_cols(ps, 3 * (d % 2)), ALU.add).then_inc(drained, 1)

        hiddens(0, 0)
        with dve.Fori(0, (PARTS - 1) // 2) as t:
            for e in range(2):
                hiddens(2 * t + e + 1, 1 - e)
                adds(2 * t + e)
        adds(PARTS - 1)


def layer_embedding(k, ctx, block, layer):
    io, ps = k.io, k.ps
    wg = io["w_ple_gate"][layer].rearrange("(k p) n -> p k n", p=P)
    wp = io["w_ple"][layer].rearrange("(k p) n -> p k n", p=P)
    KP = PLE // P
    h = k.sb(ctx, "h_ple_split", [P, 2, KD, R], F32R)
    rows = k.sb(ctx, "p_rows", [P, NT + 1, PLE])
    pT = k.sb(ctx, "pT_split", [P, 2, KP, R], F32R)
    gate = k.sb(ctx, "gate", [P, R])
    term = k.sb(ctx, "term", [P, R])
    weights = SplitWeights(k, ctx, "w_ple", KD + KP)
    (p_landed,) = k.sems(ctx, "p_landed")
    turned, p_high, p_split, gate_done, ple_done, gated, added = k.sems(
        ctx, "turned", "p_high", "p_split", "gate_done", "ple_done", "gated", "added")
    norm = SplitNorm(k, ctx, h, k.ple_w[layer])
    LAST = KD // 2 - 1

    @block.sync
    def _(sp):
        sp.dma_start(rows[:, 0:NT, :], io["p_prompt"][layer, 0].rearrange("(r p) n -> p r n", p=P)).then_inc(p_landed, 16)
        sp.dma_start(rows[0:NS, NT, :], io["p_sample"][layer].rearrange("b t n -> (b t) n")).then_inc(p_landed, 16)

        def load(s, n):
            weights.load(sp, s, 0, wg[:, :, bass.ds(n * P, P)])
            weights.load(sp, s, KD, wp[:, :, bass.ds(n * P, P)])

        for s in range(2):
            load(s, s)
        with sp.Fori(0, LAST) as t:
            for s in range(2):
                sp.wait_ge(weights.ready, 2 * t + s + 1)
                load(s, 2 * t + 2 + s)

    @block.tensor
    def _(pe):
        pe.wait_ge(p_landed, 32)
        for r in range(NT + 1):
            n = rows_of(r)
            if r >= 2:
                pe.wait_ge(p_split, r - 1)
            for i in range(KP):
                m = pe.transpose(ps[:, 6 + r % 2, i * P:i * P + n], rows[0:n, r, i * P:(i + 1) * P], k.ident[0:n, 0:n])
            m.then_inc(turned, 1)
        norm.tensor(pe)

        def product(n, s, first=False):
            pe.wait_ge(weights.ready, n + 1)
            if not first:
                pe.wait_ge(gated, n)
            for d in range(KD):
                if first:
                    pe.wait_ge(norm.normed, d + 1)
                for g in range(G):
                    m = three_pass(pe, ps[:, g, 0:GC], weights.parts(s, d), [h[:, a, d, :] for a in range(2)], g,
                                   d == 0, d == KD - 1)
            m.then_inc(gate_done, 1)
            if first:
                pe.wait_ge(p_split, NT + 1)
            else:
                pe.wait_ge(added, n)
            for i in range(KP):
                for g in range(G):
                    m = three_pass(pe, ps[:, 4 + g, 0:GC], weights.parts(s, KD + i), [pT[:, a, i, :] for a in range(2)], g,
                                   i == 0, i == KP - 1)
            m.then_inc(ple_done, 1)

        product(0, 0, first=True)
        product(1, 1)
        with pe.Fori(1, KD // 2) as t:
            for s in range(2):
                product(2 * t + s, s)

    @block.scalar
    def _(act):
        for r in range(NT + 1):
            n = rows_of(r)
            act.wait_ge(turned, r + 1)
            act.copy(pT[:, 0, :, r * P:r * P + n], ps[:, 6 + r % 2, 0:PLE].rearrange("p (i n) -> p i n", n=P)[:, :, 0:n]
                     ).then_inc(p_high, 1)
        norm.scalar(act)
        for s in range(2):
            weights.high(act, s, 32)
        norm.round(act)

        def sigmoid(n, first=False):
            act.wait_ge(gate_done, n + 1)
            if not first:
                act.wait_ge(added, n)
            act.activation(grouped(gate[:]), bank_cols(ps, 0), ACT.Sigmoid).then_inc(gated, 1)

        sigmoid(0, first=True)
        act.wait_ge(ple_done, 1)
        weights.high(act, 0, 64)
        with act.Fori(1, LAST) as t:
            for s in range(2):
                sigmoid(2 * t - 1 + s)
                act.wait_ge(ple_done, 2 * t + s)
                weights.high(act, 1 - s, 32 * t + 32 + 32 * s)
        sigmoid(KD - 3)
        act.wait_ge(ple_done, KD - 2)
        weights.high(act, 1, 32 * KD // 2)
        for n in (KD - 2, KD - 1):
            sigmoid(n)

    @block.gpsimd
    def _(pool):
        for s in range(2):
            weights.low(pool, s, s)
        norm.pool(pool)
        with pool.Fori(1, KD // 2) as t:
            for s in range(2):
                weights.low(pool, 2 * t + s, s)

    @block.vector
    def _(dve):
        for r in range(NT + 1):
            n = rows_of(r)
            dve.wait_ge(p_high, r + 1)
            at = slice(r * P, r * P + n)
            dve.tensor_tensor(pT[:, 1, :, at], ps[:, 6 + r % 2, 0:PLE].rearrange("p (i n) -> p i n", n=P)[:, :, 0:n],
                              pT[:, 0, :, at].bitcast(F32), ALU.subtract).then_inc(p_split, 1)
        norm.vector(dve)
        dve.drain()
        with dve.Fori(0, KD) as n:
            dve.wait_ge(gated, n + 1)
            dve.wait_ge(ple_done, n + 1)
            dve.tensor_tensor(grouped(term[:]), grouped(gate[:]), bank_cols(ps, 4), ALU.mult)
            dve.drain()
            x = k.xT[:, n, :]
            dve.tensor_tensor(x, x, term[:], ALU.add).then_inc(added, 1)
            dve.drain()



def pool_mix(k, ctx, block):
    io, ps = k.io, k.ps
    hT = k.sb(ctx, "h_pool", [P, KD, R])
    SEG = POOL_BUF + TD
    HEAD = POOL_BUF + SEQ
    LEN = HEAD + BD * SEG
    BUF = BD * POOL_BUF
    OUT = POOL_BUF + NS
    z = k.sb(ctx, "z", [P, KD, R])
    ext = k.sb(ctx, "ext", [P, 2, LEN])
    sums = k.sb(ctx, "sums", [P, 2, LEN])
    inv = k.sb(ctx, "inv_count", [P, len(WINDOWS), 16])
    w = k.sb(ctx, "pool_w", [P, len(WINDOWS), 2, 2 * P])
    buf = k.sb(ctx, "buf_rows", [BUF, D])
    bufT = k.sb(ctx, "bufT", [P, KD, BUF])
    last = k.sb(ctx, "last_rows", [OUT, D])
    fix = k.sb(ctx, "first_means", [P, 16])
    w_landed, buf_landed, out_stored = k.sems(ctx, "w_landed", "buf_landed", "out_stored")
    turned, copied, last_turned, last_copied, z_made, multiplied, added = k.sems(
        ctx, "turned", "copied", "last_turned", "last_copied", "z_made", "multiplied", "added")
    norm = Norm(k, ctx, hT, k.mix_w[1], square=z[:, 0:2, :], total=z[:, 2, :])

    @block.sync
    def _(sp):
        sp.dma_start(buf[:], io["state_pool"][0].rearrange("b r n -> (b r) n")).then_inc(buf_landed, 16)
        sp.dma_start(w[:], io["pool_w"][0].rearrange("g (k p) n -> p g k n", p=P)).then_inc(w_landed, 16)
        sp.dma_start(inv[:].rearrange("p w n -> p (w n)"), io["c_invcnt"].broadcast_to([P, 16 * len(WINDOWS)])).then_inc(w_landed, 16)
        sp.dma_start(io["pool_sample"][0][:, 0:POOL_BUF - TD, :], io["state_pool"][0][:, TD:POOL_BUF, :]).then_inc(out_stored, 16)
        sp.wait_ge(last_copied, 1)
        sp.dma_start(io["pool_prompt"][0, 0], last[0:POOL_BUF, :]).then_inc(out_stored, 16)
        for b in range(BD):
            at = POOL_BUF + b * TD
            sp.dma_start(io["pool_sample"][0, b, POOL_BUF - TD:POOL_BUF, :], last[at:at + TD, :]).then_inc(out_stored, 16)
        sp.wait_ge(out_stored, 16 * (BD + 2))

    @block.tensor
    def _(pe):
        pe.wait_ge(buf_landed, 16)
        for d in range(KD):
            m = pe.transpose(ps[:, 4 + d // 4, (d % 4) * P:(d % 4) * P + BUF], buf[:, d * P:(d + 1) * P], k.ident[0:BUF, 0:BUF])
        m.then_inc(turned, 1)
        norm.tensor(pe)
        pe.wait_ge(norm.normed, KD)
        for d in range(KD):
            m = pe.transpose(ps[0:OUT, 6 + d // 4, (d % 4) * P:(d % 4 + 1) * P], hT[:, d, R - OUT:R], k.ident[:])
        m.then_inc(last_turned, 1)
        pe.wait_ge(w_landed, 32)
        pe.wait_ge(copied, 1)
        for d in range(KD):
            b = 3 * (d % 2)
            pe.wait_ge(z_made, 2 * (d // 2 + 1))
            if d >= 2:
                pe.wait_ge(added, d - 1)
            for i in range(2):
                for g in range(G):
                    m = pe.matmul(ps[:, b + g, 0:GC], w[:, d // 2, i, (d % 2) * P:(d % 2 + 1) * P],
                                  z[:, 2 * (d // 2) + i, g * GC:(g + 1) * GC], start=i == 0, stop=i == 1)
            m.then_inc(multiplied, 1)

    @block.scalar
    def _(act):
        act.wait_ge(turned, 1)
        act.copy(bufT[:], ps[:, 4:6, :].rearrange("p b (d n) -> p (b d) n", n=P)[:, :, 0:BUF]).then_inc(copied, 1)
        norm.scalar(act)
        act.wait_ge(last_turned, 1)
        act.copy(last[:].rearrange("p (b n) -> p b n", b=2), ps[0:OUT, 6:8, :]).then_inc(last_copied, 1)

    @block.vector
    def _(dve):
        norm.vector(dve)
        dve.memset(ext[:, :, 0:POOL_BUF], 0.0)
        dve.memset(sums[:], 0.0)
        dve.wait_ge(copied, 1)
        dve.wait_ge(w_landed, 32)
        dve.drain()
        for d in range(KD):
            e = ext[:, d % 2, :]
            wi = d // 2
            seg = e[:, HEAD:LEN].rearrange("p (b r) -> p b r", r=SEG)
            dve.tensor_copy(e[:, POOL_BUF:HEAD], hT[:, d, 0:SEQ])
            dve.tensor_copy(seg[:, :, 0:POOL_BUF], bufT[:, d, :].rearrange("p (b r) -> p b r", r=POOL_BUF))
            dve.tensor_copy(seg[:, :, POOL_BUF:SEG], hT[:, d, SEQ:R].rearrange("p (b t) -> p b t", t=TD))
            dve.drain()
            src, reach = e, 1
            for n in range(wi + 1):
                dst = sums[:, n % 2, :]
                dve.tensor_tensor(dst[:, reach:LEN], src[:, reach:LEN], src[:, 0:LEN - reach], ALU.add)
                dve.drain()
                src, reach = dst, 2 * reach
            zp, zs = z[:, d, 0:SEQ], z[:, d, SEQ:R].rearrange("p (b t) -> p b t", t=TD)
            dve.scalar_tensor_tensor(zp, src[:, POOL_BUF:HEAD], 1.0 / reach, e[:, POOL_BUF:HEAD], ALU.mult, ALU.subtract)
            sseg = src[:, HEAD:LEN].rearrange("p (b r) -> p b r", r=SEG)
            dve.scalar_tensor_tensor(zs, sseg[:, :, POOL_BUF:SEG], 1.0 / reach, seg[:, :, POOL_BUF:SEG], ALU.mult, ALU.subtract)
            dve.tensor_tensor(fix[:], src[:, POOL_BUF:POOL_BUF + 16], inv[:, wi, :], ALU.mult)
            dve.drain()
            dve.tensor_tensor(zp[:, 0:16], fix[:], e[:, POOL_BUF:POOL_BUF + 16], ALU.subtract).then_inc(z_made, 1)
            dve.drain()
        for d in range(KD):
            dve.wait_ge(multiplied, d + 1)
            x = grouped(k.xT[:, d, :])
            dve.scalar_tensor_tensor(x, bank_cols(ps, 3 * (d % 2)), k.pool_s[:, d:d + 1], x, ALU.mult, ALU.add).then_inc(added, 1)



def finish(k, ctx, block):
    io, ps = k.io, k.ps
    rows = k.sb(ctx, "y_rows", [P, 3, D])
    square = k.sb(ctx, "y_square", [P, D])
    weight = k.sb(ctx, "final_weight", [P, D])
    stat = k.sb(ctx, "y_stat", [P, 3, 3])
    stored = k.sem_ring(ctx, "y_stored", 3)
    w_landed, turned, rooted, copied = k.sems(ctx, "w_landed", "turned", "rooted", "copied")

    @block.tensor
    def _(pe):
        for r in range(NT + 1):
            n, b = rows_of(r), 2 * (r % 3)
            if r >= 3:
                pe.wait_ge(copied, r - 2)
            for d in range(KD):
                m = pe.transpose(ps[0:n, b + d // 4, (d % 4) * P:(d % 4 + 1) * P], k.xT[:, d, r * P:r * P + n], k.ident[:])
            m.then_inc(turned, 1)

    @block.scalar
    def _(act):
        for r in range(NT + 1):
            n, b, s = rows_of(r), 2 * (r % 3), r % 3
            act.wait_ge(turned, r + 1)
            if r >= 3:
                act.wait_ge(copied, r - 2)
            act.activation(square[0:n].rearrange("p (b n) -> p b n", b=2), ps[0:n, b:b + 2, :], ACT.Square,
                           accum_out=stat[0:n, s, 0:1])
            act.drain()
            act.activation(stat[0:n, s, 1:2], stat[0:n, s, 0:1], ACT.Sqrt, bias=k.eps[0:n, 0:1], scale=1.0 / D).then_inc(rooted, 1)

    @block.vector
    def _(dve):
        dve.wait_ge(w_landed, 16)
        for r in range(NT + 1):
            n, b, s = rows_of(r), 2 * (r % 3), r % 3
            dve.wait_ge(rooted, r + 1)
            dve.reciprocal(stat[0:n, s, 2:3], stat[0:n, s, 1:2])
            dve.drain()
            if r >= 3:
                dve.wait_ge(stored[s], 16 * (r // 3))
            dve.scalar_tensor_tensor(rows[0:n, s, :].rearrange("p (b n) -> p b n", b=2), ps[0:n, b:b + 2, :], stat[0:n, s, 2:3],
                                     weight[0:n].rearrange("p (b n) -> p b n", b=2), ALU.mult, ALU.mult).then_inc(copied, 1)

    @block.sync
    def _(sp):
        sp.dma_start(weight[:], io["final_norm"].rearrange("(o n) -> o n", o=1).broadcast_to([P, D])).then_inc(w_landed, 16)
        for r in range(NT + 1):
            n = rows_of(r)
            sp.wait_ge(copied, r + 1)
            dst = io["y_prompt"][0, r * P:(r + 1) * P, :] if r < NT else io["y_sample"].rearrange("b t d -> (b t) d")
            sp.dma_start(dst, rows[0:n, r % 3, :]).then_inc(stored[r % 3], 16)
        for s in range(3):
            sp.wait_ge(stored[s], 16 * ((NT + 1 - s + 2) // 3))



def build(nc, io):
    scratch = {}
    for name, shape in dict(q_s=(NS, 512), iq_s=(NS, 512), iw_s=(NS, H), bi=(R, 512), bg=(R, 512),
                            gq=(BH, P, R), gk=(BH, P, R), gb=(BH, P, R)).items():
        scratch[name] = nc.dram_tensor(f"scratch_{name}", shape, F32, kind="Internal").ap()
    k = Program(nc, io, scratch)
    k.n_pool = io["cache_kidx"].shape[1]
    io["k_prompt"] = io["k_prompt"].rearrange("l b t h d -> (l b t) (h d)")
    io["v_prompt"] = io["v_prompt"].rearrange("l b t h d -> (l b t) (h d)")
    io["kidx_prompt"] = io["kidx_prompt"].rearrange("l b t d -> (l b t) d")
    io["k_sample"] = io["k_sample"].rearrange("l b t h d -> (l b t) (h d)")
    io["v_sample"] = io["v_sample"].rearrange("l b t h d -> (l b t) (h d)")
    io["kidx_sample"] = io["kidx_sample"].rearrange("l b t d -> (l b t) d")
    with k.keep:
        k.ps = k.keep.enter_context(nc.psum_tensor("ps", [P, 8, 512], F32))
        k.xT = k.sb(k.keep, "xT", [P, KD, R])
        k.ident = k.sb(k.keep, "ident", [P, P])
        k.ones = k.sb(k.keep, "ones", [P, P])
        k.eps = k.sb(k.keep, "eps", [P, 1])
        k.vec = k.sb(k.keep, "vec", [P, 9 * KD])
        k.stage((load_constants,))
        with ExitStack() as mixer:
            k.hT = k.sb(mixer, "hT", [P, KD, R])
            with ExitStack() as mix:
                k.qT, k.kT = (k.sb(mix, n, [P, 4, R]) for n in ("qT", "kT"))
                k.slot_row = k.sb(mix, "slot_row", [P, 2, NS], U32)
                k.slot_bias = k.sb(mix, "slot_bias", [P, 2, NS])
                k.new_bias = k.sb(mix, "new_bias_t", [NS, NS])
                with ExitStack() as index:
                    k.iqT = k.sb(index, "iqT", [P, 4, R])
                    k.ikT = k.sb(index, "ikT", [P, R])
                    k.iw = k.sb(index, "iw", [P, NT + 1, H])
                    k.lb = k.sb(index, "lb", [P, 2, BH])
                    with ExitStack() as proj:
                        k.rope = k.sb(proj, "rope", [P, NT + 1, 2 * DH])
                        k.part = k.sb(proj, "part_const", [P, 2])
                        k.stage((load_normalised,), (lower_bound,))
                        k.stage((project_rows, ["iq", "ik"]))
                        k.found = k.sb(proj, "found", [P, QUARTER + TD])
                        k.stage((score_sample,))
                        k.stage((select_sample, ["aq", "ak", "av", "bi", "bg"]))
                    k.stage((attend_sample,), (project_gates,))
                    k.stage((attend_prompt,))
            k.stage((recurrence,))
            k.stage((project_out,))
        k.stage((ffn, 0))
        k.stage((layer_embedding, 0))
        k.stage((pool_mix,))
        k.stage((ffn, 1))
        k.stage((layer_embedding, 1))
        k.stage((finish,))



_OUTS = dict(
    y_prompt=(1, SEQ, D), y_sample=(BD, TD, D),
    k_prompt=(1, 1, SEQ, H, DH), v_prompt=(1, 1, SEQ, H, DH), kidx_prompt=(1, 1, SEQ, DH),
    glr_prompt=(1, 1, BH, BK, BK), pool_prompt=(1, 1, POOL_BUF, D),
    k_sample=(1, BD, TD, H, DH), v_sample=(1, BD, TD, H, DH), kidx_sample=(1, BD, TD, DH),
    glr_sample=(1, BD, BH, BK, BK), pool_sample=(1, BD, POOL_BUF, D),
)


def kernel(**inputs):
    import concourse.bacc as _bacc
    from concourse.bass_utils import run_bass_kernel_spmd as _run

    nc = _bacc.Bacc("TRN2", target_bir_lowering=False, num_devices=1)
    arrays, io = {}, {}
    for name, a in {**inputs, **constants()}.items():
        a = np.ascontiguousarray(a)
        arrays[f"in_{name}"] = a
        io[name] = nc.dram_tensor(f"in_{name}", a.shape, mybir.dt.from_np(a.dtype), kind="ExternalInput").ap()
    for name, shape in _OUTS.items():
        io[name] = nc.dram_tensor(f"out_{name}", shape, F32, kind="ExternalOutput").ap()
    build(nc, io)
    r = _run(nc, [arrays], core_ids=[0])
    return tuple(r.results[0][f"out_{name}"] for name in _OUTS)
```
